# Optimizing a Trainium2 kernel written in Bass

```python
import jax
import jax.numpy as jnp
from jax import lax
import numpy as np

D_MODEL = 1024
BATCH = 1
SEQ = 512
DEPTH = 2
DEC_BATCH = 1
DEC_SEQ = 64
PAST_LEN = 512

CHUNK = 64
Q_BLOCK = 128
N_AB_LAYERS = (DEPTH + 1) // 2
N_MLA_LAYERS = DEPTH // 2

HEAD_DIM = 64
FOX_HEADS = 8
SB_HEADS = 8
FOX_W = FOX_HEADS * HEAD_DIM
SB_W = SB_HEADS * HEAD_DIM
AB_IN = 3 * FOX_W + FOX_HEADS + 3 * SB_W
AB_MIX = FOX_W + SB_W
FORGET_BIAS_INIT = 3.0

MLA_HEADS = 16
QK_NOPE = 64
QK_ROPE = 32
V_DIM = 64
Q_LORA = 384
KV_LORA = 256
MLA_DOWN = Q_LORA + KV_LORA + QK_ROPE
ROPE_BASE = 10000.0

N_GROUPS = 4
EXPERTS_PER_GROUP = 8
TOP_K_IN_GROUP = 2
EXPERT_HIDDEN = 256

DEEPNORM_ALPHA = (2 * DEPTH) ** 0.25
DEEPNORM_BETA = (8 * DEPTH) ** -0.25
LN_EPS = 1e-5
RMS_EPS = 1e-6
NEG_INF = -1e30

kernel_name = 'hybrid_fox_stickbreak_mla_hmoe_stream_step'

def layer_norm(x, g, b):
    xf = x.astype(jnp.float32)
    mu = jnp.mean(xf, axis=-1, keepdims=True)
    xc = xf - mu
    var = jnp.mean(xc * xc, axis=-1, keepdims=True)
    return (xc * lax.rsqrt(var + LN_EPS) * g.astype(jnp.float32) + b.astype(jnp.float32)).astype(x.dtype)

def rms_norm(x, g):
    xf = x.astype(jnp.float32)
    inv = lax.rsqrt(jnp.mean(xf * xf, axis=-1, keepdims=True) + RMS_EPS)
    return (xf * inv * g.astype(jnp.float32)).astype(x.dtype)

def rope(x, pos):
    half = x.shape[-1] // 2
    inv_freq = ROPE_BASE ** (-jnp.arange(half, dtype=jnp.float32) / half)
    ang = pos.astype(jnp.float32)[:, None] * inv_freq[None, :]
    shape = (1, pos.shape[0]) + (1,) * (x.ndim - 3) + (half,)
    cos = jnp.cos(ang).reshape(shape)
    sin = jnp.sin(ang).reshape(shape)
    xf = x.astype(jnp.float32)
    x1, x2 = xf[..., :half], xf[..., half:]
    return jnp.concatenate([x1 * cos - x2 * sin, x1 * sin + x2 * cos], axis=-1).astype(x.dtype)

def to_blocks(a, nb):
    return jnp.moveaxis(a.reshape((a.shape[0], nb, Q_BLOCK) + a.shape[2:]), 1, 0)

def from_blocks(a):
    a = jnp.moveaxis(a, 0, 1)
    return a.reshape((a.shape[0], a.shape[1] * a.shape[2]) + a.shape[3:])

def chunk_visible(pos_q, pos_k):
    return (pos_k[None, :] // CHUNK) <= (pos_q[:, None] // CHUNK)

def fox_attend(q, k, v, cum_q, cum_k, pos_q, pos_k):
    s = jnp.einsum('bqhd,bkhd->bhqk', q, k).astype(jnp.float32) * (HEAD_DIM ** -0.5)
    decay = jnp.transpose(cum_q, (0, 2, 1))[..., :, None] - jnp.transpose(cum_k, (0, 2, 1))[..., None, :]
    visible = pos_k[None, :] <= pos_q[:, None]
    p = jax.nn.softmax(jnp.where(visible, s + decay, NEG_INF), axis=-1)
    return jnp.einsum('bhqk,bkhd->bqhd', p.astype(v.dtype), v)

def sb_attend(q, k, v, pos_q, pos_k):
    z = jnp.einsum('bqhd,bkhd->bhqk', q, k).astype(jnp.float32) * (HEAD_DIM ** -0.5)
    before = pos_k[None, :] < pos_q[:, None]
    log_beta = jnp.where(before, jax.nn.log_sigmoid(z), NEG_INF)
    log_rest = jnp.where(before, jax.nn.log_sigmoid(-z), 0.0)
    later = lax.cumsum(log_rest, axis=log_rest.ndim - 1, reverse=True) - log_rest
    a = jnp.exp(log_beta + later)
    return jnp.einsum('bhqk,bkhd->bqhd', a.astype(v.dtype), v)

def ab_project(h, w_in, b_f):
    B, T, _ = h.shape
    z = h @ w_in
    cuts = [FOX_W, 2 * FOX_W, 3 * FOX_W, 3 * FOX_W + FOX_HEADS,
            3 * FOX_W + FOX_HEADS + SB_W, 3 * FOX_W + FOX_HEADS + 2 * SB_W]
    qa, ka, va, f_logit, qb, kb, vb = jnp.split(z, cuts, axis=-1)
    fh = lambda a: a.reshape(B, T, FOX_HEADS, HEAD_DIM)
    sh = lambda a: a.reshape(B, T, SB_HEADS, HEAD_DIM)
    logf = jax.nn.log_sigmoid(f_logit.astype(jnp.float32) + b_f.astype(jnp.float32))
    return fh(qa), fh(ka), fh(va), logf, sh(qb), sh(kb), sh(vb)

def ab_merge(oa, ob, w_out):
    B, T = oa.shape[0], oa.shape[1]
    return jnp.concatenate([oa.reshape(B, T, FOX_W), ob.reshape(B, T, SB_W)], axis=-1) @ w_out

def ab_prompt(h, w_in, b_f, w_out):
    B, S, _ = h.shape
    nb = S // Q_BLOCK
    qa, ka, va, logf, qb, kb, vb = ab_project(h, w_in, b_f)
    cum = jnp.cumsum(logf, axis=1)
    pos = jnp.arange(S, dtype=jnp.int32)

    def step(blk):
        qa_b, qb_b, cum_b, pos_b = blk
        return (fox_attend(qa_b, ka, va, cum_b, cum, pos_b, pos),
                sb_attend(qb_b, kb, vb, pos_b, pos))

    oa, ob = lax.map(step, (to_blocks(qa, nb), to_blocks(qb, nb), to_blocks(cum, nb),
                            pos.reshape(nb, Q_BLOCK)))
    y = ab_merge(from_blocks(oa), from_blocks(ob), w_out)
    return y, ka, va, logf.astype(h.dtype), kb, vb

def ab_sample(h, ka_past, va_past, logf_past, kb_past, vb_past, w_in, b_f, w_out):
    B, n, _ = h.shape
    P = ka_past.shape[1]
    qa, ka, va, logf, qb, kb, vb = ab_project(h, w_in, b_f)
    ka_all = jnp.concatenate([ka_past, ka.astype(ka_past.dtype)], axis=1)
    va_all = jnp.concatenate([va_past, va.astype(va_past.dtype)], axis=1)
    kb_all = jnp.concatenate([kb_past, kb.astype(kb_past.dtype)], axis=1)
    vb_all = jnp.concatenate([vb_past, vb.astype(vb_past.dtype)], axis=1)
    cum = jnp.cumsum(jnp.concatenate([logf_past.astype(jnp.float32), logf], axis=1), axis=1)
    pos_k = jnp.arange(P + n, dtype=jnp.int32)
    pos_q = P + jnp.arange(n, dtype=jnp.int32)
    oa = fox_attend(qa, ka_all, va_all, cum[:, P:], cum, pos_q, pos_k)
    ob = sb_attend(qb, kb_all, vb_all, pos_q, pos_k)
    y = ab_merge(oa, ob, w_out)
    return y, ka, va, logf.astype(h.dtype), kb, vb

def mla_project(h, w_down, g_q, g_kv, w_uq, pos):
    B, T, _ = h.shape
    z = h @ w_down
    cq, ckv, kr = jnp.split(z, [Q_LORA, Q_LORA + KV_LORA], axis=-1)
    cq = rms_norm(cq, g_q)
    ckv = rms_norm(ckv, g_kv)
    q = (cq @ w_uq).reshape(B, T, MLA_HEADS, QK_NOPE + QK_ROPE)
    q_nope, q_rope = q[..., :QK_NOPE], rope(q[..., QK_NOPE:], pos)
    kr = rope(kr, pos)
    return q_nope, q_rope, ckv, kr

def split_ukv(w_ukv):
    w = w_ukv.reshape(KV_LORA, MLA_HEADS, QK_NOPE + V_DIM)
    return w[..., :QK_NOPE], w[..., QK_NOPE:]

def mla_attend_expanded(q_nope, q_rope, k_nope, k_rope, v, pos_q, pos_k):
    s = (jnp.einsum('bqhd,bkhd->bhqk', q_nope, k_nope).astype(jnp.float32)
         + jnp.einsum('bqhr,bkr->bhqk', q_rope, k_rope).astype(jnp.float32)) * ((QK_NOPE + QK_ROPE) ** -0.5)
    p = jax.nn.softmax(jnp.where(chunk_visible(pos_q, pos_k), s, NEG_INF), axis=-1)
    return jnp.einsum('bhqk,bkhd->bqhd', p.astype(v.dtype), v)

def mla_attend_latent(q_nope, q_rope, ckv, k_rope, w_uk, w_uv, pos_q, pos_k):
    q_lat = jnp.einsum('bqhd,chd->bqhc', q_nope, w_uk)
    s = (jnp.einsum('bqhc,bkc->bhqk', q_lat, ckv).astype(jnp.float32)
         + jnp.einsum('bqhr,bkr->bhqk', q_rope, k_rope).astype(jnp.float32)) * ((QK_NOPE + QK_ROPE) ** -0.5)
    p = jax.nn.softmax(jnp.where(chunk_visible(pos_q, pos_k), s, NEG_INF), axis=-1)
    o_lat = jnp.einsum('bhqk,bkc->bqhc', p.astype(ckv.dtype), ckv)
    return jnp.einsum('bqhc,chd->bqhd', o_lat, w_uv)

def mla_prompt(h, w_down, g_q, g_kv, w_uq, w_ukv, w_out):
    B, S, _ = h.shape
    nb = S // Q_BLOCK
    pos = jnp.arange(S, dtype=jnp.int32)
    q_nope, q_rope, ckv, kr = mla_project(h, w_down, g_q, g_kv, w_uq, pos)
    w_uk, w_uv = split_ukv(w_ukv)
    k_nope = jnp.einsum('bsc,chd->bshd', ckv, w_uk)
    v = jnp.einsum('bsc,chd->bshd', ckv, w_uv)

    def step(blk):
        qn_b, qr_b, pos_b = blk
        return mla_attend_expanded(qn_b, qr_b, k_nope, kr, v, pos_b, pos)

    o = from_blocks(lax.map(step, (to_blocks(q_nope, nb), to_blocks(q_rope, nb), pos.reshape(nb, Q_BLOCK))))
    y = o.reshape(B, S, MLA_HEADS * V_DIM) @ w_out
    return y, ckv, kr

def mla_sample(h, ckv_past, kr_past, w_down, g_q, g_kv, w_uq, w_ukv, w_out):
    B, n, _ = h.shape
    P = ckv_past.shape[1]
    pos_q = P + jnp.arange(n, dtype=jnp.int32)
    pos_k = jnp.arange(P + n, dtype=jnp.int32)
    q_nope, q_rope, ckv, kr = mla_project(h, w_down, g_q, g_kv, w_uq, pos_q)
    w_uk, w_uv = split_ukv(w_ukv)
    ckv_all = jnp.concatenate([ckv_past, ckv.astype(ckv_past.dtype)], axis=1)
    kr_all = jnp.concatenate([kr_past, kr.astype(kr_past.dtype)], axis=1)
    o = mla_attend_latent(q_nope, q_rope, ckv_all, kr_all, w_uk, w_uv, pos_q, pos_k)
    y = o.reshape(B, n, MLA_HEADS * V_DIM) @ w_out
    return y, ckv, kr

def hier_moe(h, w_group, b_group, w_router, b_router, w_gate, w_up, w_down):
    x = h.reshape(-1, D_MODEL)
    g_logits = (x @ w_group).astype(jnp.float32) + b_group.astype(jnp.float32)
    g_prob = jax.nn.softmax(g_logits, axis=-1)
    g_idx = jnp.argmax(g_logits, axis=-1)
    g_gate = jnp.take_along_axis(g_prob, g_idx[:, None], axis=1)[:, 0]
    e_logits = jnp.einsum('td,gde->tge', x, w_router).astype(jnp.float32) + b_router.astype(jnp.float32)
    e_sel = jnp.take_along_axis(e_logits, g_idx[:, None, None], axis=1)[:, 0]
    top_v, top_i = lax.top_k(e_sel, TOP_K_IN_GROUP)
    top_w = jax.nn.softmax(top_v, axis=-1)
    w_e = jnp.sum(jax.nn.one_hot(top_i, EXPERTS_PER_GROUP, dtype=jnp.float32) * top_w[..., None], axis=1)
    comb = (jax.nn.one_hot(g_idx, N_GROUPS, dtype=jnp.float32)[:, :, None]
            * (g_gate[:, None] * w_e)[:, None, :]).astype(x.dtype)
    y = jnp.zeros_like(x)
    for g in range(N_GROUPS):
        a = jnp.einsum('td,edf->tef', x, w_gate[g])
        u = jnp.einsum('td,edf->tef', x, w_up[g])
        hid = jax.nn.silu(a) * u * comb[:, g, :, None]
        y = y + jnp.einsum('tef,efd->td', hid, w_down[g])
    return y.reshape(h.shape)

def setup_inputs(seed: int = 0) -> dict:
    key = jax.random.key(seed)
    ks = jax.random.split(key, 32)
    nrm = lambda k, shape, scale: jax.random.normal(k, shape, jnp.float32) * scale
    D = D_MODEL
    return {
        'x_prompt': nrm(ks[0], (BATCH, SEQ, D), 1.0),
        'x_sample': nrm(ks[1], (DEC_BATCH, DEC_SEQ, D), 1.0),
        'cache_fox_k': nrm(ks[2], (N_AB_LAYERS, DEC_BATCH, PAST_LEN, FOX_HEADS, HEAD_DIM), 1.0),
        'cache_fox_v': nrm(ks[3], (N_AB_LAYERS, DEC_BATCH, PAST_LEN, FOX_HEADS, HEAD_DIM), 1.0),
        'cache_fox_logf': jax.nn.log_sigmoid(FORGET_BIAS_INIT + nrm(ks[4], (N_AB_LAYERS, DEC_BATCH, PAST_LEN, FOX_HEADS), 1.0)),
        'cache_sb_k': nrm(ks[5], (N_AB_LAYERS, DEC_BATCH, PAST_LEN, SB_HEADS, HEAD_DIM), 1.0),
        'cache_sb_v': nrm(ks[6], (N_AB_LAYERS, DEC_BATCH, PAST_LEN, SB_HEADS, HEAD_DIM), 1.0),
        'cache_mla_ckv': nrm(ks[7], (N_MLA_LAYERS, DEC_BATCH, PAST_LEN, KV_LORA), 1.0),
        'cache_mla_krope': nrm(ks[8], (N_MLA_LAYERS, DEC_BATCH, PAST_LEN, QK_ROPE), 1.0),
        'ab_w_in': nrm(ks[9], (N_AB_LAYERS, D, AB_IN), D ** -0.5),
        'ab_b_forget': FORGET_BIAS_INIT + nrm(ks[10], (N_AB_LAYERS, FOX_HEADS), 0.1),
        'ab_w_out': nrm(ks[11], (N_AB_LAYERS, AB_MIX, D), AB_MIX ** -0.5 * DEEPNORM_BETA),
        'mla_w_down': nrm(ks[12], (N_MLA_LAYERS, D, MLA_DOWN), D ** -0.5),
        'mla_g_q': 1.0 + nrm(ks[13], (N_MLA_LAYERS, Q_LORA), 0.01),
        'mla_g_kv': 1.0 + nrm(ks[14], (N_MLA_LAYERS, KV_LORA), 0.01),
        'mla_w_uq': nrm(ks[15], (N_MLA_LAYERS, Q_LORA, MLA_HEADS * (QK_NOPE + QK_ROPE)), Q_LORA ** -0.5),
        'mla_w_ukv': nrm(ks[16], (N_MLA_LAYERS, KV_LORA, MLA_HEADS * (QK_NOPE + V_DIM)), KV_LORA ** -0.5),
        'mla_w_out': nrm(ks[17], (N_MLA_LAYERS, MLA_HEADS * V_DIM, D), (MLA_HEADS * V_DIM) ** -0.5 * DEEPNORM_BETA),
        'moe_w_group': nrm(ks[18], (DEPTH, D, N_GROUPS), D ** -0.5),
        'moe_b_group': nrm(ks[19], (DEPTH, N_GROUPS), 0.01),
        'moe_w_router': nrm(ks[20], (DEPTH, N_GROUPS, D, EXPERTS_PER_GROUP), D ** -0.5),
        'moe_b_router': nrm(ks[21], (DEPTH, N_GROUPS, EXPERTS_PER_GROUP), 0.01),
        'moe_w_gate': nrm(ks[22], (DEPTH, N_GROUPS, EXPERTS_PER_GROUP, D, EXPERT_HIDDEN), D ** -0.5),
        'moe_w_up': nrm(ks[23], (DEPTH, N_GROUPS, EXPERTS_PER_GROUP, D, EXPERT_HIDDEN), D ** -0.5),
        'moe_w_down': nrm(ks[24], (DEPTH, N_GROUPS, EXPERTS_PER_GROUP, EXPERT_HIDDEN, D), EXPERT_HIDDEN ** -0.5 * DEEPNORM_BETA),
        'ln_g': 1.0 + nrm(ks[25], (DEPTH, 2, D), 0.01),
        'ln_b': nrm(ks[26], (DEPTH, 2, D), 0.01),
    }

def reference(x_prompt, x_sample, cache_fox_k, cache_fox_v, cache_fox_logf, cache_sb_k, cache_sb_v,
              cache_mla_ckv, cache_mla_krope, ab_w_in, ab_b_forget, ab_w_out, mla_w_down, mla_g_q,
              mla_g_kv, mla_w_uq, mla_w_ukv, mla_w_out, moe_w_group, moe_b_group, moe_w_router,
              moe_b_router, moe_w_gate, moe_w_up, moe_w_down, ln_g, ln_b):
    xp, xs = x_prompt, x_sample
    fk_p, fv_p, fl_p, sk_p, sv_p, mc_p, mr_p = [], [], [], [], [], [], []
    fk_s, fv_s, fl_s, sk_s, sv_s, mc_s, mr_s = [], [], [], [], [], [], []
    for layer in range(DEPTH):
        i = layer // 2
        if layer % 2 == 0:
            mp, ka, va, lf, kb, vb = ab_prompt(xp, ab_w_in[i], ab_b_forget[i], ab_w_out[i])
            ms, ka2, va2, lf2, kb2, vb2 = ab_sample(xs, cache_fox_k[i], cache_fox_v[i], cache_fox_logf[i],
                                                    cache_sb_k[i], cache_sb_v[i],
                                                    ab_w_in[i], ab_b_forget[i], ab_w_out[i])
            fk_p.append(ka); fv_p.append(va); fl_p.append(lf); sk_p.append(kb); sv_p.append(vb)
            fk_s.append(ka2); fv_s.append(va2); fl_s.append(lf2); sk_s.append(kb2); sv_s.append(vb2)
        else:
            mp, ckv, kr = mla_prompt(xp, mla_w_down[i], mla_g_q[i], mla_g_kv[i], mla_w_uq[i],
                                     mla_w_ukv[i], mla_w_out[i])
            ms, ckv2, kr2 = mla_sample(xs, cache_mla_ckv[i], cache_mla_krope[i], mla_w_down[i], mla_g_q[i],
                                       mla_g_kv[i], mla_w_uq[i], mla_w_ukv[i], mla_w_out[i])
            mc_p.append(ckv); mr_p.append(kr); mc_s.append(ckv2); mr_s.append(kr2)
        xp = layer_norm(DEEPNORM_ALPHA * xp + mp, ln_g[layer, 0], ln_b[layer, 0])
        xs = layer_norm(DEEPNORM_ALPHA * xs + ms, ln_g[layer, 0], ln_b[layer, 0])
        fp = hier_moe(xp, moe_w_group[layer], moe_b_group[layer], moe_w_router[layer], moe_b_router[layer],
                      moe_w_gate[layer], moe_w_up[layer], moe_w_down[layer])
        fs = hier_moe(xs, moe_w_group[layer], moe_b_group[layer], moe_w_router[layer], moe_b_router[layer],
                      moe_w_gate[layer], moe_w_up[layer], moe_w_down[layer])
        xp = layer_norm(DEEPNORM_ALPHA * xp + fp, ln_g[layer, 1], ln_b[layer, 1])
        xs = layer_norm(DEEPNORM_ALPHA * xs + fs, ln_g[layer, 1], ln_b[layer, 1])
    return (xp, xs,
            jnp.stack(fk_p), jnp.stack(fv_p), jnp.stack(fl_p), jnp.stack(sk_p), jnp.stack(sv_p),
            jnp.stack(mc_p), jnp.stack(mr_p),
            jnp.stack(fk_s), jnp.stack(fv_s), jnp.stack(fl_s), jnp.stack(sk_s), jnp.stack(sv_s),
            jnp.stack(mc_s), jnp.stack(mr_s))


_drawn_inputs = setup_inputs


def setup_inputs(seed=0):
    import zlib

    import numpy as np

    out = dict(_drawn_inputs(seed))
    spreads = {}
    factors = {'cache_fox_logf': 5.607,
     'cache_sb_k': 3.902,
     'cache_mla_krope': 3.602,
     'mla_g_q': 8.0,
     'mla_g_kv': 5.872,
     'moe_b_group': 5.658,
     'moe_b_router': 6.227}
    for name, (base, spread) in spreads.items():
        noise = np.random.default_rng([zlib.crc32(name.encode()), seed]).standard_normal(out[name].shape)
        drawn = base * np.exp(spread * noise) if base else spread * noise
        out[name] = jnp.asarray(drawn.astype(out[name].dtype))
    for name, factor in factors.items():
        out[name] = (out[name] * factor).astype(out[name].dtype)
    return out
```

```python
from contextlib import ExitStack

import concourse.bass as bass
from concourse import mybir

F32 = mybir.dt.float32
I32 = mybir.dt.int32
U32 = mybir.dt.uint32
ALU = mybir.AluOpType
ACT = mybir.ActivationFunctionType
AX_X = mybir.AxisListType.X

P = 128
BANK = 512
D = 1024
J = D // P
SEQ, NEW, PAST = 512, 64, 512
T = SEQ + NEW
NT = 5
TP = NT * P
ROWS = [P, P, P, P, NEW]
KEYS = SEQ + PAST + NEW
NEW_AT = SEQ + PAST
VB = 9
KEY_RANGE = [(0, P), (0, 2 * P), (0, 3 * P), (0, 4 * P), (SEQ, KEYS)]
HD = 64
HEADS = 8
ROPE = 32
QW = HD + ROPE
Q_LORA, KV_LORA = 384, 256
JQ, JC = Q_LORA // P, KV_LORA // P
DOWN = Q_LORA + KV_LORA + ROPE
GROUPS, PER_GROUP, NE = 4, 8, 32
EH = 256
JE = EH // P
CB = 64
RING = 4
NB_MAX = NE + (2 * T) // CB
NB_TAB = -(-NB_MAX // RING) * RING + RING
ALPHA = 4.0 ** 0.25
LN_EPS, RMS_EPS = 1e-5, 1e-6
NEG = -1e30
FAR = 1e6
UNITS = 2 * NT
BLOCKS_OF = [1, 2, 3, 4, 5]


def hold(eng, passed, *counts):
    for sem, count in counts:
        eng.wait_ge(sem, count)
    eng.sem_inc(passed, 1)


class Steps:

    def __init__(self, eng, sem, base=0, passed=None):
        self.eng, self.sem, self.base, self.n, self.passed = eng, sem, base, 0, passed

    def then(self, ins):
        self.n += 1
        ins.then_inc(self.sem, 1)
        self.eng.wait_ge(self.sem, self.base + self.n)
        if self.passed is not None:
            self.eng.sem_inc(self.passed, 1)


class Core:

    def __init__(self, nc, ctx, dram):
        self.nc, self.ctx = nc, ctx
        self.x_rows = dram["x_rows"]
        self.x_t = dram["x_t"]
        self.w_ab = dram["w_ab"]
        self.w_f = dram["w_f"]
        self.b_f = dram["b_f"]
        self.logf_past = dram["logf_past"]
        self.k_past = dram["k_past"]
        self.v_past = dram["v_past"]
        self.ab_w_out = dram["ab_w_out"]
        self.mla_w_out = dram["mla_w_out"]
        self.w_mla_down = dram["w_mla_down"]
        self.g_q = dram["g_q"]
        self.g_kv = dram["g_kv"]
        self.w_uq = dram["w_uq"]
        self.w_ukv = dram["w_ukv"]
        self.ckv_past = dram["ckv_past"]
        self.kr_past = dram["kr_past"]
        self.cos = dram["cos"]
        self.sin = dram["sin"]
        self.w_r = dram["w_r"]
        self.b_r = dram["b_r"]
        self.w_gate = dram["w_gate"]
        self.w_up = dram["w_up"]
        self.w_down = dram["w_down"]
        self.ln_g = dram["ln_g"]
        self.ln_b = dram["ln_b"]
        self.o_y_p = dram["o_y_p"]
        self.o_y_s = dram["o_y_s"]
        self.o_logf_p = dram["o_logf_p"]
        self.o_ckv_p = dram["o_ckv_p"]
        self.o_kr_p = dram["o_kr_p"]
        self.o_logf_s = dram["o_logf_s"]
        self.o_ckv_s = dram["o_ckv_s"]
        self.o_kr_s = dram["o_kr_s"]
        self.cum_d = dram["cum_d"]
        self.x_d = dram["x_d"]
        self.y_d = dram["y_d"]
        self.o_kv = dram["o_kv"]

        def sb(name, shape, dt=F32):
            return ctx.enter_context(nc.sbuf_tensor(name, shape, dt))

        self.psum = ctx.enter_context(nc.psum_tensor("psum", [P, 8, BANK], F32))
        self.passed = ctx.enter_context(nc.semaphore("passed"))
        self.signals = []
        self.sb = sb
        self.xT = sb("xT", [P, J, TP])
        self.x = sb("x", [P, NT, D])
        self.mix = sb("mix", [P, NT, D])
        self.ident = sb("ident", [P, P])
        self.cum_tok = sb("cum_tok", [P, NT, HEADS])
        self.half = sb("half", [P, 1])
        self.logits = sb("logits", [P, NT, GROUPS + NE])
        self.w_gu = [sb(f"w_gu{s}", [P, J, 2 * EH]) for s in range(3)]
        self.w_dn = [sb(f"w_dn{s}", [P, JE, D]) for s in range(3)]


def new_signal(k, name):
    k.signals.append(k.nc.alloc_semaphore(name))
    return k.signals[-1]


def clear_signals(k):
    k.nc.clear_and_free_semaphores(k.signals)
    k.signals = []
    k.nc.all_engine_barrier()


def banks(k, first, count):
    return k.psum[:, first:first + count, :].rearrange("p b n -> p (b n)")


def setup_and_gates(k):
    nc = k.nc
    with ExitStack() as c:
        sb = lambda n, s, d=F32: c.enter_context(nc.sbuf_tensor(n, s, d))
        sem = lambda n: new_signal(k, n)
        wf = sb("wf", [P, J, HEADS])
        bf = sb("bf", [HEADS, 1])
        logf = sb("logf", [HEADS, KEYS])
        cum = sb("cum", [HEADS, KEYS])
        ones = sb("ones", [HEADS, KEYS])
        t_abs = sb("t_abs", [HEADS, T])
        t_exp = sb("t_exp", [HEADS, T])
        t_ln = sb("t_ln", [HEADS, T])
        low = sb("low", [HEADS, T])
        tok = sb("tok", [P, NT, HEADS])
        xt_in, x_in, f_in, filled, z_ready, act_step, dve_step, out_sem, tok_t, tok_e, cum_ready = (
            sem(n) for n in ("g_xt_in", "g_x_in", "g_f_in", "g_filled", "g_z_ready", "g_act_step", "g_dve_step",
                             "g_out", "g_tok_t", "g_tok_e", "g_cum_ready"))
        z = banks(k, 0, 2)[0:HEADS, 0:T]
        trans = banks(k, 2, 1)

        with nc.Block() as block:

            @block.sync
            def _(sp):
                sp.dma_start(wf[:], k.w_f).then_inc(f_in, 16)
                sp.dma_start(bf[:], k.b_f).then_inc(f_in, 16)
                sp.dma_start(k.xT[:, :, 0:T], k.x_t).then_inc(xt_in, 16)
                sp.dma_start(logf[:, SEQ:NEW_AT], k.logf_past).then_inc(f_in, 16)
                sp.dma_start(k.x[:, 0:4, :], k.x_rows[0:SEQ, :].rearrange("(t p) d -> p t d", p=P)).then_inc(x_in, 16)
                sp.dma_start(k.x[0:NEW, 4, :], k.x_rows[SEQ:T, :]).then_inc(x_in, 16)
                sp.wait_ge(cum_ready, 2)
                sp.dma_start(k.cum_d, cum[:]).then_inc(out_sem, 16)
                sp.wait_ge(tok_e, 2)
                sp.dma_start(k.o_logf_p.rearrange("a b (t p) h -> p (a b t) h", p=P), tok[:, 0:4, :]).then_inc(out_sem, 16)
                sp.dma_start(k.o_logf_s.rearrange("a b t h -> (a b t) h"), tok[0:NEW, 4, :]).then_inc(out_sem, 16)
                sp.wait_ge(out_sem, 48)
                sp.wait_ge(x_in, 32)

            @block.gpsimd
            def _(pool):
                pool.memset(k.ident[:], 0.0).then_inc(filled, 1)
                pool.wait_ge(filled, 1)
                pool.affine_select(out=k.ident[:], in_=k.ident[:], compare_op=ALU.not_equal, fill=1.0, base=0,
                                   pattern=[[-1, P]], channel_multiplier=1).then_inc(filled, 1)
                for n, (dst, value) in enumerate(((k.half[:], -0.5), (ones[:], 1.0), (k.xT[:, :, T:TP], 0.0), (k.x[NEW:P, 4, :], 0.0),
                                                  (k.mix[NEW:P, 4, :], 0.0), (k.cum_tok[NEW:P, 4, :], 0.0))):
                    pool.wait_ge(filled, n + 2)
                    pool.memset(dst, value).then_inc(filled, 1)

            @block.tensor
            def _(pe):
                pe.wait_ge(xt_in, 16)
                pe.wait_ge(f_in, 48)
                for j in range(J):
                    nc.tensor.matmul(z[:, 0:SEQ], wf[:, j, :], k.xT[:, j, 0:SEQ], start=(j == 0), stop=(j == J - 1))
                    last = nc.tensor.matmul(z[:, SEQ:T], wf[:, j, :], k.xT[:, j, SEQ:T], start=(j == 0), stop=(j == J - 1))
                last.then_inc(z_ready, 1)
                pe.wait_ge(filled, 2)
                pe.wait_ge(cum_ready, 2)
                for n, src in enumerate((logf, cum)):
                    for t in range(NT):
                        at = t * P if t < 4 else NEW_AT
                        last = nc.tensor.transpose(trans[0:ROWS[t], (n * NT + t) * HEADS:(n * NT + t + 1) * HEADS],
                                                   src[:, at:at + ROWS[t]], k.ident[0:HEADS, 0:HEADS])
                last.then_inc(tok_t, 1)

            @block.scalar
            def _(act):
                steps = Steps(act, act_step)
                act.wait_ge(z_ready, 1)
                act.wait_ge(f_in, 48)
                steps.then(nc.scalar.activation(t_abs[:], z, ACT.Abs, bias=bf[:, 0:1]))
                steps.then(nc.scalar.activation(t_exp[:], t_abs[:], ACT.Exp, scale=-1.0))
                nc.scalar.activation(t_ln[:], t_exp[:], ACT.Ln, bias=1.0).then_inc(act_step, 1)

            @block.vector
            def _(dve):
                steps = Steps(dve, dve_step)
                dve.wait_ge(f_in, 48)
                dve.wait_ge(act_step, 1)
                steps.then(nc.vector.tensor_scalar(low[:], z, bf[:, 0:1], 0.0, ALU.add, ALU.min))
                dve.wait_ge(act_step, 3)
                nc.vector.tensor_tensor(logf[:, 0:SEQ], low[:, 0:SEQ], t_ln[:, 0:SEQ], ALU.subtract).then_inc(dve_step, 1)
                steps.n += 1
                steps.then(nc.vector.tensor_tensor(logf[:, NEW_AT:KEYS], low[:, SEQ:T], t_ln[:, SEQ:T], ALU.subtract))
                dve.wait_ge(filled, 8)
                nc.vector.tensor_tensor_scan(cum[:, 0:SEQ], ones[:, 0:SEQ], logf[:, 0:SEQ], 0.0, ALU.mult, ALU.add).then_inc(cum_ready, 1)
                nc.vector.tensor_tensor_scan(cum[:, SEQ:KEYS], ones[:, SEQ:KEYS], logf[:, SEQ:KEYS], 0.0, ALU.mult, ALU.add).then_inc(cum_ready, 1)
                dve.wait_ge(tok_t, 1)
                for n, dst in enumerate((tok, k.cum_tok)):
                    at = n * NT * HEADS
                    nc.vector.tensor_copy(dst[:, 0:4, :], trans[:, at:at + 4 * HEADS].rearrange("p (t h) -> p t h", h=HEADS)).then_inc(tok_e, 1)
                    nc.vector.tensor_copy(dst[0:NEW, 4, :], trans[0:NEW, at + 4 * HEADS:at + 5 * HEADS]).then_inc(tok_e, 1)


def unit_of(u):
    return u // NT, u % NT


def attend_pairs(k, kind, first, trips, m):
    nc, passed = k.nc, k.passed
    fox, sbk, mla = kind == "fox", kind == "sb", kind == "mla"
    with ExitStack() as c:
        sb = lambda n, s, d=F32: c.enter_context(nc.sbuf_tensor(f"{kind}_{n}", s, d))
        sem = lambda n: new_signal(k, f"{kind}_{n}")
        v_all = sb("v_all", [P, VB, P])
        score = sb("score", [P, 2, T + 0])
        probs = sb("probs", [P, 2, T])
        probsT = sb("probsT", [P, 2, 5, P])
        small = sb("small", [P, 2, 4])
        if mla:
            wq = sb("wq", [P, JQ, 2 * QW])
            wkv = sb("wkv", [P, JC, 2 * P])
            q_tok = sb("q_tok", [P, NT, 2, QW])
            rot = sb("rot", [P, 4, NT, 2, ROPE // 2])
            qh = [sb(f"q{h}", [QW, T]) for h in range(2)]
            kh = m["kh"]
        else:
            wp = [sb(f"w_{n}", [P, J, P]) for n in "qkv"]
            qz = [sb(f"q{h}", [P, T]) for h in range(2)]
            qh = qz
            kT = sb("kT", [P, KEYS])
            kh = [kT, kT]
            vT = sb("vT", [P, T])
            k_tok = sb("k_tok", [P, NT, P])
        if fox:
            cumk = sb("cumk", [P, 2, KEYS])
            bias = sb("bias", [P, 2, T])
            cumq = sb("cumq", [P, 2, NT])
        if sbk:
            rest = sb("rest", [P, 2, T])
            ones = sb("ones", [P, T])
        if mla:
            names = ("zeroed w0_in w1_in projected proj_act proj_dve tok_ready tok_act tok_dve scores_ready scored "
                     "probs_ready probsT_ready probsT_used o_ready o_done dve_step act_step roped").split()
        else:
          names = ("zeroed w0_in w1_in w2_in kp_in vp_in cumk_in cumq_ready projected proj_act proj_dve tok_ready "
                 "tok_act tok_dve k_out v_out scores_ready scored bias_ready bias_step probs_ready probsT_ready "
                 "probsT_used o_ready o_done dve_step act_step soft_ready masked rest_done logit_ready").split()
        s = {n: sem(n) for n in names}
        slot = lambda u: banks(k, 2 * (u % 2), 2)
        bank_t, bank_o = banks(k, 4, 1), banks(k, 5, 1)
        proj = banks(k, 6, 2)

        def loop(eng, body):
            with eng.Fori(0, trips) as i:
                body(i)

        def sp_loads(sp, i):
            if mla:
                hold(sp, passed, (s["projected"], i * 3))
                sp.dma_start(wq[:], k.w_uq[bass.ds(i, 1), :, :].rearrange("a p n -> p (a n)")).then_inc(s["w0_in"], 16)
                sp.dma_start(wkv[:], k.w_ukv[bass.ds(i, 1), :, :].rearrange("a p n -> p (a n)")).then_inc(s["w1_in"], 16)
                return
            for n in range(3):
                hold(sp, passed, (s["projected"], i * 3))
                sp.dma_start(wp[n][:].rearrange("p j n -> p (j n)"),
                             k.w_ab[bass.ds((i + first) * 3 + n, 1), :, :].rearrange("a p n -> p (a n)")).then_inc(s[f"w{n}_in"], 16)
            hold(sp, passed, (s["o_ready"], i * UNITS))
            sp.dma_start(kT[:, SEQ:NEW_AT], k.k_past[bass.ds(i + first, 1), :, :].rearrange("a p n -> p (a n)")).then_inc(s["kp_in"], 16)
            sp.dma_start(v_all[:, 4:8, :].rearrange("p b n -> p (b n)"),
                         k.v_past[bass.ds(i + first, 1), :, :].rearrange("a p n -> p (a n)")).then_inc(s["vp_in"], 16)
            if fox:
                for h in range(2):
                    hold(sp, passed, (s["bias_ready"], i * UNITS))
                    sp.dma_start(cumk[:, h, :], k.cum_d[bass.ds(2 * (i + first) + h, 1), :].to_broadcast([P, KEYS])).then_inc(s["cumk_in"], 16)

        def sp_outs(sp, i):
            if mla:
                return
            o_k_p, o_v_p, o_k_s, o_v_s = k.o_kv[kind]
            cols = bass.ds(i * P, P)
            hold(sp, passed, (s["tok_act"], 2 * i + 1), (s["tok_dve"], 2 * i + 1))
            sp.dma_start(o_k_p.rearrange("(t p) c -> p t c", p=P)[:, :, cols], k_tok[:, 0:4, :]).then_inc(s["k_out"], 16)
            sp.dma_start(o_k_s[:, cols], k_tok[0:NEW, 4, :]).then_inc(s["k_out"], 16)
            hold(sp, passed, (s["tok_act"], 2 * i + 2), (s["tok_dve"], 2 * i + 2))
            sp.dma_start(o_v_p.rearrange("(t p) c -> p t c", p=P)[:, :, cols], v_all[:, 0:4, :]).then_inc(s["v_out"], 16)
            sp.dma_start(o_v_s[:, cols], v_all[0:NEW, 8, :]).then_inc(s["v_out"], 16)

        with nc.Block() as block:

            @block.sync
            def _(sp):
                sp_loads(sp, 0)
                if trips > 1:
                    with sp.Fori(0, trips - 1) as i:
                        sp_outs(sp, i)
                        sp_loads(sp, i + 1)
                sp_outs(sp, trips - 1)
                if not mla:
                    sp.wait_ge(s["k_out"], 32 * trips)
                    sp.wait_ge(s["v_out"], 32 * trips)

            def pe_project(pe, i):
                for n in range(3):
                    hold(pe, passed, (s[f"w{n}_in"], 16 * (i + 1)), *[(s["proj_act"], 3 * i + n), (s["proj_dve"], 3 * i + n)] * (n > 0))
                    for j in range(J):
                        nc.tensor.matmul(proj[:, 0:SEQ], wp[n][:, j, :], k.xT[:, j, 0:SEQ], start=(j == 0), stop=(j == J - 1))
                        last = nc.tensor.matmul(proj[:, SEQ:T], wp[n][:, j, :], k.xT[:, j, SEQ:T], start=(j == 0), stop=(j == J - 1))
                    last.then_inc(s["projected"], 1)
                for n, src in enumerate((kT, vT)):
                    hold(pe, passed, (s["proj_act"], 3 * i + 2 + n), (s["proj_dve"], 3 * i + 2 + n),
                         *([(s["tok_act"], 2 * i + 1), (s["tok_dve"], 2 * i + 1)] if n else [(s["o_done"], UNITS * i)]))
                    for t in range(NT):
                        at = NEW_AT if (t == 4 and n == 0) else t * P
                        dst = bank_t[:, t * P:(t + 1) * P] if t < 4 else bank_o[0:NEW, 0:P]
                        last = nc.tensor.transpose(dst, src[:, at:at + ROWS[t]], k.ident[:])
                    last.then_inc(s["tok_ready"], 1)

            def pe_project_mla(pe, i):
                hold(pe, passed, (s["w0_in"], 16 * (i + 1)), (s["w1_in"], 16 * (i + 1)))
                for t in range(NT):
                    dst = k.psum[0:ROWS[t], t if t < 4 else 6, 0:2 * QW]
                    for j in range(JQ):
                        last = nc.tensor.matmul(dst, m["cqT"][:, j, t * P:t * P + ROWS[t]], wq[:, j, :], start=(j == 0), stop=(j == JQ - 1))
                last.then_inc(s["projected"], 1)
                hold(pe, passed, (s["o_done"], UNITS * i))
                for dst, lo, hi in ((banks(k, 4, 1)[:, 0:512], 0, 512), (banks(k, 5, 1)[:, 0:512], 512, 1024), (banks(k, 7, 1)[:, 0:NEW], 1024, KEYS)):
                    for j in range(JC):
                        last = nc.tensor.matmul(dst, wkv[:, j, 0:P], m["ckvT"][:, j, lo:hi], start=(j == 0), stop=(j == JC - 1))
                last.then_inc(s["projected"], 1)
                for n, (bank, blocks) in enumerate(((6, range(4)), (7, range(4, 8)), (4, range(8, 9)))):
                    hold(pe, passed, (s["proj_act"], 2 * i + min(n + 1, 2)), (s["proj_dve"], 2 * i + min(n + 1, 2)))
                    for b in blocks:
                        rows = P if b < 8 else NEW
                        for j in range(JC):
                            last = nc.tensor.matmul(k.psum[0:rows, bank, (b % 4) * P:(b % 4 + 1) * P], m["ckvT"][:, j, b * P:b * P + rows],
                                                    wkv[:, j, P:2 * P], start=(j == 0), stop=(j == JC - 1))
                last.then_inc(s["projected"], 1)
                hold(pe, passed, (s["roped"], i + 1))
                for h in range(2):
                    for t in range(NT):
                        last = nc.tensor.transpose(slot(h)[0:QW, t * P:t * P + ROWS[t]], q_tok[0:ROWS[t], t, h, :], k.ident[0:ROWS[t], 0:ROWS[t]])
                last.then_inc(s["tok_ready"], 1)

            def pe_scores(pe, i, u):
                h, t = unit_of(u)
                lo, hi = KEY_RANGE[t]
                n = i * UNITS + u
                if u == 0 and mla:
                    hold(pe, passed, (s["tok_act"], 2 * i + 2), (s["tok_dve"], 2 * i + 2))
                elif u == 0:
                    hold(pe, passed, (s["proj_act"], 3 * i + 3), (s["proj_dve"], 3 * i + 3), (s["kp_in"], 16 * (i + 1)))
                elif u >= 2:
                    hold(pe, passed, (s["scored"], n - 1))
                q = qh[h][0:QW, t * P:t * P + ROWS[t]] if mla else qh[h][:, t * P:t * P + ROWS[t]]
                key = kh[h][0:QW, lo:hi] if mla else kh[h][:, lo:hi]
                last = nc.tensor.matmul(slot(u)[0:ROWS[t], 0:min(hi - lo, BANK)], q, key[:, 0:min(hi - lo, BANK)], start=True, stop=True)
                if hi - lo > BANK:
                    last = nc.tensor.matmul(slot(u)[0:ROWS[t], BANK:hi - lo], q, key[:, BANK:hi - lo], start=True, stop=True)
                last.then_inc(s["scores_ready"], 1)

            def pe_turn(pe, i, u):
                h, t = unit_of(u)
                n = i * UNITS + u
                hold(pe, passed, (s["probs_ready"], n + 1), (s["probsT_used"], n),
                     *[(s["tok_act"], 2 * i + 2), (s["tok_dve"], 2 * i + 2)] * (u == 0))
                for b in range(BLOCKS_OF[t]):
                    wide = NEW if b == 4 else P
                    last = nc.tensor.transpose(bank_t[0:wide, b * ROWS[t]:(b + 1) * ROWS[t]],
                                               probs[0:ROWS[t], u % 2, b * P:b * P + wide], k.ident[0:ROWS[t], 0:ROWS[t]])
                last.then_inc(s["probsT_ready"], 1)

            def pe_values(pe, i, u):
                h, t = unit_of(u)
                n = i * UNITS + u
                hold(pe, passed, (s["probsT_used"], n + 1), (s["o_done"], n), *([(s["vp_in"], 16 * (i + 1))] if u == 4 and not mla else []))
                first_block = 0 if t < 4 else 4
                for b in range(BLOCKS_OF[t]):
                    last = nc.tensor.matmul(bank_o[0:ROWS[t], 0:HD], probsT[:, u % 2, b, 0:ROWS[t]],
                                            v_all[:, first_block + b, h * HD:(h + 1) * HD], start=(b == 0), stop=(b == BLOCKS_OF[t] - 1))
                last.then_inc(s["o_ready"], 1)

            @block.tensor
            def _(pe):
                pe.wait_ge(s["zeroed"], m["zeroed"])

                def body(i):
                    if mla:
                        pe_project_mla(pe, i)
                    else:
                        pe_project(pe, i)
                    pe_scores(pe, i, 0)
                    pe_scores(pe, i, 1)
                    for u in range(UNITS):
                        pe_turn(pe, i, u)
                        if u + 2 < UNITS:
                            pe_scores(pe, i, u + 2)
                        pe_values(pe, i, u)
                loop(pe, body)

            @block.scalar
            def _(act):
                nc.scalar.preload_act_table_set("natural_log_exp_and_others")
                act.wait_ge(s["zeroed"], m["zeroed"])

                def copy_out(i):
                    if mla:
                        hold(act, passed, (s["projected"], 3 * i + 1))
                        nc.scalar.activation(q_tok[:, 0:4, :, :].rearrange("p t h c -> p t (h c)"), k.psum[:, 0:4, 0:2 * QW], ACT.Copy).then_inc(s["proj_act"], 1)
                        hold(act, passed, (s["projected"], 3 * i + 2))
                        nc.scalar.activation(kh[0][0:HD, 0:NEW_AT], banks(k, 4, 2)[0:HD, :], ACT.Copy)
                        nc.scalar.activation(kh[0][0:HD, NEW_AT:KEYS], banks(k, 7, 1)[0:HD, 0:NEW], ACT.Copy).then_inc(s["proj_act"], 1)
                        hold(act, passed, (s["projected"], 3 * i + 3))
                        nc.scalar.activation(v_all[:, 0:4, :].rearrange("p b c -> p (b c)"), banks(k, 6, 1), ACT.Copy).then_inc(s["tok_act"], 1)
                        hold(act, passed, (s["tok_ready"], i + 1))
                        nc.scalar.activation(qh[0][:, :], slot(0)[0:QW, 0:T], ACT.Copy).then_inc(s["tok_act"], 1)
                        return
                    hold(act, passed, (s["projected"], 3 * i + 1), (s["o_ready"], UNITS * i))
                    nc.scalar.activation(qz[0][0:HD, :], proj[0:HD, 0:T], ACT.Copy, scale=HD ** -0.5).then_inc(s["proj_act"], 1)
                    hold(act, passed, (s["projected"], 3 * i + 2))
                    nc.scalar.activation(kT[:, 0:SEQ], proj[:, 0:SEQ], ACT.Copy).then_inc(s["proj_act"], 1)
                    hold(act, passed, (s["projected"], 3 * i + 3))
                    nc.scalar.activation(vT[:, 0:SEQ], proj[:, 0:SEQ], ACT.Copy).then_inc(s["proj_act"], 1)
                    hold(act, passed, (s["tok_ready"], 2 * i + 1), (s["k_out"], 32 * i))
                    nc.scalar.activation(k_tok[:, 0:4, :].rearrange("p t c -> p (t c)"), bank_t, ACT.Copy).then_inc(s["tok_act"], 1)
                    hold(act, passed, (s["tok_ready"], 2 * i + 2), (s["v_out"], 32 * i))
                    nc.scalar.activation(v_all[:, 0:4, :].rearrange("p t c -> p (t c)"), bank_t, ACT.Copy).then_inc(s["tok_act"], 1)

                def soften(i, u):
                    _, t = unit_of(u)
                    rows, width = ROWS[t], KEY_RANGE[t][1] - KEY_RANGE[t][0]
                    n = i * UNITS + u
                    z, r = slot(u)[0:rows, 0:width], rest[0:rows, u % 2, 0:width]
                    steps = Steps(act, s["act_step"], base=2 * n, passed=passed)
                    hold(act, passed, (s["scores_ready"], n + 1), *[(s["scored"], n - 1)] * (u >= 2))
                    steps.then(nc.scalar.activation(r, z, ACT.Abs))
                    steps.then(nc.scalar.activation(r, r, ACT.Exp, scale=-1.0))
                    nc.scalar.activation(r, r, ACT.Ln, bias=1.0).then_inc(s["soft_ready"], 1)

                def exponent(i, u):
                    _, t = unit_of(u)
                    rows, width = ROWS[t], KEY_RANGE[t][1] - KEY_RANGE[t][0]
                    n = i * UNITS + u
                    hold(act, passed, (s["logit_ready"] if sbk else s["scored"], n + 1), *[(s["probsT_ready"], n - 1)] * (u >= 2))
                    if sbk:
                        nc.scalar.activation(probs[0:rows, u % 2, 0:width], score[0:rows, u % 2, 0:width], ACT.Exp).then_inc(s["probs_ready"], 1)
                    else:
                        nc.scalar.activation(probs[0:rows, u % 2, 0:width], score[0:rows, u % 2, 0:width], ACT.Exp, scale=-1.0,
                                             bias=small[0:rows, u % 2, 0:1], accum_out=small[0:rows, u % 2, 1:2]).then_inc(s["probs_ready"], 1)

                def turn_out(i, u):
                    _, t = unit_of(u)
                    n = i * UNITS + u
                    hold(act, passed, (s["probsT_ready"], n + 1), *[(s["o_ready"], n - 1)] * (u >= 2))
                    full = min(BLOCKS_OF[t], 4)
                    last = nc.scalar.activation(probsT[:, u % 2, 0:full, 0:ROWS[t]],
                                                bank_t[:, 0:full * ROWS[t]].rearrange("p (b q) -> p b q", q=ROWS[t]), ACT.Copy)
                    if t == 4:
                        last = nc.scalar.activation(probsT[0:NEW, u % 2, 4, 0:NEW], bank_t[0:NEW, 4 * NEW:5 * NEW], ACT.Copy)
                    last.then_inc(s["probsT_used"], 1)

                def body(i):
                    copy_out(i)
                    if sbk:
                        soften(i, 0)
                        soften(i, 1)
                        exponent(i, 0)
                        for u in range(UNITS):
                            if u + 2 < UNITS:
                                soften(i, u + 2)
                            if u + 1 < UNITS:
                                exponent(i, u + 1)
                            turn_out(i, u)
                    else:
                        exponent(i, 0)
                        for u in range(UNITS):
                            if u + 1 < UNITS:
                                exponent(i, u + 1)
                            turn_out(i, u)
                loop(act, body)

            @block.vector
            def _(dve):
                if not mla:
                    nc.vector.memset(qz[0][HD:P, :], 0.0).then_inc(s["zeroed"], 1)
                    nc.vector.memset(qz[1][0:HD, :], 0.0).then_inc(s["zeroed"], 1)
                else:
                    nc.vector.memset(q_tok[NEW:P, 4, :, :], 0.0).then_inc(s["zeroed"], 1)
                nc.vector.memset(v_all[NEW:P, 8, :], 0.0).then_inc(s["zeroed"], 1)
                nc.vector.memset(probsT[:, :, 4, :], 0.0).then_inc(s["zeroed"], 1)
                if sbk:
                    nc.vector.memset(ones[:], 1.0).then_inc(s["zeroed"], 1)
                dve.wait_ge(s["zeroed"], m["zeroed"])

                def copy_out(i):
                    if mla:
                        hold(dve, passed, (s["projected"], 3 * i + 1))
                        nc.vector.tensor_copy(q_tok[0:NEW, 4, :, :].rearrange("p h c -> p (h c)"), k.psum[0:NEW, 6, 0:2 * QW]).then_inc(s["proj_dve"], 1)
                        hold(dve, passed, (s["projected"], 3 * i + 2))
                        nc.vector.tensor_copy(kh[1][0:HD, 0:NEW_AT], banks(k, 4, 2)[HD:P, :])
                        nc.vector.tensor_copy(kh[1][0:HD, NEW_AT:KEYS], banks(k, 7, 1)[HD:P, 0:NEW]).then_inc(s["proj_dve"], 1)
                        steps = Steps(dve, s["act_step"], base=i, passed=passed)
                        half = ROPE // 2
                        x1, x2 = q_tok[:, :, :, HD:HD + half], q_tok[:, :, :, HD + half:QW]
                        both = lambda a: a.unsqueeze(2).to_broadcast([P, NT, 2, half])
                        hold(dve, passed, (s["proj_act"], 2 * i + 1), (s["proj_dve"], 2 * i + 1))
                        nc.vector.tensor_tensor(rot[:, 0], x1, both(m["cos"][:]), ALU.mult)
                        nc.vector.tensor_tensor(rot[:, 1], x2, both(m["sin"][:]), ALU.mult)
                        nc.vector.tensor_tensor(rot[:, 2], x1, both(m["sin"][:]), ALU.mult)
                        steps.then(nc.vector.tensor_tensor(rot[:, 3], x2, both(m["cos"][:]), ALU.mult))
                        nc.vector.tensor_tensor(x1, rot[:, 0], rot[:, 1], ALU.subtract)
                        nc.vector.tensor_tensor(x2, rot[:, 2], rot[:, 3], ALU.add).then_inc(s["roped"], 1)
                        hold(dve, passed, (s["projected"], 3 * i + 3))
                        nc.vector.tensor_copy(v_all[:, 4:8, :].rearrange("p b c -> p (b c)"), banks(k, 7, 1))
                        nc.vector.tensor_copy(v_all[0:NEW, 8, :], banks(k, 4, 1)[0:NEW, 0:P]).then_inc(s["tok_dve"], 1)
                        hold(dve, passed, (s["tok_ready"], i + 1))
                        nc.vector.tensor_copy(qh[1][:, :], slot(1)[0:QW, 0:T]).then_inc(s["tok_dve"], 1)
                        return
                    hold(dve, passed, (s["projected"], 3 * i + 1), (s["o_ready"], UNITS * i))
                    nc.vector.tensor_scalar(qz[1][HD:P, :], proj[HD:P, 0:T], HD ** -0.5, None, ALU.mult).then_inc(s["proj_dve"], 1)
                    hold(dve, passed, (s["projected"], 3 * i + 2))
                    nc.vector.tensor_copy(kT[:, NEW_AT:KEYS], proj[:, SEQ:T]).then_inc(s["proj_dve"], 1)
                    if fox:
                        hold(dve, passed, (s["bias_ready"], UNITS * i))
                        for h in range(2):
                            last = nc.vector.tensor_copy(cumq[:, h, :].unsqueeze(2), k.cum_tok[:, :, bass.ds(2 * i + h, 1)])
                        last.then_inc(s["cumq_ready"], 1)
                    hold(dve, passed, (s["projected"], 3 * i + 3))
                    nc.vector.tensor_copy(vT[:, SEQ:T], proj[:, SEQ:T]).then_inc(s["proj_dve"], 1)
                    hold(dve, passed, (s["tok_ready"], 2 * i + 1), (s["k_out"], 32 * i))
                    nc.vector.tensor_copy(k_tok[0:NEW, 4, :], bank_o[0:NEW, 0:P]).then_inc(s["tok_dve"], 1)
                    hold(dve, passed, (s["tok_ready"], 2 * i + 2), (s["v_out"], 32 * i))
                    nc.vector.tensor_copy(v_all[0:NEW, 8, :], bank_o[0:NEW, 0:P]).then_inc(s["tok_dve"], 1)

                def spec(u):
                    _, t = unit_of(u)
                    return ROWS[t], KEY_RANGE[t][1] - KEY_RANGE[t][0]

                def logits(i, u):
                    rows, width = spec(u)
                    _, t = unit_of(u)
                    n = i * UNITS + u
                    hold(dve, passed, (s["scores_ready"], n + 1), *([(s["bias_ready"], n + 1)] if fox else []),
                         *[(s["probs_ready"], n - 1)] * (u >= 2))
                    add = bias[0:rows, u % 2, 0:width] if fox else m["mask"][0:rows, m["mask_width"][t] - width:m["mask_width"][t]]
                    nc.vector.tensor_tensor_reduce(out=score[0:rows, u % 2, 0:width], in0=slot(u)[0:rows, 0:width], in1=add,
                                                   scale=-1.0 if fox else -float(QW) ** -0.5, scalar=3e38, op0=ALU.add, op1=ALU.min,
                                                   accum_out=small[0:rows, u % 2, 0:1]).then_inc(s["scored"], 1)

                def softplus(i, u):
                    rows, width = spec(u)
                    n = i * UNITS + u
                    hold(dve, passed, (s["soft_ready"], n + 1), *[(s["probs_ready"], n - 1)] * (u >= 2))
                    nc.vector.scalar_tensor_tensor(score[0:rows, u % 2, 0:width], slot(u)[0:rows, 0:width], 0.0,
                                                   rest[0:rows, u % 2, 0:width], ALU.max, ALU.add).then_inc(s["rest_done"], 1)

                def stick(i, u):
                    rows, width = spec(u)
                    n = i * UNITS + u
                    hold(dve, passed, (s["masked"], n + 1))
                    steps = Steps(dve, s["dve_step"], base=n, passed=passed)
                    steps.then(nc.vector.tensor_tensor_scan(rest[0:rows, u % 2, 0:width][:, ::-1], ones[0:rows, 0:width],
                                                            score[0:rows, u % 2, 0:width][:, ::-1], 0.0, ALU.mult, ALU.add))
                    nc.vector.tensor_tensor(score[0:rows, u % 2, 0:width], slot(u)[0:rows, 0:width], rest[0:rows, u % 2, 0:width],
                                            ALU.subtract).then_inc(s["scored"], 1)

                def finish(i, u):
                    h, t = unit_of(u)
                    rows, _ = spec(u)
                    n = i * UNITS + u
                    dst = k.mix[0:rows, t, bass.ds((i + (0 if mla else first)) * P + h * HD, HD)]
                    if sbk:
                        hold(dve, passed, (s["o_ready"], n + 1))
                        nc.vector.tensor_copy(dst, bank_o[0:rows, 0:HD]).then_inc(s["o_done"], 1)
                        return
                    steps = Steps(dve, s["dve_step"], base=n, passed=passed)
                    hold(dve, passed, (s["probs_ready"], n + 1))
                    steps.then(nc.vector.reciprocal(small[0:rows, u % 2, 2:3], small[0:rows, u % 2, 1:2]))
                    hold(dve, passed, (s["o_ready"], n + 1))
                    nc.vector.tensor_scalar(dst, bank_o[0:rows, 0:HD], small[0:rows, u % 2, 2:3], None, ALU.mult).then_inc(s["o_done"], 1)

                def body(i):
                    copy_out(i)
                    if sbk:
                        softplus(i, 0)
                        softplus(i, 1)
                        stick(i, 0)
                        for u in range(UNITS):
                            if u + 1 < UNITS:
                                stick(i, u + 1)
                            if u + 2 < UNITS:
                                softplus(i, u + 2)
                            finish(i, u)
                    else:
                        logits(i, 0)
                        for u in range(UNITS):
                            if u + 1 < UNITS:
                                logits(i, u + 1)
                            finish(i, u)
                loop(dve, body)

            @block.gpsimd
            def _(pool):
                if mla:
                    return
                pool.wait_ge(s["zeroed"], m["zeroed"])
                fills = {v: pool.to_reg(v) for v in (NEG, 0.0)}

                def decay(i, u):
                    h, t = unit_of(u)
                    lo, hi = KEY_RANGE[t]
                    rows, width = ROWS[t], hi - lo
                    n = i * UNITS + u
                    steps = Steps(pool, s["bias_step"], base=n, passed=passed)
                    hold(pool, passed, *[(s["cumk_in"], 32 * (i + 1)), (s["cumq_ready"], i + 1), (s["scored"], n)] * (u == 0),
                         *[(s["scored"], n - 1)] * (u >= 2))
                    steps.then(pool.tensor_scalar(bias[0:rows, u % 2, 0:width], cumk[0:rows, h, lo:hi], -1.0, cumq[0:rows, h, t:t + 1],
                                                  ALU.mult, ALU.add))
                    d = bias[0:rows, u % 2, width - rows:width]
                    pool.affine_select(out=d, in_=d, compare_op=ALU.is_ge, fill=fills[NEG], base=0, pattern=[[-1, rows]],
                                       channel_multiplier=1).then_inc(s["bias_ready"], 1)

                def cut(i, u, src, fill, done):
                    _, t = unit_of(u)
                    rows, width = ROWS[t], KEY_RANGE[t][1] - KEY_RANGE[t][0]
                    hold(pool, passed, (s[src], i * UNITS + u + 1))
                    d = score[0:rows, u % 2, width - rows:width]
                    pool.affine_select(out=d, in_=d, compare_op=ALU.is_gt, fill=fills[fill], base=0, pattern=[[-1, rows]],
                                       channel_multiplier=1).then_inc(s[done], 1)

                def body(i):
                    if fox:
                        for u in range(UNITS):
                            decay(i, u)
                        return
                    cut(i, 0, "rest_done", 0.0, "masked")
                    cut(i, 1, "rest_done", 0.0, "masked")
                    cut(i, 0, "scored", NEG, "logit_ready")
                    for u in range(UNITS):
                        if u + 1 < UNITS:
                            cut(i, u + 1, "scored", NEG, "logit_ready")
                        if u + 2 < UNITS:
                            cut(i, u + 2, "rest_done", 0.0, "masked")
                loop(pool, body)


def mla_latents(k, m):
    nc = k.nc
    half = ROPE // 2
    with ExitStack() as c:
        sb = lambda n, s, d=F32: c.enter_context(nc.sbuf_tensor(f"lat_{n}", s, d))
        sem = lambda n: new_signal(k, f"lat_{n}")
        w = sb("w", [P, J, DOWN])
        gains = sb("gains", [P, Q_LORA + KV_LORA])
        junk = sb("junk", [P, 2, Q_LORA + KV_LORA])
        cq = sb("cq", [P, 2, Q_LORA])
        ckv = sb("ckv", [P, NT, KV_LORA])
        kr = sb("kr", [P, NT, ROPE])
        rot = sb("rot", [P, 4, half])
        ms = sb("ms", [P, NT, 4])
        w_in, g_in, past_in, z_ready, squared, mean_done, inv_done, normed, turned, turned_q, turned_k, rot_step, out_sem, filled = (
            sem(n) for n in ("w_in g_in past_in z_ready squared mean_done inv_done normed turned turned_q turned_k "
                             "rot_step out filled").split())
        z = lambda t: banks(k, 2 * (t % 2), 2)
        tr = lambda t: banks(k, 4 + 2 * (t % 2), 2)

        with nc.Block() as block:

            @block.sync
            def _(sp):
                sp.dma_start(w[:], k.w_mla_down.rearrange("(j p) n -> p j n", p=P)).then_inc(w_in, 16)
                sp.dma_start(gains[:, 0:Q_LORA], k.g_q.to_broadcast([P, Q_LORA])).then_inc(g_in, 16)
                sp.dma_start(gains[:, Q_LORA:], k.g_kv.to_broadcast([P, KV_LORA])).then_inc(g_in, 16)
                sp.dma_start(m["cos"][:], k.cos).then_inc(g_in, 16)
                sp.dma_start(m["sin"][:], k.sin).then_inc(g_in, 16)
                sp.dma_start(m["ckvT"][:, :, SEQ:NEW_AT], k.ckv_past).then_inc(past_in, 16)
                for h in range(2):
                    sp.dma_start(m["kh"][h][HD:QW, SEQ:NEW_AT], k.kr_past).then_inc(past_in, 16)
                sp.wait_ge(normed, NT)
                sp.dma_start(k.o_ckv_p.rearrange("a b (t p) c -> p (a b t) c", p=P), ckv[:, 0:4, :]).then_inc(out_sem, 16)
                sp.dma_start(k.o_ckv_s.rearrange("a b t c -> (a b t) c"), ckv[0:NEW, 4, :]).then_inc(out_sem, 16)
                sp.dma_start(k.o_kr_p.rearrange("a b (t p) c -> p (a b t) c", p=P), kr[:, 0:4, :]).then_inc(out_sem, 16)
                sp.dma_start(k.o_kr_s.rearrange("a b t c -> (a b t) c"), kr[0:NEW, 4, :]).then_inc(out_sem, 16)
                sp.wait_ge(out_sem, 64)
                sp.wait_ge(past_in, 48)

            @block.tensor
            def _(pe):
                pe.wait_ge(w_in, 16)

                def down(t):
                    if t >= 2:
                        pe.wait_ge(normed, t - 1)
                        pe.wait_ge(squared, t - 1)
                    for lo, hi in ((0, BANK), (BANK, DOWN)):
                        for j in range(J):
                            last = nc.tensor.matmul(z(t)[0:ROWS[t], lo:hi], k.xT[:, j, t * P:t * P + ROWS[t]], w[:, j, lo:hi],
                                                    start=(j == 0), stop=(j == J - 1))
                    last.then_inc(z_ready, 1)

                def turn(t):
                    r = ROWS[t]
                    pe.wait_ge(normed, t + 1)
                    if t >= 2:
                        pe.wait_ge(turned_q, t - 1)
                        pe.wait_ge(turned_k, t - 1)
                    for j in range(JQ):
                        nc.tensor.transpose(tr(t)[:, j * P:j * P + r], cq[0:r, t % 2, j * P:(j + 1) * P], k.ident[0:r, 0:r])
                    for j in range(JC):
                        nc.tensor.transpose(tr(t)[:, BANK + j * P:BANK + j * P + r], ckv[0:r, t, j * P:(j + 1) * P], k.ident[0:r, 0:r])
                    nc.tensor.transpose(tr(t)[0:ROPE, BANK + 2 * P:BANK + 2 * P + r], kr[0:r, t, :], k.ident[0:r, 0:r]).then_inc(turned, 1)

                for t in range(NT):
                    down(t)
                    if t:
                        turn(t - 1)
                turn(NT - 1)

            def copy_q(act, t):
                r = ROWS[t]
                act.wait_ge(turned, t + 1)
                nc.scalar.activation(m["cqT"][:, :, t * P:t * P + r], tr(t)[:, 0:JQ * P].rearrange("p (j q) -> p j q", q=P)[:, :, 0:r],
                                     ACT.Copy).then_inc(turned_q, 1)

            @block.scalar
            def _(act):
                for t in range(NT):
                    r = ROWS[t]
                    act.wait_ge(z_ready, t + 1)
                    if t >= 2:
                        act.wait_ge(squared, t - 1)
                    nc.scalar.activation(junk[0:r, t % 2, 0:Q_LORA], z(t)[0:r, 0:Q_LORA], ACT.Square, accum_out=ms[0:r, t, 0:1])
                    nc.scalar.activation(junk[0:r, t % 2, Q_LORA:], z(t)[0:r, Q_LORA:Q_LORA + KV_LORA], ACT.Square,
                                         accum_out=ms[0:r, t, 1:2]).then_inc(squared, 1)
                    if t:
                        copy_q(act, t - 1)
                copy_q(act, NT - 1)

            @block.gpsimd
            def _(pool):
                pool.memset(m["mask"][:], 0.0).then_inc(filled, 1)
                pool.wait_ge(filled, 1)
                pool.memset(m["mask"][0:HD, m["mask_width"][0] - HD:m["mask_width"][0]], NEG).then_inc(filled, 1)
                for t in range(NT):
                    r = ROWS[t]
                    pool.wait_ge(mean_done, 2 * (t + 1))
                    pool.tensor_tensor(ms[0:r, t, 2:4], ms[0:r, t, 0:2], k.half[0:r, 0:1].to_broadcast([r, 2]), ALU.pow).then_inc(inv_done, 1)

            @block.vector
            def _(dve):
                steps = Steps(dve, rot_step)
                dve.wait_ge(g_in, 64)

                def norm(t):
                    r = ROWS[t]
                    dve.wait_ge(squared, t + 1)
                    dve.wait_ge(z_ready, t + 1)
                    nc.vector.tensor_scalar(ms[0:r, t, 0:1], ms[0:r, t, 0:1], 1.0 / Q_LORA, RMS_EPS, ALU.mult, ALU.add).then_inc(mean_done, 1)
                    nc.vector.tensor_scalar(ms[0:r, t, 1:2], ms[0:r, t, 1:2], 1.0 / KV_LORA, RMS_EPS, ALU.mult, ALU.add).then_inc(mean_done, 1)
                    x1 = z(t)[0:r, DOWN - ROPE:DOWN - half]
                    x2 = z(t)[0:r, DOWN - half:DOWN]
                    cos, sin = m["cos"][0:r, t, :], m["sin"][0:r, t, :]
                    nc.vector.tensor_tensor(rot[0:r, 0], x1, cos, ALU.mult)
                    nc.vector.tensor_tensor(rot[0:r, 1], x2, sin, ALU.mult)
                    nc.vector.tensor_tensor(rot[0:r, 2], x1, sin, ALU.mult)
                    steps.then(nc.vector.tensor_tensor(rot[0:r, 3], x2, cos, ALU.mult))
                    nc.vector.tensor_tensor(kr[0:r, t, 0:half], rot[0:r, 0], rot[0:r, 1], ALU.subtract)
                    steps.then(nc.vector.tensor_tensor(kr[0:r, t, half:ROPE], rot[0:r, 2], rot[0:r, 3], ALU.add))
                    dve.wait_ge(inv_done, t + 1)
                    if t >= 2:
                        dve.wait_ge(turned, t - 1)
                    nc.vector.scalar_tensor_tensor(cq[0:r, t % 2, :], z(t)[0:r, 0:Q_LORA], ms[0:r, t, 2:3], gains[0:r, 0:Q_LORA], ALU.mult, ALU.mult)
                    nc.vector.scalar_tensor_tensor(ckv[0:r, t, :], z(t)[0:r, Q_LORA:Q_LORA + KV_LORA], ms[0:r, t, 3:4],
                                                   gains[0:r, Q_LORA:], ALU.mult, ALU.mult).then_inc(normed, 1)

                def copy_k(t):
                    r = ROWS[t]
                    at = NEW_AT if t == 4 else t * P
                    dve.wait_ge(turned, t + 1)
                    nc.vector.tensor_copy(m["ckvT"][:, :, at:at + r], tr(t)[:, BANK:BANK + JC * P].rearrange("p (j q) -> p j q", q=P)[:, :, 0:r])
                    for h in range(2):
                        last = nc.vector.tensor_copy(m["kh"][h][HD:QW, at:at + r], tr(t)[0:ROPE, BANK + 2 * P:BANK + 2 * P + r])
                    last.then_inc(turned_k, 1)

                for t in range(NT):
                    norm(t)
                    if t:
                        copy_k(t - 1)
                copy_k(NT - 1)


def expert_loads(k, sp, layer, slot, expert, gu_in, dn_in, gu, dn):
    at = bass.ds(expert, 1)
    sp.dma_start(gu[:, :, 0:EH], k.w_gate[layer, at].rearrange("a (j p) f -> p (a j) f", p=P)).then_inc(gu_in, 16)
    sp.dma_start(gu[:, :, EH:2 * EH], k.w_up[layer, at].rearrange("a (j p) f -> p (a j) f", p=P)).then_inc(gu_in, 16)
    sp.dma_start(dn[:], k.w_down[layer, at].rearrange("a (j p) d -> p (a j) d", p=P)).then_inc(dn_in, 16)


def mix_out(k, tag, layer, w_out):
    nc = k.nc
    with ExitStack() as c:
        sb = lambda n, s, d=F32: c.enter_context(nc.sbuf_tensor(f"{tag}_{n}", s, d))
        sem = lambda n: new_signal(k, f"{tag}_{n}")
        w = sb("w", [P, J, D])
        g = sb("g", [P, D])
        b = sb("b", [P, D])
        wr = sb("wr", [P, J, GROUPS + NE])
        br = sb("br", [P, GROUPS + NE])
        stats = sb("stats", [P, 2, 2, 6])
        mv = sb("mv", [P, 2, 4])
        w_in, p_in, turned, mixT_act, mixT_dve, y_ready, y_read, steps_s, var_done, inv_done, centred, scaled, x_ready = (
            sem(n) for n in ("w_in p_in turned mixT_act mixT_dve y_ready y_read step var_done inv_done centred "
                             "scaled x_ready").split())
        xt_ready, xt_act, xt_dve, logit_mm, logit_done, out_sem = (sem(n) for n in "xt_ready xt_act xt_dve logit_mm logit_done out".split())
        tr = banks(k, 0, 2)
        y = lambda t: banks(k, 2 + 2 * (t % 2), 2)
        xtr = banks(k, 6, 1)
        lg = banks(k, 7, 1)

        with nc.Block() as block:

            @block.sync
            def _(sp):
                sp.dma_start(w[:], w_out.rearrange("(j p) n -> p j n", p=P)).then_inc(w_in, 16)
                sp.dma_start(g[:], k.ln_g[layer, 0:1, :].to_broadcast([P, D])).then_inc(p_in, 16)
                sp.dma_start(b[:], k.ln_b[layer, 0:1, :].to_broadcast([P, D])).then_inc(p_in, 16)
                sp.dma_start(wr[:], k.w_r[layer]).then_inc(p_in, 16)
                sp.dma_start(br[:], k.b_r[layer:layer + 1, :].to_broadcast([P, GROUPS + NE])).then_inc(p_in, 16)
                for t in range(NT):
                    sp.wait_ge(x_ready, t + 1)
                    sp.dma_start(k.x_d[t * P:t * P + ROWS[t], :], k.x[0:ROWS[t], t, :]).then_inc(out_sem, 16)
                sp.wait_ge(out_sem, 16 * NT)

            @block.tensor
            def _(pe):
                for t in range(NT):
                    if t:
                        pe.wait_ge(mixT_act, t)
                        pe.wait_ge(mixT_dve, t)
                    for j in range(J):
                        last = nc.tensor.transpose(tr[:, j * P:j * P + ROWS[t]], k.mix[0:ROWS[t], t, j * P:(j + 1) * P],
                                                   k.ident[0:ROWS[t], 0:ROWS[t]])
                    last.then_inc(turned, 1)
                pe.wait_ge(w_in, 16)
                pe.wait_ge(mixT_act, NT)
                pe.wait_ge(mixT_dve, NT)

                def out_proj(t):
                    if t >= 2:
                        pe.wait_ge(y_read, t - 1)
                    for h in range(2):
                        for j in range(J):
                            last = nc.tensor.matmul(y(t)[0:ROWS[t], h * BANK:(h + 1) * BANK], k.xT[:, j, t * P:t * P + ROWS[t]],
                                                    w[:, j, h * BANK:(h + 1) * BANK], start=(j == 0), stop=(j == J - 1))
                    last.then_inc(y_ready, 1)

                def turn_x(t):
                    pe.wait_ge(x_ready, t + 1)
                    for h in range(2):
                        if t or h:
                            pe.wait_ge(xt_act if h else xt_dve, t + h)
                        for j in range(4):
                            f = (4 * h + j) * P
                            last = nc.tensor.transpose(xtr[:, j * P:j * P + ROWS[t]], k.x[0:ROWS[t], t, f:f + P], k.ident[0:ROWS[t], 0:ROWS[t]])
                        last.then_inc(xt_ready, 1)
                    pe.wait_ge(xt_act, t + 1)
                    pe.wait_ge(xt_dve, t + 1)
                    pe.wait_ge(p_in, 64)
                    if t:
                        pe.wait_ge(logit_done, t)
                    for j in range(J):
                        last = nc.tensor.matmul(lg[:, t * 64:t * 64 + GROUPS + NE], k.xT[:, j, t * P:(t + 1) * P], wr[:, j, :],
                                                start=(j == 0), stop=(j == J - 1))
                    last.then_inc(logit_mm, 1)

                for t in range(NT):
                    out_proj(t)
                    if t:
                        turn_x(t - 1)
                turn_x(NT - 1)

            @block.scalar
            def _(act):
                for t in range(NT):
                    r = ROWS[t]
                    act.wait_ge(turned, t + 1)
                    nc.scalar.activation(k.xT[:, 0:4, t * P:t * P + r], tr[:, 0:BANK].rearrange("p (j q) -> p j q", q=P)[:, :, 0:r],
                                         ACT.Copy).then_inc(mixT_act, 1)
                for t in range(NT):
                    r = ROWS[t]
                    act.wait_ge(xt_ready, 2 * t + 1)
                    act.wait_ge(y_ready, t + 1)
                    nc.scalar.activation(k.xT[:, 0:4, t * P:t * P + r], xtr.rearrange("p (j q) -> p j q", q=P)[:, :, 0:r],
                                         ACT.Copy).then_inc(xt_act, 1)

            @block.vector
            def _(dve):
                for t in range(NT):
                    r = ROWS[t]
                    dve.wait_ge(turned, t + 1)
                    nc.vector.tensor_copy(k.xT[:, 4:8, t * P:t * P + r], tr[:, BANK:2 * BANK].rearrange("p (j q) -> p j q", q=P)[:, :, 0:r]).then_inc(mixT_dve, 1)
                dve.wait_ge(p_in, 64)
                steps = Steps(dve, steps_s)

                def rest(t):
                    r = ROWS[t]
                    dve.wait_ge(xt_ready, 2 * t + 2)
                    nc.vector.tensor_copy(k.xT[:, 4:8, t * P:t * P + r], xtr.rearrange("p (j q) -> p j q", q=P)[:, :, 0:r]).then_inc(xt_dve, 1)
                    dve.wait_ge(logit_mm, t + 1)
                    nc.vector.tensor_tensor(k.logits[:, t, :], lg[:, t * 64:t * 64 + GROUPS + NE], br[:], ALU.add).then_inc(logit_done, 1)

                for t in range(NT):
                    norm_tile(k, dve, steps, t, lambda t: y(t)[0:ROWS[t], :], y_ready, t + 1, y_read, stats, mv, var_done, inv_done, centred)
                    if t:
                        rest(t - 1)
                rest(NT - 1)

            @block.gpsimd
            def _(pool):
                pool.wait_ge(p_in, 64)
                for t in range(NT):
                    norm_tail(k, pool, t, g, b, mv, var_done, inv_done, centred, scaled, x_ready)


def norm_tile(k, dve, steps, t, y, y_sem, y_count, y_read, stats, mv, var_done, inv_done, centred):
    nc = k.nc
    r = ROWS[t]
    x = k.x[0:r, t, :]
    dve.wait_ge(y_sem, y_count)
    steps.then(nc.vector.scalar_tensor_tensor(x, x, ALPHA, y(t), ALU.mult, ALU.add))
    for h in range(2):
        last = nc.vector.bn_stats(stats[0:r, t % 2, h, :], x[:, h * BANK:(h + 1) * BANK])
        if y_read is not None and h == 0:
            last.then_inc(y_read, 1)
    steps.then(last)
    steps.then(nc.vector.bn_aggr(mv[0:r, t % 2, 0:2], stats[0:r, t % 2, :, :].rearrange("p a b -> p (a b)")))
    nc.vector.tensor_scalar(mv[0:r, t % 2, 2:3], mv[0:r, t % 2, 1:2], LN_EPS, None, ALU.add).then_inc(var_done, 1)
    dve.wait_ge(inv_done, t + 1)
    nc.vector.tensor_scalar(x, x, mv[0:r, t % 2, 0:1], mv[0:r, t % 2, 3:4], ALU.subtract, ALU.mult).then_inc(centred, 1)


def norm_tail(k, pool, t, g, b, mv, var_done, inv_done, centred, scaled, x_ready):
    r = ROWS[t]
    pool.wait_ge(var_done, t + 1)
    pool.tensor_tensor(mv[0:r, t % 2, 3:4], mv[0:r, t % 2, 2:3], k.half[0:r, :], ALU.pow).then_inc(inv_done, 1)
    pool.wait_ge(centred, t + 1)
    pool.tensor_tensor(k.x[0:r, t, :], k.x[0:r, t, :], g[0:r, :], ALU.mult).then_inc(scaled, 1)
    pool.wait_ge(scaled, t + 1)
    pool.tensor_tensor(k.x[0:r, t, :], k.x[0:r, t, :], b[0:r, :], ALU.add).then_inc(x_ready, 1)


def route(k, tag, layer, r):
    nc = k.nc
    NX = NB_TAB - NE
    with ExitStack() as c:
        sb = lambda n, s, d=F32: c.enter_context(nc.sbuf_tensor(f"{tag}_{n}", s, d))
        sem = lambda n: new_signal(k, f"{tag}_{n}")
        glog = sb("glog", [P, NT, 8])
        top_g = sb("top_g", [P, NT, 8])
        idx_g = sb("idx_g", [P, NT, 8], U32)
        neg_g = sb("neg_g", [P, NT])
        exp_g = sb("exp_g", [P, NT, GROUPS])
        gate = sb("gate", [P, NT])
        g_of = sb("g_of", [P, NT])
        pen = sb("pen", [P, NT, GROUPS])
        elog = sb("elog", [P, NT, NE])
        top_e = sb("top_e", [P, NT, 8])
        idx_e = sb("idx_e", [P, NT, 8], U32)
        gap = sb("gap", [P, NT])
        e_gap = sb("e_gap", [P, NT])
        den = sb("den", [P, NT])
        e_of = sb("e_of", [P, 2, NT])
        hot = sb("hot", [P, 2, NT, NE])
        both = sb("both", [P, NT, NE])
        work = sb("work", [P, 2, NT, NE])
        rank = sb("rank", [P, 2, NT])
        over = sb("over", [P, 2, NT])
        base = sb("base", [P, 2, NT])
        flag = sb("flag", [P, 2, NT])
        block_of = sb("block_of", [P, 2, NT])
        place = sb("place", [P, 2, NT])
        count = sb("count", [P, NE])
        extra = sb("extra", [P, NE])
        xend = sb("xend", [P, NE])
        xbase = sb("xbase", [P, NE])
        tri = sb("tri", [P, P])
        ones = sb("ones", [P, P])
        valid = sb("valid", [P, NT])
        slot_id = sb("slot_id", [P, 2, NT])
        iota_i = sb("iota_i", [P, P], I32)
        iota = sb("iota", [P, P])
        id_i = sb("id_i", [P, 2, NT], I32)
        hot_p = sb("hot_p", [P, 2, NT, CB])
        hot_b = sb("hot_b", [P, 2, NT, NB_TAB])
        lst = sb("lst", [CB, NB_TAB])
        far = sb("far", [CB, NB_TAB])
        tok = sb("tok", [CB, NB_TAB])
        tab_a = sb("tab_a", [1, NX, NE])
        tab_b = sb("tab_b", [1, NX, NE])
        tab_f = sb("tab_f", [1, NB_TAB])
        trip = sb("trip", [1, 4])
        steps_s, filled, consts, gmax_done, gexp_done, gap_done, egap_done, hot_done, ranked, listed, lists_ready = (
            sem(n) for n in "step filled consts gmax_done gexp_done gap_done egap_done hot_done ranked listed lists".split())
        cum = banks(k, 0, 1)
        tot = banks(k, 1, 1)
        lps = banks(k, 2, 1)

        with nc.Block() as block:

            @block.gpsimd
            def _(pool):
                n = 0

                def step(ins):
                    nonlocal n
                    n += 1
                    ins.then_inc(filled, 1)
                    pool.wait_ge(filled, n)
                step(pool.memset(tri[:], 1.0))
                step(pool.affine_select(out=tri[:], in_=tri[:], compare_op=ALU.is_gt, fill=0.0, base=0, pattern=[[1, P]], channel_multiplier=-1))
                step(pool.memset(ones[:], 1.0))
                step(pool.memset(valid[:], 1.0))
                step(pool.memset(valid[NEW:P, 4:5], 0.0))
                step(pool.iota(iota_i[:], [[1, P]], base=0, channel_multiplier=0))
                step(pool.tensor_copy(iota[:], iota_i[:]))
                step(pool.iota(id_i[:], [[T, 2], [P, NT]], base=1, channel_multiplier=1))
                step(pool.tensor_copy(slot_id[:], id_i[:]))
                step(pool.memset(slot_id[NEW:P, :, 4], 0.0))
                step(pool.memset(glog[:], -3e38))
                pool.sem_inc(consts, 1)

            @block.scalar
            def _(act):
                act.wait_ge(gmax_done, 1)
                for t in range(NT):
                    last = nc.scalar.activation(exp_g[:, t, :], glog[:, t, 0:GROUPS], ACT.Exp, bias=neg_g[:, t:t + 1], accum_out=gate[:, t:t + 1])
                last.then_inc(gexp_done, 1)
                act.wait_ge(gap_done, 1)
                nc.scalar.activation(e_gap[:], gap[:], ACT.Exp).then_inc(egap_done, 1)

            @block.tensor
            def _(pe):
                pe.wait_ge(hot_done, 1)
                for t in range(NT):
                    for a in range(t):
                        nc.tensor.matmul(cum[:, t * NE:(t + 1) * NE], ones[:], both[:, a, :], start=(a == 0), stop=False)
                    nc.tensor.matmul(cum[:, t * NE:(t + 1) * NE], tri[:], both[:, t, :], start=(t == 0), stop=True)
                for t in range(NT):
                    last = nc.tensor.matmul(tot[:, 0:NE], ones[:], both[:, t, :], start=(t == 0), stop=(t == NT - 1))
                last.then_inc(ranked, 1)
                pe.wait_ge(listed, 1)
                for n in range(2 * NT):
                    c_, t = n // NT, n % NT
                    last = nc.tensor.matmul(lps[0:CB, 0:NB_TAB], hot_p[:, c_, t, :], hot_b[:, c_, t, :], start=(n == 0), stop=(n == 2 * NT - 1))
                last.then_inc(lists_ready, 1)

            @block.vector
            def _(dve):
                v = nc.vector
                steps = Steps(dve, steps_s)
                dve.wait_ge(consts, 1)
                steps.then(v.tensor_copy(glog[:, :, 0:GROUPS], k.logits[:, :, 0:GROUPS]))
                for t in range(NT):
                    last = v.max(top_g[:, t, :], glog[:, t, :])
                steps.then(last)
                v.tensor_scalar(neg_g[:], top_g[:, :, 0], -1.0, None, ALU.mult).then_inc(gmax_done, 1)
                for t in range(NT):
                    last = v.max_index(idx_g[:, t, :], top_g[:, t, :], glog[:, t, :])
                steps.then(last)
                steps.then(v.tensor_copy(g_of[:], idx_g[:, :, 0]))
                steps.then(v.tensor_tensor(pen[:], iota[:, 0:GROUPS].unsqueeze(1).to_broadcast([P, NT, GROUPS]),
                                           g_of[:].unsqueeze(2).to_broadcast([P, NT, GROUPS]), ALU.is_equal))
                steps.then(v.tensor_scalar(pen[:], pen[:], 1e30, -1e30, ALU.mult, ALU.add))
                for t in range(NT):
                    last = v.tensor_tensor(elog[:, t, :].rearrange("p (g e) -> p g e", e=PER_GROUP),
                                           k.logits[:, t, GROUPS:].rearrange("p (g e) -> p g e", e=PER_GROUP),
                                           pen[:, t, :].unsqueeze(2).to_broadcast([P, GROUPS, PER_GROUP]), ALU.add)
                steps.then(last)
                for t in range(NT):
                    last = v.max(top_e[:, t, :], elog[:, t, :])
                steps.then(last)
                v.tensor_tensor(gap[:], top_e[:, :, 1], top_e[:, :, 0], ALU.subtract).then_inc(gap_done, 1)
                for t in range(NT):
                    last = v.max_index(idx_e[:, t, :], top_e[:, t, :], elog[:, t, :])
                steps.then(last)
                for c_ in range(2):
                    last = v.tensor_copy(e_of[:, c_, :], idx_e[:, :, c_])
                steps.then(last)
                for c_ in range(2):
                    last = v.tensor_tensor(hot[:, c_], iota[:, 0:NE].unsqueeze(1).to_broadcast([P, NT, NE]),
                                           e_of[:, c_, :].unsqueeze(2).to_broadcast([P, NT, NE]), ALU.is_equal)
                steps.then(last)
                for c_ in range(2):
                    last = v.tensor_tensor(hot[:, c_], hot[:, c_], valid[:].unsqueeze(2).to_broadcast([P, NT, NE]), ALU.mult)
                steps.then(last)
                v.tensor_tensor(both[:], hot[:, 0], hot[:, 1], ALU.add).then_inc(hot_done, 1)
                dve.wait_ge(gexp_done, 1)
                dve.wait_ge(egap_done, 1)
                v.tensor_scalar(den[:], e_gap[:], 1.0, None, ALU.add)
                steps.then(v.reciprocal(gate[:], gate[:]))
                steps.then(v.reciprocal(den[:], den[:]))
                steps.then(v.tensor_tensor(r["weight"][:, 0, :], gate[:], den[:], ALU.mult))
                v.tensor_tensor(r["weight"][:, 1, :], r["weight"][:, 0, :], e_gap[:], ALU.mult)
                dve.wait_ge(ranked, 1)
                steps.then(v.tensor_copy(count[:], tot[:, 0:NE]))
                steps.then(v.tensor_scalar(extra[:], count[:], float(CB), None, ALU.is_gt))
                for n in range(2, -(-T // CB)):
                    steps.then(v.tensor_scalar(xbase[:], count[:], float(n * CB), None, ALU.is_gt))
                    steps.then(v.tensor_tensor(extra[:], extra[:], xbase[:], ALU.add))
                steps.then(v.tensor_tensor_scan(xend[:], ones[:, 0:NE], extra[:], float(NE), ALU.mult, ALU.add))
                steps.then(v.tensor_tensor(xbase[:], xend[:], extra[:], ALU.subtract))
                for src, dst in ((cum[:, 0:NT * NE].rearrange("p (t e) -> p t e", e=NE), rank),
                                 (xbase[:].unsqueeze(1).to_broadcast([P, NT, NE]), base)):
                    for c_ in range(2):
                        last = v.tensor_tensor(work[:, c_], hot[:, c_], src, ALU.mult)
                    steps.then(last)
                    steps.then(v.tensor_reduce(dst[:], work[:], AX_X, ALU.add))
                steps.then(v.tensor_scalar(over[:], rank[:], float(CB), None, ALU.is_ge))
                for n in range(2, -(-T // CB)):
                    steps.then(v.tensor_scalar(flag[:], rank[:], float(n * CB), None, ALU.is_ge))
                    steps.then(v.tensor_tensor(over[:], over[:], flag[:], ALU.add))
                steps.then(v.tensor_tensor(block_of[:], base[:], over[:], ALU.add))
                steps.then(v.tensor_tensor(block_of[:], block_of[:], e_of[:], ALU.subtract))
                steps.then(v.tensor_scalar(flag[:], over[:], 1.0, None, ALU.is_ge))
                steps.then(v.scalar_tensor_tensor(block_of[:], block_of[:], -1.0, flag[:], ALU.add, ALU.mult))
                steps.then(v.tensor_tensor(block_of[:], block_of[:], e_of[:], ALU.add))
                steps.then(v.scalar_tensor_tensor(place[:], over[:], -float(CB), rank[:], ALU.mult, ALU.add))
                for c_ in range(2):
                    v.tensor_tensor(hot_p[:, c_], iota[:, 0:CB].unsqueeze(1).to_broadcast([P, NT, CB]),
                                    place[:, c_, :].unsqueeze(2).to_broadcast([P, NT, CB]), ALU.is_equal)
                    last = v.tensor_tensor(hot_b[:, c_], iota[:, 0:NB_TAB].unsqueeze(1).to_broadcast([P, NT, NB_TAB]),
                                           block_of[:, c_, :].unsqueeze(2).to_broadcast([P, NT, NB_TAB]), ALU.is_equal)
                steps.then(last)
                for c_ in range(2):
                    last = v.tensor_tensor(hot_b[:, c_], hot_b[:, c_], slot_id[:, c_, :].unsqueeze(2).to_broadcast([P, NT, NB_TAB]), ALU.mult)
                last.then_inc(listed, 1)
                nx = iota[0:1, NE:NE + NX].unsqueeze(2).to_broadcast([1, NX, NE])
                v.tensor_tensor(tab_a[:], nx, xbase[0:1, :].unsqueeze(1).to_broadcast([1, NX, NE]), ALU.is_ge)
                steps.then(v.tensor_tensor(tab_b[:], nx, xend[0:1, :].unsqueeze(1).to_broadcast([1, NX, NE]), ALU.is_lt))
                steps.then(v.tensor_tensor(tab_a[:], tab_a[:], tab_b[:], ALU.mult))
                steps.then(v.tensor_tensor(tab_a[:], tab_a[:], iota[0:1, 0:NE].unsqueeze(1).to_broadcast([1, NX, NE]), ALU.mult))
                v.tensor_copy(tab_f[:, 0:NE], iota[0:1, 0:NE])
                steps.then(v.tensor_reduce(tab_f[:, NE:NB_TAB], tab_a[:], AX_X, ALU.add))
                steps.then(v.tensor_copy(r["expert"][:], tab_f[:]))
                steps.then(v.tensor_scalar(trip[:, 0:1], xend[0:1, NE - 1:NE], float(NE), None, ALU.is_gt))
                for n in range(1, (NB_TAB - NE) // RING):
                    steps.then(v.tensor_scalar(trip[:, 1:2], xend[0:1, NE - 1:NE], float(NE + n * RING), None, ALU.is_gt))
                    steps.then(v.tensor_tensor(trip[:, 0:1], trip[:, 0:1], trip[:, 1:2], ALU.add))
                steps.then(v.tensor_scalar(trip[:, 2:3], trip[:, 0:1], float(NE // RING), None, ALU.add))
                steps.then(v.tensor_copy(r["trips"][:], trip[:, 2:3]))
                dve.wait_ge(lists_ready, 1)
                steps.then(v.tensor_scalar(lst[:], lps[0:CB, 0:NB_TAB], -1.0, None, ALU.add))
                v.tensor_scalar(far[:], lst[:], 0.0, FAR, ALU.is_lt, ALU.mult)
                steps.then(v.tensor_scalar(tok[:], lst[:], float(T), -float(T), ALU.is_ge, ALU.mult))
                steps.then(v.tensor_tensor(lst[:], lst[:], far[:], ALU.add))
                v.tensor_copy(r["slots"][:], lst[:])
                steps.then(v.tensor_tensor(tok[:], tok[:], lst[:], ALU.add))
                steps.then(v.tensor_copy(r["tokens"][:], tok[:]))


def experts(k, tag, layer, r):
    nc, passed = k.nc, k.passed
    first_trips = NE // RING
    with ExitStack() as c:
        sb = lambda n, s, d=F32: c.enter_context(nc.sbuf_tensor(f"{tag}_{n}", s, d))
        sem = lambda n: new_signal(k, f"{tag}_{n}")
        w_gu = [*k.w_gu, sb("w_gu3", [P, J, 2 * EH])]
        w_dn = [*k.w_dn, sb("w_dn3", [P, JE, D])]
        x_idx = [sb(f"x_idx{n}", [CB, 1], I32) for n in range(RING)]
        y_idx = [sb(f"y_idx{n}", [CB, 1], I32) for n in range(RING)]
        xg = [sb(f"xg{n}", [CB, D]) for n in range(RING)]
        xgT = sb("xgT", [P, 2, J, CB])
        silu = sb("silu", [CB, 2, EH])
        hid = sb("hid", [CB, 2, EH])
        hidT = sb("hidT", [P, 2, JE, CB])
        yo = [sb(f"yo{n}", [CB, D]) for n in range(RING)]
        gu_in = [sem(f"gu_in{n}") for n in range(RING)]
        dn_in = [sem(f"dn_in{n}") for n in range(RING)]
        x_in = [sem(f"x_in{n}") for n in range(RING)]
        y_out = [sem(f"y_out{n}") for n in range(RING)]
        zeroed, x_turned, xgT_ready, gu_ready, silu_ready, hid_ready, hid_turned, hidT_ready, y_ready, y_act, y_dve, idx_done = (
            sem(n) for n in ("zeroed x_turned xgT_ready gu_ready silu_ready hid_ready hid_turned hidT_ready y_ready "
                             "y_act y_dve idx_done").split())
        gu = lambda b: banks(k, b % 2, 1)
        y = lambda b: banks(k, 2 + b % 2, 1)
        xtr = lambda b: banks(k, 4 + b % 2, 1)
        htr = lambda b: banks(k, 6 + b % 2, 1)

        def trips(eng):
            return eng.value_load(r["trips"][0:1, 0:1], min_val=first_trips, max_val=NB_TAB // RING - 1)

        with nc.Block() as block:

            @block.sync
            def _(sp):
                n_trips = trips(sp)
                for s in range(RING):
                    expert_loads(k, sp, layer, s, s, gu_in[s], dn_in[s], w_gu[s], w_dn[s])
                with sp.Fori(0, n_trips - 1) as i:
                    for s in range(RING):
                        hold(sp, passed, (y_ready, RING * i + s + 1))
                        expert = sp.value_load(r["expert"][0:1, bass.ds(RING * (i + 1) + s, 1)], min_val=0, max_val=NE - 1)
                        expert_loads(k, sp, layer, s, expert, gu_in[s], dn_in[s], w_gu[s], w_dn[s])

            @block.gpsimd
            def _(pool):
                n_trips = trips(pool)
                for s in range(RING):
                    pool.memset(xg[s][:], 0.0).then_inc(zeroed, 1)
                pool.wait_ge(zeroed, RING)

                def gather(i, s):
                    hold(pool, passed, (x_turned, RING * i), (y_out[s], 16 * i))
                    pool.tensor_copy(x_idx[s][:], r["tokens"][:, bass.ds(RING * i + s, 1)]).then_inc(idx_done, 1)
                    pool.tensor_copy(y_idx[s][:], r["slots"][:, bass.ds(RING * i + s, 1)]).then_inc(idx_done, 1)
                    hold(pool, passed, (idx_done, 2 * (RING * i + s) + 2))
                    pool.indirect_dma_start(out=xg[s][:], out_offset=None, in_=k.x_d[:, :],
                                            in_offset=bass.IndirectOffsetOnAxis(ap=x_idx[s][:, 0:1], axis=0),
                                            bounds_check=T - 1, oob_is_err=False).then_inc(x_in[s], 16)

                def scatter(i, s):
                    hold(pool, passed, (y_act, RING * i + s + 1), (y_dve, RING * i + s + 1))
                    pool.indirect_dma_start(out=k.y_d[:, :], out_offset=bass.IndirectOffsetOnAxis(ap=y_idx[s][:, 0:1], axis=0),
                                            in_=yo[s][:], in_offset=None, bounds_check=2 * T - 1, oob_is_err=False).then_inc(y_out[s], 16)

                with pool.Fori(0, n_trips) as i:
                    for s in range(RING):
                        gather(i, s)
                    for s in range(RING):
                        scatter(i, s)
                for s in range(RING):
                    hold(pool, passed, (y_out[s], 16 * n_trips))

            @block.tensor
            def _(pe):
                n_trips = trips(pe)

                def turn_x(i, s):
                    b = RING * i + s
                    hold(pe, passed, (x_in[s], 16 * (i + 1)), *([(xgT_ready, b - 1)] if s >= 2 else [(y_act, RING * i), (y_dve, RING * i)]))
                    for j in range(J):
                        last = nc.tensor.transpose(xtr(s)[:, j * CB:(j + 1) * CB], xg[s][:, j * P:(j + 1) * P], k.ident[0:CB, 0:CB])
                    last.then_inc(x_turned, 1)

                def up(i, s):
                    b = RING * i + s
                    hold(pe, passed, (gu_in[s], 32 * (i + 1)), (xgT_ready, b + 1), *[(hid_ready, b - 1)] * (s >= 2))
                    for j in range(J):
                        for h in range(2):
                            last = nc.tensor.matmul(gu(s)[h * CB:(h + 1) * CB, 0:EH], xgT[:, s % 2, j, :], w_gu[s][:, j, h * EH:(h + 1) * EH],
                                                    start=(j == 0), stop=(j == J - 1))
                    last.then_inc(gu_ready, 1)

                def down(i, s):
                    b = RING * i + s
                    hold(pe, passed, (hid_ready, b + 1), *[(hidT_ready, b - 1)] * (s >= 2))
                    for j in range(JE):
                        last = nc.tensor.transpose(htr(s)[:, j * CB:(j + 1) * CB], hid[:, s % 2, j * P:(j + 1) * P], k.ident[0:CB, 0:CB])
                    last.then_inc(hid_turned, 1)
                    hold(pe, passed, (dn_in[s], 16 * (i + 1)), (hidT_ready, b + 1), *[(y_act, b - 1), (y_dve, b - 1)] * (s >= 2))
                    for j in range(JE):
                        for h in range(2):
                            last = nc.tensor.matmul(y(s)[h * CB:(h + 1) * CB, :], hidT[:, s % 2, j, :], w_dn[s][:, j, h * BANK:(h + 1) * BANK],
                                                    start=(j == 0), stop=(j == JE - 1))
                    last.then_inc(y_ready, 1)

                with pe.Fori(0, n_trips) as i:
                    turn_x(i, 0)
                    for s in range(RING):
                        up(i, s)
                        if s + 1 < RING:
                            turn_x(i, s + 1)
                        if s:
                            down(i, s - 1)
                    down(i, RING - 1)

            @block.scalar
            def _(act):
                n_trips = trips(act)
                nc.scalar.preload_act_table(ACT.Silu)

                def gate(i, s):
                    b = RING * i + s
                    hold(act, passed, (gu_ready, b + 1), (hid_ready, b - 1 if s >= 2 else RING * i))
                    nc.scalar.activation(silu[:, s % 2, :], gu(s)[0:CB, 0:EH], ACT.Silu).then_inc(silu_ready, 1)

                def out(i, s):
                    hold(act, passed, (y_ready, RING * i + s + 1), (y_out[s], 16 * i))
                    nc.scalar.activation(yo[s][:, 0:BANK], y(s)[0:CB, :], ACT.Copy).then_inc(y_act, 1)

                with act.Fori(0, n_trips) as i:
                    for s in range(RING):
                        gate(i, s)
                        if s:
                            out(i, s - 1)
                    out(i, RING - 1)

            @block.vector
            def _(dve):
                n_trips = trips(dve)

                def copy_x(i, s):
                    b = RING * i + s
                    hold(dve, passed, (x_turned, b + 1), (gu_ready, b - 1 if s >= 2 else RING * i))
                    nc.vector.tensor_copy(xgT[:, s % 2, :, :].rearrange("p j q -> p (j q)"), xtr(s)).then_inc(xgT_ready, 1)

                def hidden(i, s):
                    b = RING * i + s
                    hold(dve, passed, (silu_ready, b + 1), (hid_turned, b - 1 if s >= 2 else RING * i))
                    nc.vector.tensor_tensor(hid[:, s % 2, :], silu[:, s % 2, :], gu(s)[CB:P, 0:EH], ALU.mult).then_inc(hid_ready, 1)

                def copy_h(i, s):
                    b = RING * i + s
                    hold(dve, passed, (hid_turned, b + 1), (y_ready, b - 1 if s >= 2 else RING * i))
                    nc.vector.tensor_copy(hidT[:, s % 2, :, :].rearrange("p j q -> p (j q)"), htr(s)[:, 0:JE * CB]).then_inc(hidT_ready, 1)

                def out(i, s):
                    hold(dve, passed, (y_ready, RING * i + s + 1), (y_out[s], 16 * i))
                    nc.vector.tensor_copy(yo[s][:, BANK:D], y(s)[CB:P, :]).then_inc(y_dve, 1)

                with dve.Fori(0, n_trips) as i:
                    copy_x(i, 0)
                    for s in range(RING):
                        if s + 1 < RING:
                            copy_x(i, s + 1)
                        hidden(i, s)
                        if s:
                            copy_h(i, s - 1)
                            out(i, s - 1)
                    copy_h(i, RING - 1)
                    out(i, RING - 1)


def combine(k, tag, layer, r, last_layer):
    nc = k.nc
    with ExitStack() as c:
        sb = lambda n, s, d=F32: c.enter_context(nc.sbuf_tensor(f"{tag}_{n}", s, d))
        sem = lambda n: new_signal(k, f"{tag}_{n}")
        g = sb("g", [P, D])
        b = sb("b", [P, D])
        ys = sb("ys", [P, 2, 2, D])
        stats = sb("stats", [P, 2, 2, 6])
        mv = sb("mv", [P, 2, 4])
        y_in = [sem("y_in0"), sem("y_in1")]
        p_in, steps_s, y_sum, y_used, var_done, inv_done, centred, scaled, x_ready, xt_ready, xt_act, xt_dve, out_sem = (
            sem(n) for n in "p_in step y_sum y_used var_done inv_done centred scaled x_ready xt_ready xt_act xt_dve out".split())
        tr = lambda t: banks(k, 2 * (t % 2), 2)

        with nc.Block() as block:

            @block.sync
            def _(sp):
                sp.dma_start(g[:], k.ln_g[layer, 1:2, :].to_broadcast([P, D])).then_inc(p_in, 16)
                sp.dma_start(b[:], k.ln_b[layer, 1:2, :].to_broadcast([P, D])).then_inc(p_in, 16)

                def out(t):
                    sp.wait_ge(x_ready, t + 1)
                    dst = k.o_y_p[0, t * P:(t + 1) * P, :] if t < 4 else k.o_y_s[0, :, :]
                    sp.dma_start(dst, k.x[0:ROWS[t], t, :]).then_inc(out_sem, 16)

                for t in range(NT):
                    if t >= 2:
                        sp.wait_ge(y_used, t - 1)
                    for c_ in range(2):
                        at = c_ * T + t * P
                        sp.dma_start(ys[0:ROWS[t], t % 2, c_, :], k.y_d[at:at + ROWS[t], :]).then_inc(y_in[t % 2], 16)
                    if last_layer and t >= 2:
                        out(t - 2)
                if last_layer:
                    out(3)
                    out(4)
                    sp.wait_ge(out_sem, 16 * NT)

            def half_out(dve, t):
                dve.wait_ge(xt_ready, t + 1)
                nc.vector.tensor_copy(k.xT[:, 4:8, t * P:t * P + ROWS[t]],
                                      tr(t)[:, BANK:].rearrange("p (j q) -> p j q", q=P)[:, :, 0:ROWS[t]]).then_inc(xt_dve, 1)

            @block.vector
            def _(dve):
                steps = Steps(dve, steps_s)
                dve.wait_ge(p_in, 32)
                for t in range(NT):
                    rr = ROWS[t]
                    dve.wait_ge(y_in[t % 2], 32 * (t // 2 + 1))
                    y0, y1 = ys[0:rr, t % 2, 0, :], ys[0:rr, t % 2, 1, :]
                    steps.then(nc.vector.tensor_scalar(y0, y0, r["weight"][0:rr, 0, t:t + 1], None, ALU.mult))
                    nc.vector.scalar_tensor_tensor(y0, y1, r["weight"][0:rr, 1, t:t + 1], y0, ALU.mult, ALU.add).then_inc(y_sum, 1)
                    norm_tile(k, dve, steps, t, lambda t: ys[0:ROWS[t], t % 2, 0, :], y_sum, t + 1, y_used, stats, mv, var_done, inv_done, centred)
                    if not last_layer and t:
                        half_out(dve, t - 1)
                if not last_layer:
                    half_out(dve, NT - 1)

            @block.gpsimd
            def _(pool):
                pool.wait_ge(p_in, 32)
                for t in range(NT):
                    norm_tail(k, pool, t, g, b, mv, var_done, inv_done, centred, scaled, x_ready)

            if not last_layer:

                @block.tensor
                def _(pe):
                    for t in range(NT):
                        pe.wait_ge(x_ready, t + 1)
                        if t >= 2:
                            pe.wait_ge(xt_act, t - 1)
                            pe.wait_ge(xt_dve, t - 1)
                        for j in range(J):
                            last = nc.tensor.transpose(tr(t)[:, j * P:j * P + ROWS[t]], k.x[0:ROWS[t], t, j * P:(j + 1) * P], k.ident[0:ROWS[t], 0:ROWS[t]])
                        last.then_inc(xt_ready, 1)

                @block.scalar
                def _(act):
                    for t in range(NT):
                        act.wait_ge(xt_ready, t + 1)
                        nc.scalar.activation(k.xT[:, 0:4, t * P:t * P + ROWS[t]],
                                             tr(t)[:, 0:BANK].rearrange("p (j q) -> p j q", q=P)[:, :, 0:ROWS[t]], ACT.Copy).then_inc(xt_act, 1)


def mixture(k, tag, layer, last_layer):
    with ExitStack() as c:
        sb = lambda n, s, d=F32: c.enter_context(k.nc.sbuf_tensor(f"{tag}_{n}", s, d))
        r = {"weight": sb("weight", [P, 2, NT]), "expert": sb("expert", [1, NB_TAB], I32), "trips": sb("trips", [1, 1], I32),
             "slots": sb("slots", [CB, NB_TAB], I32), "tokens": sb("tokens", [CB, NB_TAB], I32)}
        route(k, tag + "_route", layer, r)
        experts(k, tag + "_experts", layer, r)
        combine(k, tag + "_combine", layer, r, last_layer)


def stream_step(nc, dram):
    with ExitStack() as ctx:
        k = Core(nc, ctx, dram)
        setup_and_gates(k)
        attend_pairs(k, "fox", 0, 4, {"zeroed": 4})
        attend_pairs(k, "sb", 4, 4, {"zeroed": 5})
        mix_out(k, "mix0", 0, k.ab_w_out)
        clear_signals(k)
        mixture(k, "moe0", 0, False)
        clear_signals(k)
        with ExitStack() as c:
            sb = lambda n, s, d=F32: c.enter_context(nc.sbuf_tensor(f"mla_{n}", s, d))
            m = {"zeroed": 3, "cqT": sb("cqT", [P, JQ, TP]), "ckvT": sb("ckvT", [P, JC, KEYS]),
                 "kh": [sb(f"kh{h}", [QW, KEYS]) for h in range(2)], "mask": sb("mask", [P, 704]),
                 "mask_width": [704, 704, 704, 704, T], "cos": sb("cos", [P, NT, ROPE // 2]), "sin": sb("sin", [P, NT, ROPE // 2])}
            mla_latents(k, m)
            attend_pairs(k, "mla", 0, 8, m)
        mix_out(k, "mix1", 1, k.mla_w_out)
        clear_signals(k)
        mixture(k, "moe1", 1, True)
        clear_signals(k)


_OUTS = [
    ("o_y_p", (1, SEQ, D)), ("o_y_s", (1, NEW, D)),
    ("o_fk_p", (1, 1, SEQ, HEADS, HD)), ("o_fv_p", (1, 1, SEQ, HEADS, HD)), ("o_logf_p", (1, 1, SEQ, HEADS)),
    ("o_sk_p", (1, 1, SEQ, HEADS, HD)), ("o_sv_p", (1, 1, SEQ, HEADS, HD)),
    ("o_ckv_p", (1, 1, SEQ, KV_LORA)), ("o_kr_p", (1, 1, SEQ, ROPE)),
    ("o_fk_s", (1, 1, NEW, HEADS, HD)), ("o_fv_s", (1, 1, NEW, HEADS, HD)), ("o_logf_s", (1, 1, NEW, HEADS)),
    ("o_sk_s", (1, 1, NEW, HEADS, HD)), ("o_sv_s", (1, 1, NEW, HEADS, HD)),
    ("o_ckv_s", (1, 1, NEW, KV_LORA)), ("o_kr_s", (1, 1, NEW, ROPE)),
]


def _laid_out(np, a):
    def by_feature(w):
        return w.reshape(w.shape[0] // P, P, -1).transpose(1, 0, 2)

    x_rows = np.concatenate([a["x_prompt"][0], a["x_sample"][0]])
    w_in = a["ab_w_in"][0]
    W = HEADS * HD
    starts = [0, W, 2 * W, 3 * W + HEADS, 4 * W + HEADS, 5 * W + HEADS]
    tiles = [by_feature(w_in[:, starts[3 * side + n] + p * P:starts[3 * side + n] + (p + 1) * P]).reshape(P, J * P)
             for side in range(2) for p in range(4) for n in range(3)]
    heads_t = lambda c: c[0, 0].reshape(PAST, 4, P).transpose(1, 2, 0)
    heads_v = lambda c: c[0, 0].reshape(4, P, 4, P).transpose(2, 1, 0, 3).reshape(4, P, 4 * P)
    w_uq = a["mla_w_uq"][0].reshape(JQ, P, 8, 2 * QW).transpose(2, 1, 0, 3).reshape(8, P, JQ * 2 * QW)
    ukv = a["mla_w_ukv"][0].reshape(JC, P, 8, 2, 2, HD)
    ukv = ukv.transpose(2, 1, 0, 4, 3, 5).reshape(8, P, JC * 2 * P)
    w_r = np.stack([by_feature(np.concatenate([a["moe_w_group"][l]] + [a["moe_w_router"][l, g] for g in range(GROUPS)], axis=1))
                    for l in range(2)])
    b_r = np.concatenate([a["moe_b_group"], a["moe_b_router"].reshape(2, NE)], axis=1)
    half = ROPE // 2
    freq = np.float32(10000.0) ** (-np.arange(half, dtype=np.float32) / np.float32(half))
    pos = np.concatenate([np.arange(SEQ), PAST + np.arange(NEW), np.zeros(TP - T)]).astype(np.float32)
    ang = pos[:, None] * freq[None, :].astype(np.float32)
    table = lambda f: f(ang).astype(np.float32).reshape(NT, P, half).transpose(1, 0, 2)
    return {
        "x_rows": x_rows, "x_t": by_feature(x_rows.T), "w_ab": np.stack(tiles),
        "w_f": by_feature(w_in[:, 3 * W:3 * W + HEADS]), "b_f": a["ab_b_forget"][0][:, None],
        "logf_past": a["cache_fox_logf"][0, 0].T,
        "k_past": np.concatenate([heads_t(a["cache_fox_k"]), heads_t(a["cache_sb_k"])]),
        "v_past": np.concatenate([heads_v(a["cache_fox_v"]), heads_v(a["cache_sb_v"])]),
        "ab_w_out": a["ab_w_out"][0], "mla_w_out": a["mla_w_out"][0], "w_mla_down": a["mla_w_down"][0],
        "g_q": a["mla_g_q"], "g_kv": a["mla_g_kv"], "w_uq": w_uq, "w_ukv": ukv,
        "ckv_past": by_feature(a["cache_mla_ckv"][0, 0].T), "kr_past": a["cache_mla_krope"][0, 0].T,
        "cos": table(np.cos), "sin": table(np.sin), "w_r": w_r, "b_r": b_r,
        "w_gate": a["moe_w_gate"].reshape(2, NE, D, EH), "w_up": a["moe_w_up"].reshape(2, NE, D, EH),
        "w_down": a["moe_w_down"].reshape(2, NE, EH, D), "ln_g": a["ln_g"], "ln_b": a["ln_b"],
    }


def kernel(**inputs):
    import numpy as np
    import concourse.bacc as bacc
    from concourse.bass_utils import run_bass_kernel_spmd

    nc = bacc.Bacc("TRN2", target_bir_lowering=False, num_devices=1)
    arrays = {f"in_{n}": np.ascontiguousarray(v) for n, v in _laid_out(np, {n: np.asarray(v) for n, v in inputs.items()}).items()}
    dram = {n[3:]: nc.dram_tensor(n, v.shape, F32, kind="ExternalInput").ap() for n, v in arrays.items()}
    for name, shape in _OUTS:
        dram[name] = nc.dram_tensor(name, shape, F32, kind="ExternalOutput").ap()
    for name, shape in (("cum_d", (HEADS, KEYS)), ("x_d", (T, D)), ("y_d", (2 * T, D))):
        dram[name] = nc.dram_tensor(name, shape, F32, kind="Internal").ap()
    rows = lambda n: dram[n].rearrange("a b t h d -> (a b t) (h d)")
    dram["o_kv"] = {"fox": [rows(n) for n in ("o_fk_p", "o_fv_p", "o_fk_s", "o_fv_s")],
                    "sb": [rows(n) for n in ("o_sk_p", "o_sv_p", "o_sk_s", "o_sv_s")]}
    stream_step(nc, dram)
    got = run_bass_kernel_spmd(nc, [arrays], core_ids=[0]).results[0]
    return tuple(got[name] for name, _ in _OUTS)
```

```python
from contextlib import ExitStack

import concourse.bass as bass
from concourse import mybir

F32 = mybir.dt.float32
I32 = mybir.dt.int32
U32 = mybir.dt.uint32
ALU = mybir.AluOpType
ACT = mybir.ActivationFunctionType
AX_X = mybir.AxisListType.X

P = 128
BANK = 512
D = 1024
J = D // P
SEQ, NEW, PAST = 512, 64, 512
T = SEQ + NEW
NT = 5
TP = NT * P
ROWS = [P, P, P, P, NEW]
KEYS = SEQ + PAST + NEW
NEW_AT = SEQ + PAST
VB = 9
KEY_RANGE = [(0, P), (0, 2 * P), (0, 3 * P), (0, 4 * P), (SEQ, KEYS)]
HD = 64
HEADS = 8
ROPE = 32
QW = HD + ROPE
Q_LORA, KV_LORA = 384, 256
JQ, JC = Q_LORA // P, KV_LORA // P
DOWN = Q_LORA + KV_LORA + ROPE
GROUPS, PER_GROUP, NE = 4, 8, 32
EH = 256
JE = EH // P
CB = 64
RING = 4
NB_MAX = NE + (2 * T) // CB
NB_TAB = -(-NB_MAX // RING) * RING + RING
ALPHA = 4.0 ** 0.25
LN_EPS, RMS_EPS = 1e-5, 1e-6
NEG = -1e30
FAR = 1e6
UNITS = 2 * NT
BLOCKS_OF = [1, 2, 3, 4, 5]


def hold(eng, passed, *counts):
    for sem, count in counts:
        eng.wait_ge(sem, count)
    eng.sem_inc(passed, 1)


class Steps:

    def __init__(self, eng, sem, base=0, passed=None):
        self.eng, self.sem, self.base, self.n, self.passed = eng, sem, base, 0, passed

    def then(self, ins):
        self.n += 1
        ins.then_inc(self.sem, 1)
        self.eng.wait_ge(self.sem, self.base + self.n)
        if self.passed is not None:
            self.eng.sem_inc(self.passed, 1)


class Core:

    def __init__(self, nc, ctx, dram):
        self.nc, self.ctx = nc, ctx
        self.x_rows = dram["x_rows"]
        self.x_t = dram["x_t"]
        self.w_ab = dram["w_ab"]
        self.w_f = dram["w_f"]
        self.b_f = dram["b_f"]
        self.logf_past = dram["logf_past"]
        self.k_past = dram["k_past"]
        self.v_past = dram["v_past"]
        self.ab_w_out = dram["ab_w_out"]
        self.mla_w_out = dram["mla_w_out"]
        self.w_mla_down = dram["w_mla_down"]
        self.g_q = dram["g_q"]
        self.g_kv = dram["g_kv"]
        self.w_uq = dram["w_uq"]
        self.w_ukv = dram["w_ukv"]
        self.ckv_past = dram["ckv_past"]
        self.kr_past = dram["kr_past"]
        self.cos = dram["cos"]
        self.sin = dram["sin"]
        self.w_r = dram["w_r"]
        self.b_r = dram["b_r"]
        self.w_gate = dram["w_gate"]
        self.w_up = dram["w_up"]
        self.w_down = dram["w_down"]
        self.ln_g = dram["ln_g"]
        self.ln_b = dram["ln_b"]
        self.o_y_p = dram["o_y_p"]
        self.o_y_s = dram["o_y_s"]
        self.o_logf_p = dram["o_logf_p"]
        self.o_ckv_p = dram["o_ckv_p"]
        self.o_kr_p = dram["o_kr_p"]
        self.o_logf_s = dram["o_logf_s"]
        self.o_ckv_s = dram["o_ckv_s"]
        self.o_kr_s = dram["o_kr_s"]
        self.cum_d = dram["cum_d"]
        self.x_d = dram["x_d"]
        self.y_d = dram["y_d"]
        self.o_kv = dram["o_kv"]

        def sb(name, shape, dt=F32):
            return ctx.enter_context(nc.sbuf_tensor(name, shape, dt))

        self.psum = ctx.enter_context(nc.psum_tensor("psum", [P, 8, BANK], F32))
        self.passed = ctx.enter_context(nc.semaphore("passed"))
        self.gu_in = [[ctx.enter_context(nc.semaphore(f"gu_in{l}{n}")) for n in range(RING)] for l in range(2)]
        self.dn_in = [[ctx.enter_context(nc.semaphore(f"dn_in{l}{n}")) for n in range(RING)] for l in range(2)]
        self.signals = []
        self.sb = sb
        self.xT = sb("xT", [P, J, TP])
        self.x = sb("x", [P, NT, D])
        self.mix = sb("mix", [P, NT, D])
        self.ident = sb("ident", [P, P])
        self.cum_tok = sb("cum_tok", [P, NT, HEADS])
        self.half = sb("half", [P, 1])
        self.logits = sb("logits", [P, NT, GROUPS + NE])
        self.w_gu = [sb(f"w_gu{s}", [P, J, 2 * EH]) for s in range(3)]
        self.w_dn = [sb(f"w_dn{s}", [P, JE, D]) for s in range(3)]


def new_signal(k, name):
    k.signals.append(k.nc.alloc_semaphore(name))
    return k.signals[-1]


def clear_signals(k):
    k.nc.clear_and_free_semaphores(k.signals)
    k.signals = []
    k.nc.all_engine_barrier()


def banks(k, first, count):
    return k.psum[:, first:first + count, :].rearrange("p b n -> p (b n)")


def setup_and_gates(k):
    nc = k.nc
    with ExitStack() as c:
        sb = lambda n, s, d=F32: c.enter_context(nc.sbuf_tensor(n, s, d))
        sem = lambda n: new_signal(k, n)
        wf = sb("wf", [P, J, HEADS])
        bf = sb("bf", [HEADS, 1])
        logf = sb("logf", [HEADS, KEYS])
        cum = sb("cum", [HEADS, KEYS])
        ones = sb("ones", [HEADS, KEYS])
        t_abs = sb("t_abs", [HEADS, T])
        t_exp = sb("t_exp", [HEADS, T])
        t_ln = sb("t_ln", [HEADS, T])
        low = sb("low", [HEADS, T])
        tok = sb("tok", [P, NT, HEADS])
        xt_in, f_in, filled, z_ready, act_step, dve_step, out_sem, tok_t, tok_e, cum_ready = (
            sem(n) for n in ("g_xt_in", "g_f_in", "g_filled", "g_z_ready", "g_act_step", "g_dve_step",
                             "g_out", "g_tok_t", "g_tok_e", "g_cum_ready"))
        z = banks(k, 0, 2)[0:HEADS, 0:T]
        trans = banks(k, 2, 1)

        with nc.Block() as block:

            @block.sync
            def _(sp):
                sp.dma_start(wf[:], k.w_f).then_inc(f_in, 16)
                sp.dma_start(bf[:], k.b_f).then_inc(f_in, 16)
                sp.dma_start(k.xT[:, :, 0:T], k.x_t).then_inc(xt_in, 16)
                sp.dma_start(logf[:, SEQ:NEW_AT], k.logf_past).then_inc(f_in, 16)
                sp.wait_ge(cum_ready, 2)
                sp.dma_start(k.cum_d, cum[:]).then_inc(out_sem, 16)
                sp.wait_ge(tok_e, 2)
                sp.dma_start(k.o_logf_p.rearrange("a b (t p) h -> p (a b t) h", p=P), tok[:, 0:4, :]).then_inc(out_sem, 16)
                sp.dma_start(k.o_logf_s.rearrange("a b t h -> (a b t) h"), tok[0:NEW, 4, :]).then_inc(out_sem, 16)
                sp.wait_ge(out_sem, 48)

            @block.gpsimd
            def _(pool):
                pool.memset(k.ident[:], 0.0).then_inc(filled, 1)
                pool.wait_ge(filled, 1)
                pool.affine_select(out=k.ident[:], in_=k.ident[:], compare_op=ALU.not_equal, fill=1.0, base=0,
                                   pattern=[[-1, P]], channel_multiplier=1).then_inc(filled, 1)
                for n, (dst, value) in enumerate(((k.half[:], -0.5), (ones[:], 1.0), (k.xT[:, :, T:TP], 0.0), (k.mix[NEW:P, 4, :], 0.0), (k.cum_tok[NEW:P, 4, :], 0.0))):
                    pool.wait_ge(filled, n + 2)
                    pool.memset(dst, value).then_inc(filled, 1)

            @block.tensor
            def _(pe):
                pe.wait_ge(xt_in, 16)
                pe.wait_ge(f_in, 48)
                for j in range(J):
                    nc.tensor.matmul(z[:, 0:SEQ], wf[:, j, :], k.xT[:, j, 0:SEQ], start=(j == 0), stop=(j == J - 1))
                    last = nc.tensor.matmul(z[:, SEQ:T], wf[:, j, :], k.xT[:, j, SEQ:T], start=(j == 0), stop=(j == J - 1))
                last.then_inc(z_ready, 1)
                pe.wait_ge(filled, 2)
                pe.wait_ge(cum_ready, 2)
                for n, src in enumerate((logf, cum)):
                    for t in range(NT):
                        at = t * P if t < 4 else NEW_AT
                        last = nc.tensor.transpose(trans[0:ROWS[t], (n * NT + t) * HEADS:(n * NT + t + 1) * HEADS],
                                                   src[:, at:at + ROWS[t]], k.ident[0:HEADS, 0:HEADS])
                last.then_inc(tok_t, 1)

            @block.scalar
            def _(act):
                steps = Steps(act, act_step)
                act.wait_ge(z_ready, 1)
                act.wait_ge(f_in, 48)
                steps.then(nc.scalar.activation(t_abs[:], z, ACT.Abs, bias=bf[:, 0:1]))
                steps.then(nc.scalar.activation(t_exp[:], t_abs[:], ACT.Exp, scale=-1.0))
                nc.scalar.activation(t_ln[:], t_exp[:], ACT.Ln, bias=1.0).then_inc(act_step, 1)

            @block.vector
            def _(dve):
                steps = Steps(dve, dve_step)
                dve.wait_ge(f_in, 48)
                dve.wait_ge(act_step, 1)
                steps.then(nc.vector.tensor_scalar(low[:], z, bf[:, 0:1], 0.0, ALU.add, ALU.min))
                dve.wait_ge(act_step, 3)
                nc.vector.tensor_tensor(logf[:, 0:SEQ], low[:, 0:SEQ], t_ln[:, 0:SEQ], ALU.subtract).then_inc(dve_step, 1)
                steps.n += 1
                steps.then(nc.vector.tensor_tensor(logf[:, NEW_AT:KEYS], low[:, SEQ:T], t_ln[:, SEQ:T], ALU.subtract))
                dve.wait_ge(filled, 7)
                nc.vector.tensor_tensor_scan(cum[:, 0:SEQ], ones[:, 0:SEQ], logf[:, 0:SEQ], 0.0, ALU.mult, ALU.add).then_inc(cum_ready, 1)
                nc.vector.tensor_tensor_scan(cum[:, SEQ:KEYS], ones[:, SEQ:KEYS], logf[:, SEQ:KEYS], 0.0, ALU.mult, ALU.add).then_inc(cum_ready, 1)
                dve.wait_ge(tok_t, 1)
                for n, dst in enumerate((tok, k.cum_tok)):
                    at = n * NT * HEADS
                    nc.vector.tensor_copy(dst[:, 0:4, :], trans[:, at:at + 4 * HEADS].rearrange("p (t h) -> p t h", h=HEADS)).then_inc(tok_e, 1)
                    nc.vector.tensor_copy(dst[0:NEW, 4, :], trans[0:NEW, at + 4 * HEADS:at + 5 * HEADS]).then_inc(tok_e, 1)


def unit_of(u):
    h, t = u // NT, u % NT
    lo, hi = KEY_RANGE[t]
    return h, t, ROWS[t], lo, hi - lo


AB_AFTER = {"q0": -1, "q1": 0, "k0": 1, "k1": 2, "kt": 4, "v0": 5, "v1": 6, "vt": 8}
MLA_AFTER = {"q": -1, "q4": 0, "k": 2, "v": 4, "t4": 6, "t": 8}


def attend(k, mla, m):
    nc, passed = k.nc, k.passed
    PAIRS, FOX_PAIRS = 8, 4
    tag = "mla" if mla else "ab"
    with ExitStack() as c:
        sb = lambda n, s, d=F32: c.enter_context(nc.sbuf_tensor(f"{tag}_{n}", s, d))
        sem = lambda n: new_signal(k, f"{tag}_{n}")
        v_all = [sb(f"v_all{a}", [P, VB, P]) for a in range(2)]
        score = sb("score", [P, 2, T])
        probs = sb("probs", [P, 2, T])
        probsT = sb("probsT", [P, 2, 5, P])
        small = sb("small", [P, NT, 4])
        if mla:
            wq = sb("wq", [P, JQ, 2 * QW])
            wkv = sb("wkv", [P, JC, 2 * P])
            q_tok = sb("q_tok", [P, NT, 2, QW])
            rot = sb("rot", [P, 4, NT, 2, ROPE // 2])
            qh = [[sb(f"q{a}{h}", [QW, T]) for h in range(2)] for a in range(2)]
            kh = m["kh"]
        else:
            wp = [sb(f"w_{n}", [P, J, P]) for n in "qkv"]
            qh = [[sb(f"q{a}{h}", [P, T]) for h in range(2)] for a in range(2)]
            kT = [sb(f"kT{a}", [P, KEYS]) for a in range(2)]
            kh = [[kT[a], kT[a]] for a in range(2)]
            vT = sb("vT", [P, T])
            k_tok = sb("k_tok", [P, NT, P])
            cumk = k.x[:, :, :].rearrange("p t d -> p (t d)")[:, 0:4 * KEYS].rearrange("p (a h n) -> p a h n", a=2, h=2)
            bias = sb("bias", [P, 2, T])
            rest = bias
            cumq = sb("cumq", [P, 2, NT])
            ones = sb("ones", [P, T])
        if mla:
            names = ("zeroed w0_in w1_in projected proj_act proj_dve scores_ready scored probs_ready probsT_ready "
                     "probsT_used o_ready o_done dve_step rot_step roped")
        else:
            names = ("zeroed w0_in w1_in w2_in kp_in0 kp_in1 vp_in0 vp_in1 cumk_in0 cumk_in1 cumq_ready projected proj_act proj_dve k_out v_out "
                     "scores_ready scored bias_ready bias_step probs_ready probsT_ready probsT_used o_ready o_done "
                     "dve_step act_step soft_ready masked rest_done logit_ready")
        s = {n: sem(n) for n in names.split()}
        n_zeroed = 5 if mla else 8
        STEPS = 6 if mla else 5
        slot = lambda u: banks(k, 2 * (u % 2), 2)
        bank_t, bank_o = banks(k, 4, 1), banks(k, 5, 1)
        proj = banks(k, 6, 2)

        def of_parity(each, p, par):
            return p * (each // 2) + (each - par * (each // 2))

        def each_pair(eng, pair):
            if mla:
                with eng.Fori(0, PAIRS // 2 - 1) as i:
                    pair(2 * i, 0, "mla", True)
                    pair(2 * i + 1, 1, "mla", True)
                pair(PAIRS - 2, 0, "mla", True)
                pair(PAIRS - 1, 1, "mla", False)
                return
            with eng.Fori(0, FOX_PAIRS // 2) as i:
                pair(2 * i, 0, "fox", True)
                pair(2 * i + 1, 1, "fox", True)
            for p in range(FOX_PAIRS, PAIRS):
                pair(p, p % 2, "sb", p + 1 < PAIRS)

        def steps_after(after, u):
            return [name for name in after if after[name] == u]

        with nc.Block() as block:

            @block.sync
            def _(sp):
                row = lambda a, at: a[bass.ds(at, 1), :, :].rearrange("a p n -> p (a n)")

                def load_w(p, n):
                    if mla:
                        hold(sp, passed, (s["projected"], STEPS * p))
                        sp.dma_start(wq[:], row(k.w_uq, p)).then_inc(s["w0_in"], 16)
                        sp.dma_start(wkv[:], row(k.w_ukv, p)).then_inc(s["w1_in"], 16)
                        return
                    if not isinstance(p, int) or p:
                        hold(sp, passed, (s["projected"], STEPS * (p - 1) + (1, 2, 4)[n]))
                    sp.dma_start(wp[n][:].rearrange("p j n -> p (j n)"), row(k.w_ab, p * 3 + n)).then_inc(s[f"w{n}_in"], 16)

                def load_past(p, par, fox):
                    if not isinstance(p, int) or p:
                        hold(sp, passed, (s["o_ready"], UNITS * (p - 1)))
                    sp.dma_start(kT[par][:, SEQ:NEW_AT], row(k.k_past, p)).then_inc(s[f"kp_in{par}"], 16)
                    sp.dma_start(v_all[par][:, 4:8, :].rearrange("p b n -> p (b n)"), row(k.v_past, p)).then_inc(s[f"vp_in{par}"], 16)
                    if fox:
                        if not isinstance(p, int) or p:
                            hold(sp, passed, (s["bias_ready"], UNITS * (p - 1)))
                        for h in range(2):
                            sp.dma_start(cumk[:, par, h, :], k.cum_d[bass.ds(2 * p + h, 1), :].to_broadcast([P, KEYS])).then_inc(s[f"cumk_in{par}"], 16)

                def store(p, par, kind, kv):
                    o_p, o_s = k.o_kv[kind][kv], k.o_kv[kind][kv + 2]
                    at = p if kind == "fox" else p - FOX_PAIRS
                    done = STEPS * p + (5 if kv else 3)
                    hold(sp, passed, (s["proj_act"], done), (s["proj_dve"], done))
                    full, new = (v_all[par][:, 0:4, :], v_all[par][0:NEW, 8, :]) if kv else (k_tok[:, 0:4, :], k_tok[0:NEW, 4, :])
                    out = s["v_out"] if kv else s["k_out"]
                    sp.dma_start(o_p.rearrange("(t p) c -> p t c", p=P)[:, :, bass.ds(at * P, P)], full).then_inc(out, 16)
                    sp.dma_start(o_s[:, bass.ds(at * P, P)], new).then_inc(out, 16)

                def pair(p, par, kind, more):
                    if not more:
                        return
                    if mla:
                        if not (isinstance(p, int) and p + 2 >= PAIRS):
                            load_w(p + 2, 0)
                        return
                    last_w = isinstance(p, int) and p + 2 >= PAIRS
                    load_past(p + 1, 1 - par, kind == "fox")
                    for n in range(3):
                        if not last_w:
                            load_w(p + 2, n)
                    store(p + 1, 1 - par, kind, 0)
                    store(p + 1, 1 - par, kind, 1)

                for n in range(1 if mla else 3):
                    load_w(0, n)
                if mla:
                    load_w(1, 0)
                    with sp.Fori(0, PAIRS // 2 - 1) as i:
                        pair(2 * i, 0, "mla", True)
                        pair(2 * i + 1, 1, "mla", True)
                else:
                    load_past(0, 0, True)
                    for n in range(3):
                        load_w(1, n)
                    store(0, 0, "fox", 0)
                    store(0, 0, "fox", 1)
                    for p in range(FOX_PAIRS - 1):
                        pair(p, p % 2, "fox", True)
                    prefetch_experts(k, sp, 0, range(3))
                    for p in range(FOX_PAIRS - 1, PAIRS):
                        pair(p, p % 2, "sb", p + 1 < PAIRS)
                    sp.wait_ge(s["k_out"], 32 * PAIRS)
                    sp.wait_ge(s["v_out"], 32 * PAIRS)

            @block.tensor
            def _(pe):
                def banks_free(p, step, *more):
                    n = STEPS * p + step
                    hold(pe, passed, (s["proj_act"], n), (s["proj_dve"], n), *more)

                def project_ab(p, par, step):
                    n = "qkv".index(step[0])
                    if step[1] == "t":
                        banks_free(p, 2 if n == 1 else 4)
                        for t in range(NT):
                            at = NEW_AT if (t == 4 and n == 1) else t * P
                            src = kT[par] if n == 1 else vT
                            last = nc.tensor.transpose(proj[0:ROWS[t], t * P:(t + 1) * P], src[:, at:at + ROWS[t]], k.ident[:])
                        last.then_inc(s["projected"], 1)
                        return
                    half = int(step[1])
                    if half == 0:
                        banks_free(p, (0, 1, 3)[n], (s[f"w{n}_in"], 16 * (p + 1)))
                    for j in range(4 * half, 4 * half + 4):
                        nc.tensor.matmul(proj[:, 0:SEQ], wp[n][:, j, :], k.xT[:, j, 0:SEQ], start=(j == 0), stop=(j == J - 1))
                        last = nc.tensor.matmul(proj[:, SEQ:T], wp[n][:, j, :], k.xT[:, j, SEQ:T], start=(j == 0), stop=(j == J - 1))
                    if half:
                        last.then_inc(s["projected"], 1)

                def project_mla(p, par, step):
                    order = list(MLA_AFTER).index(step)
                    more = {"q": [(s["w0_in"], 16 * (p + 1))], "k": [], "q4": [(s["w1_in"], 16 * (p + 1))], "v": [],
                            "t4": [(s["roped"], p + 1)], "t": []}[step]
                    banks_free(p, order, *more)
                    group = lambda dst, pairs: [nc.tensor.matmul(dst, a, b, start=(n == 0), stop=(n == len(pairs) - 1)) for n, (a, b) in enumerate(pairs)][-1]
                    q_tile = lambda t: [(m["cqT"][:, j, t * P:t * P + ROWS[t]], wq[:, j, :]) for j in range(JQ)]
                    k_part = lambda lo, hi: [(wkv[:, j, 0:P], m["ckvT"][:, j, lo:hi]) for j in range(JC)]
                    v_block = lambda b, rows: [(m["ckvT"][:, j, b * P:b * P + rows], wkv[:, j, P:2 * P]) for j in range(JC)]
                    turn = lambda dst, h, t: nc.tensor.transpose(dst, q_tok[0:ROWS[t], t, h, :], k.ident[0:ROWS[t], 0:ROWS[t]])
                    if step == "q":
                        for t in range(4):
                            last = group(k.psum[:, 6 + t // 2, (t % 2) * 2 * QW:(t % 2 + 1) * 2 * QW], q_tile(t))
                    elif step == "q4":
                        group(proj[0:NEW, 0:2 * QW], q_tile(4))
                        last = group(proj[:, BANK:BANK + NEW], k_part(NEW_AT, KEYS))
                    elif step == "k":
                        group(proj[:, 0:BANK], k_part(0, BANK))
                        last = group(proj[:, BANK:2 * BANK], k_part(BANK, 2 * BANK))
                    elif step == "v":
                        for b in range(8):
                            last = group(proj[:, b * P:(b + 1) * P], v_block(b, P))
                    elif step == "t4":
                        group(proj[0:NEW, 0:P], v_block(8, NEW))
                        for h in range(2):
                            last = turn(proj[0:QW, BANK + h * NEW:BANK + (h + 1) * NEW], h, 4)
                    else:
                        for h in range(2):
                            for t in range(4):
                                last = turn(proj[0:QW, h * BANK + t * P:h * BANK + (t + 1) * P], h, t)
                    last.then_inc(s["projected"], 1)

                project, after = (project_mla, MLA_AFTER) if mla else (project_ab, AB_AFTER)

                def scores(p, par, u):
                    h, t, rows, lo, width = unit_of(u)
                    n = UNITS * p + u
                    if u == 0:
                        hold(pe, passed, (s["proj_act"], STEPS * (p + 1)), (s["proj_dve"], STEPS * (p + 1)),
                             *([] if mla else [(s[f"kp_in{par}"], of_parity(16, p, par))]))
                    elif u >= 2:
                        hold(pe, passed, (s["scored"], n - 1))
                    q = qh[par][h][0:QW, t * P:t * P + rows] if mla else qh[par][h][:, t * P:t * P + rows]
                    key = kh[par][h][0:QW, lo:lo + width] if mla else kh[par][h][:, lo:lo + width]
                    last = nc.tensor.matmul(slot(u)[0:rows, 0:min(width, BANK)], q, key[:, 0:min(width, BANK)], start=True, stop=True)
                    if width > BANK:
                        last = nc.tensor.matmul(slot(u)[0:rows, BANK:width], q, key[:, BANK:width], start=True, stop=True)
                    last.then_inc(s["scores_ready"], 1)

                def turn(p, u):
                    _, t, rows, _, _ = unit_of(u)
                    n = UNITS * p + u
                    hold(pe, passed, (s["probs_ready"], n + 1), (s["probsT_used"], n))
                    for b in range(BLOCKS_OF[t]):
                        wide = NEW if b == 4 else P
                        last = nc.tensor.transpose(bank_t[0:wide, b * rows:(b + 1) * rows],
                                                   probs[0:rows, u % 2, b * P:b * P + wide], k.ident[0:rows, 0:rows])
                    last.then_inc(s["probsT_ready"], 1)

                def values(p, par, u):
                    h, t, rows, _, _ = unit_of(u)
                    n = UNITS * p + u
                    hold(pe, passed, (s["probsT_used"], n + 1), (s["o_done"], n), *([(s[f"vp_in{par}"], of_parity(16, p, par))] if u == 4 and not mla else []))
                    first_block = 0 if t < 4 else 4
                    for b in range(BLOCKS_OF[t]):
                        last = nc.tensor.matmul(bank_o[0:rows, 0:HD], probsT[:, u % 2, b, 0:rows],
                                                v_all[par][:, first_block + b, h * HD:(h + 1) * HD], start=(b == 0), stop=(b == BLOCKS_OF[t] - 1))
                    last.then_inc(s["o_ready"], 1)

                def pair(p, par, kind, more):
                    def projections(u):
                        for step in steps_after(after, u) if more else []:
                            project(p + 1, 1 - par, step)
                    scores(p, par, 0)
                    scores(p, par, 1)
                    projections(-1)
                    for u in range(UNITS):
                        turn(p, u)
                        if u + 2 < UNITS:
                            scores(p, par, u + 2)
                        projections(u)
                        values(p, par, u)

                pe.wait_ge(s["zeroed"], n_zeroed)
                for step in after:
                    project(0, 0, step)
                each_pair(pe, pair)

            copied = list(MLA_AFTER) if mla else ["q1", "k1", "kt", "v1", "vt"]
            after_of = MLA_AFTER if mla else AB_AFTER

            @block.scalar
            def _(act):
                nc.scalar.preload_act_table_set("natural_log_exp_and_others")
                act.wait_ge(s["zeroed"], n_zeroed)
                copy = lambda dst, src, scale=1.0: nc.scalar.activation(dst, src, ACT.Copy, scale=scale)

                def copy_out(p, par, step):
                    n = STEPS * p + copied.index(step) + 1
                    waits = [(s["projected"], n)]
                    if step == "kt":
                        waits.append((s["k_out"], 32 * p))
                    if step == "vt":
                        waits.append((s["v_out"], 32 * p))
                    hold(act, passed, *waits)
                    if mla:
                        last = {
                            "q": lambda: copy(q_tok[:, 0:2, :, :].rearrange("p t h c -> p (t h c)"), proj[:, 0:4 * QW]),
                            "q4": lambda: copy(q_tok[0:NEW, 4, :, :].rearrange("p h c -> p (h c)"), proj[0:NEW, 0:2 * QW]),
                            "k": lambda: copy(kh[par][0][0:HD, 0:NEW_AT], proj[0:HD, :]),
                            "v": lambda: copy(v_all[par][:, 0:4, :].rearrange("p b c -> p (b c)"), proj[:, 0:BANK]),
                            "t4": lambda: copy(v_all[par][0:NEW, 8, :], proj[0:NEW, 0:P]),
                            "t": lambda: copy(qh[par][0][:, 0:SEQ], proj[0:QW, 0:BANK]),
                        }[step]()
                    else:
                        last = {
                            "q1": lambda: copy(qh[par][0][0:HD, :], proj[0:HD, 0:T], HD ** -0.5),
                            "k1": lambda: copy(kT[par][:, 0:SEQ], proj[:, 0:SEQ]),
                            "kt": lambda: copy(k_tok[:, 0:4, :].rearrange("p t c -> p (t c)"), proj[:, 0:BANK]),
                            "v1": lambda: copy(vT[:, 0:SEQ], proj[:, 0:SEQ]),
                            "vt": lambda: copy(v_all[par][:, 0:4, :].rearrange("p t c -> p (t c)"), proj[:, 0:BANK]),
                        }[step]()
                    last.then_inc(s["proj_act"], 1)

                def soften(p, u):
                    _, t, rows, _, width = unit_of(u)
                    n = UNITS * p + u
                    z, r = slot(u)[0:rows, 0:width], rest[0:rows, u % 2, 0:width]
                    steps = Steps(act, s["act_step"], base=2 * (n - UNITS * FOX_PAIRS), passed=passed)
                    hold(act, passed, (s["scores_ready"], n + 1), (s["scored"], n - 1 if u >= 2 else UNITS * p))
                    steps.then(nc.scalar.activation(r, z, ACT.Abs))
                    steps.then(nc.scalar.activation(r, r, ACT.Exp, scale=-1.0))
                    nc.scalar.activation(r, r, ACT.Ln, bias=1.0).then_inc(s["soft_ready"], 1)

                def exponent(p, u, kind):
                    _, t, rows, _, width = unit_of(u)
                    n = UNITS * p + u
                    ready = (s["logit_ready"], n + 1 - UNITS * FOX_PAIRS) if kind == "sb" else (s["scored"], n + 1)
                    hold(act, passed, ready, (s["probsT_ready"], n - 1 if u >= 2 else UNITS * p))
                    if kind == "sb":
                        nc.scalar.activation(probs[0:rows, u % 2, 0:width], score[0:rows, u % 2, 0:width], ACT.Exp).then_inc(s["probs_ready"], 1)
                    else:
                        nc.scalar.activation(probs[0:rows, u % 2, 0:width], score[0:rows, u % 2, 0:width], ACT.Exp, scale=-1.0,
                                             bias=small[0:rows, u % NT, 0:1], accum_out=small[0:rows, u % NT, 1:2]).then_inc(s["probs_ready"], 1)

                def turn_out(p, u):
                    _, t, rows, _, _ = unit_of(u)
                    n = UNITS * p + u
                    hold(act, passed, (s["probsT_ready"], n + 1), (s["o_ready"], n - 1 if u >= 2 else UNITS * p))
                    full = min(BLOCKS_OF[t], 4)
                    last = copy(probsT[:, u % 2, 0:full, 0:rows], bank_t[:, 0:full * rows].rearrange("p (b q) -> p b q", q=rows))
                    if t == 4:
                        last = copy(probsT[0:NEW, u % 2, 4, 0:NEW], bank_t[0:NEW, 4 * NEW:5 * NEW])
                    last.then_inc(s["probsT_used"], 1)

                def pair(p, par, kind, more):
                    def copies(u):
                        for step in copied if more else []:
                            if after_of[step] == u:
                                copy_out(p + 1, 1 - par, step)
                    if kind == "sb":
                        soften(p, 0)
                        soften(p, 1)
                    exponent(p, 0, kind)
                    if kind != "sb":
                        exponent(p, 1, kind)
                    copies(-1)
                    for u in range(UNITS):
                        turn_out(p, u)
                        if kind == "sb":
                            if u + 2 < UNITS:
                                soften(p, u + 2)
                            if u + 1 < UNITS:
                                exponent(p, u + 1, kind)
                        elif u + 2 < UNITS:
                            exponent(p, u + 2, kind)
                        copies(u)

                for step in copied:
                    copy_out(0, 0, step)
                each_pair(act, pair)

            @block.vector
            def _(dve):
                v = nc.vector
                if mla:
                    v.memset(q_tok[NEW:P, 4, :, :], 0.0).then_inc(s["zeroed"], 1)
                    v.memset(small[:], 0.0).then_inc(s["zeroed"], 1)
                else:
                    for a in range(2):
                        v.memset(qh[a][0][HD:P, :], 0.0).then_inc(s["zeroed"], 1)
                        v.memset(qh[a][1][0:HD, :], 0.0).then_inc(s["zeroed"], 1)
                    v.memset(ones[:], 1.0).then_inc(s["zeroed"], 1)
                for a in range(2):
                    v.memset(v_all[a][NEW:P, 8, :], 0.0).then_inc(s["zeroed"], 1)
                v.memset(probsT[:, :, 4, :], 0.0).then_inc(s["zeroed"], 1)
                dve.wait_ge(s["zeroed"], n_zeroed)

                def rotate(p):
                    steps = Steps(dve, s["rot_step"], base=p, passed=passed)
                    half = ROPE // 2
                    x1, x2 = q_tok[:, :, :, HD:HD + half], q_tok[:, :, :, HD + half:QW]
                    both = lambda a: a.unsqueeze(2).to_broadcast([P, NT, 2, half])
                    hold(dve, passed, (s["proj_act"], STEPS * p + 2), (s["proj_dve"], STEPS * p + 2))
                    v.tensor_tensor(rot[:, 0], x1, both(m["cos"][:]), ALU.mult)
                    v.tensor_tensor(rot[:, 1], x2, both(m["sin"][:]), ALU.mult)
                    v.tensor_tensor(rot[:, 2], x1, both(m["sin"][:]), ALU.mult)
                    steps.then(v.tensor_tensor(rot[:, 3], x2, both(m["cos"][:]), ALU.mult))
                    v.tensor_tensor(x1, rot[:, 0], rot[:, 1], ALU.subtract)
                    v.tensor_tensor(x2, rot[:, 2], rot[:, 3], ALU.add).then_inc(s["roped"], 1)

                def copy_out(p, par, step):
                    n = STEPS * p + copied.index(step) + 1
                    waits = [(s["projected"], n)]
                    if step == "kt":
                        waits.append((s["k_out"], 32 * p))
                    if step == "vt":
                        waits.append((s["v_out"], 32 * p))
                    hold(dve, passed, *waits)
                    if mla:
                        def q4():
                            v.tensor_copy(kh[par][0][0:HD, NEW_AT:KEYS], proj[0:HD, BANK:BANK + NEW])
                            return v.tensor_copy(kh[par][1][0:HD, NEW_AT:KEYS], proj[HD:P, BANK:BANK + NEW])

                        def t4():
                            v.tensor_copy(qh[par][0][:, SEQ:T], proj[0:QW, BANK:BANK + NEW])
                            return v.tensor_copy(qh[par][1][:, SEQ:T], proj[0:QW, BANK + NEW:BANK + 2 * NEW])
                        last = {
                            "q": lambda: v.tensor_copy(q_tok[:, 2:4, :, :].rearrange("p t h c -> p (t h c)"), proj[:, BANK:BANK + 4 * QW]),
                            "q4": q4,
                            "k": lambda: v.tensor_copy(kh[par][1][0:HD, 0:NEW_AT], proj[HD:P, :]),
                            "v": lambda: v.tensor_copy(v_all[par][:, 4:8, :].rearrange("p b c -> p (b c)"), proj[:, BANK:2 * BANK]),
                            "t4": t4,
                            "t": lambda: v.tensor_copy(qh[par][1][:, 0:SEQ], proj[0:QW, BANK:2 * BANK]),
                        }[step]()
                    else:
                        last = {
                            "q1": lambda: v.tensor_scalar(qh[par][1][HD:P, :], proj[HD:P, 0:T], HD ** -0.5, None, ALU.mult),
                            "k1": lambda: v.tensor_copy(kT[par][:, NEW_AT:KEYS], proj[:, SEQ:T]),
                            "kt": lambda: v.tensor_copy(k_tok[0:NEW, 4, :], proj[0:NEW, BANK:BANK + P]),
                            "v1": lambda: v.tensor_copy(vT[:, SEQ:T], proj[:, SEQ:T]),
                            "vt": lambda: v.tensor_copy(v_all[par][0:NEW, 8, :], proj[0:NEW, BANK:BANK + P]),
                        }[step]()
                    last.then_inc(s["proj_dve"], 1)
                    if step == "q4":
                        rotate(p)

                def logits(p, u, kind):
                    _, t, rows, _, width = unit_of(u)
                    n = UNITS * p + u
                    hold(dve, passed, (s["scores_ready"], n + 1), *([(s["bias_ready"], n + 1)] if kind == "fox" else []),
                         (s["probs_ready"], n - 1 if u >= 2 else UNITS * p))
                    add = bias[0:rows, u % 2, 0:width] if kind == "fox" else m["mask"][0:rows, m["mask_width"][t] - width:m["mask_width"][t]]
                    v.tensor_tensor_reduce(out=score[0:rows, u % 2, 0:width], in0=slot(u)[0:rows, 0:width], in1=add,
                                           scale=-1.0 if kind == "fox" else -float(QW) ** -0.5, scalar=3e38, op0=ALU.add, op1=ALU.min,
                                           accum_out=small[0:rows, u % NT, 0:1]).then_inc(s["scored"], 1)

                def softplus(p, u):
                    _, t, rows, _, width = unit_of(u)
                    n = UNITS * p + u
                    hold(dve, passed, (s["soft_ready"], n + 1 - UNITS * FOX_PAIRS), (s["probs_ready"], n - 1 if u >= 2 else UNITS * p))
                    v.scalar_tensor_tensor(score[0:rows, u % 2, 0:width], slot(u)[0:rows, 0:width], 0.0,
                                           rest[0:rows, u % 2, 0:width], ALU.max, ALU.add).then_inc(s["rest_done"], 1)

                def stick(p, u):
                    _, t, rows, _, width = unit_of(u)
                    n = UNITS * p + u
                    hold(dve, passed, (s["masked"], n + 1 - UNITS * FOX_PAIRS))
                    steps = Steps(dve, s["dve_step"], base=n, passed=passed)
                    steps.then(v.tensor_tensor_scan(rest[0:rows, u % 2, 0:width][:, ::-1], ones[0:rows, 0:width],
                                                    score[0:rows, u % 2, 0:width][:, ::-1], 0.0, ALU.mult, ALU.add))
                    v.tensor_tensor(score[0:rows, u % 2, 0:width], slot(u)[0:rows, 0:width], rest[0:rows, u % 2, 0:width],
                                    ALU.subtract).then_inc(s["scored"], 1)

                def finish(p, u, kind):
                    h, t, rows, _, _ = unit_of(u)
                    n = UNITS * p + u
                    dst = k.mix[0:rows, t, bass.ds(p * P + h * HD, HD)]
                    if kind == "sb":
                        hold(dve, passed, (s["o_ready"], n + 1))
                        v.tensor_copy(dst, bank_o[0:rows, 0:HD]).then_inc(s["o_done"], 1)
                        return
                    steps = Steps(dve, s["dve_step"], base=n, passed=passed)
                    hold(dve, passed, (s["probs_ready"], n + 1))
                    steps.then(v.reciprocal(small[0:rows, u % NT, 2:3], small[0:rows, u % NT, 1:2]))
                    hold(dve, passed, (s["o_ready"], n + 1))
                    v.tensor_scalar(dst, bank_o[0:rows, 0:HD], small[0:rows, u % NT, 2:3], None, ALU.mult).then_inc(s["o_done"], 1)

                def pair(p, par, kind, more):
                    def copies(u):
                        for step in copied if more else []:
                            if after_of[step] == u:
                                copy_out(p + 1, 1 - par, step)
                    if kind == "sb":
                        softplus(p, 0)
                        softplus(p, 1)
                        stick(p, 0)
                    else:
                        if kind == "fox":
                            hold(dve, passed, (s["bias_ready"], UNITS * p))
                            for h in range(2):
                                last = v.tensor_copy(cumq[:, h, :].unsqueeze(2), k.cum_tok[:, :, bass.ds(2 * p + h, 1)])
                            last.then_inc(s["cumq_ready"], 1)
                        logits(p, 0, kind)
                        logits(p, 1, kind)
                    copies(-1)
                    for u in range(UNITS):
                        if kind == "sb":
                            if u + 1 < UNITS:
                                stick(p, u + 1)
                            if u + 2 < UNITS:
                                softplus(p, u + 2)
                        elif u + 2 < UNITS:
                            logits(p, u + 2, kind)
                        finish(p, u, kind)
                        copies(u)

                for step in copied:
                    copy_out(0, 0, step)
                each_pair(dve, pair)

            if not mla:

                @block.gpsimd
                def _(pool):
                    pool.wait_ge(s["zeroed"], n_zeroed)
                    fills = {x: pool.to_reg(x) for x in (NEG, 0.0)}

                    def decay(p, par, u):
                        h, t, rows, lo, width = unit_of(u)
                        n = UNITS * p + u
                        steps = Steps(pool, s["bias_step"], base=n, passed=passed)
                        hold(pool, passed, *([(s[f"cumk_in{par}"], of_parity(32, p, par)), (s["cumq_ready"], p + 1)] if u == 0 else []),
                             (s["scored"], n - 1 if u >= 2 else UNITS * p))
                        steps.then(pool.tensor_scalar(bias[0:rows, u % 2, 0:width], cumk[0:rows, par, h, lo:lo + width], -1.0,
                                                      cumq[0:rows, h, t:t + 1], ALU.mult, ALU.add))
                        d = bias[0:rows, u % 2, width - rows:width]
                        pool.affine_select(out=d, in_=d, compare_op=ALU.is_ge, fill=fills[NEG], base=0, pattern=[[-1, rows]],
                                           channel_multiplier=1).then_inc(s["bias_ready"], 1)

                    def cut(p, u, src, base, fill, done):
                        _, t, rows, _, width = unit_of(u)
                        hold(pool, passed, (s[src], UNITS * (p - base) + u + 1))
                        d = score[0:rows, u % 2, width - rows:width]
                        pool.affine_select(out=d, in_=d, compare_op=ALU.is_gt, fill=fills[fill], base=0, pattern=[[-1, rows]],
                                           channel_multiplier=1).then_inc(s[done], 1)

                    def pair(p, par, kind, more):
                        if kind == "fox":
                            for u in range(UNITS):
                                decay(p, par, u)
                            return
                        for u in range(2):
                            cut(p, u, "rest_done", FOX_PAIRS, 0.0, "masked")
                        cut(p, 0, "scored", 0, NEG, "logit_ready")
                        for u in range(UNITS):
                            if u + 1 < UNITS:
                                cut(p, u + 1, "scored", 0, NEG, "logit_ready")
                            if u + 2 < UNITS:
                                cut(p, u + 2, "rest_done", FOX_PAIRS, 0.0, "masked")

                    each_pair(pool, pair)


def mla_latents(k, m):
    nc = k.nc
    half = ROPE // 2
    with ExitStack() as c:
        sb = lambda n, s, d=F32: c.enter_context(nc.sbuf_tensor(f"lat_{n}", s, d))
        sem = lambda n: new_signal(k, f"lat_{n}")
        w = sb("w", [P, J, DOWN])
        gains = sb("gains", [P, Q_LORA + KV_LORA])
        junk = sb("junk", [P, 2, Q_LORA + KV_LORA])
        cq = sb("cq", [P, 2, Q_LORA])
        ckv = sb("ckv", [P, NT, KV_LORA])
        kr = sb("kr", [P, NT, ROPE])
        rot = sb("rot", [P, 4, half])
        ms = sb("ms", [P, NT, 4])
        w_in, g_in, past_in, z_ready, squared, mean_done, inv_done, normed, turned, turned_q, turned_k, rot_step, out_sem, filled = (
            sem(n) for n in ("w_in g_in past_in z_ready squared mean_done inv_done normed turned turned_q turned_k "
                             "rot_step out filled").split())
        z = lambda t: banks(k, 2 * (t % 2), 2)
        tr = lambda t: banks(k, 4 + 2 * (t % 2), 2)

        with nc.Block() as block:

            @block.sync
            def _(sp):
                sp.dma_start(w[:], k.w_mla_down.rearrange("(j p) n -> p j n", p=P)).then_inc(w_in, 16)
                sp.dma_start(gains[:, 0:Q_LORA], k.g_q.to_broadcast([P, Q_LORA])).then_inc(g_in, 16)
                sp.dma_start(gains[:, Q_LORA:], k.g_kv.to_broadcast([P, KV_LORA])).then_inc(g_in, 16)
                sp.dma_start(m["cos"][:], k.cos).then_inc(g_in, 16)
                sp.dma_start(m["sin"][:], k.sin).then_inc(g_in, 16)
                sp.dma_start(m["ckvT"][:, :, SEQ:NEW_AT], k.ckv_past).then_inc(past_in, 16)
                for h in range(4):
                    sp.dma_start(m["kh"][h // 2][h % 2][HD:QW, SEQ:NEW_AT], k.kr_past).then_inc(past_in, 16)
                sp.wait_ge(normed, NT)
                sp.dma_start(k.o_ckv_p.rearrange("a b (t p) c -> p (a b t) c", p=P), ckv[:, 0:4, :]).then_inc(out_sem, 16)
                sp.dma_start(k.o_ckv_s.rearrange("a b t c -> (a b t) c"), ckv[0:NEW, 4, :]).then_inc(out_sem, 16)
                sp.dma_start(k.o_kr_p.rearrange("a b (t p) c -> p (a b t) c", p=P), kr[:, 0:4, :]).then_inc(out_sem, 16)
                sp.dma_start(k.o_kr_s.rearrange("a b t c -> (a b t) c"), kr[0:NEW, 4, :]).then_inc(out_sem, 16)
                sp.wait_ge(out_sem, 64)
                sp.wait_ge(past_in, 80)

            @block.tensor
            def _(pe):
                pe.wait_ge(w_in, 16)

                def down(t):
                    if t >= 2:
                        pe.wait_ge(normed, t - 1)
                        pe.wait_ge(squared, t - 1)
                    for lo, hi in ((0, BANK), (BANK, DOWN)):
                        for j in range(J):
                            last = nc.tensor.matmul(z(t)[0:ROWS[t], lo:hi], k.xT[:, j, t * P:t * P + ROWS[t]], w[:, j, lo:hi],
                                                    start=(j == 0), stop=(j == J - 1))
                    last.then_inc(z_ready, 1)

                def turn(t):
                    r = ROWS[t]
                    pe.wait_ge(normed, t + 1)
                    if t >= 2:
                        pe.wait_ge(turned_q, t - 1)
                        pe.wait_ge(turned_k, t - 1)
                    for j in range(JQ):
                        nc.tensor.transpose(tr(t)[:, j * P:j * P + r], cq[0:r, t % 2, j * P:(j + 1) * P], k.ident[0:r, 0:r])
                    for j in range(JC):
                        nc.tensor.transpose(tr(t)[:, BANK + j * P:BANK + j * P + r], ckv[0:r, t, j * P:(j + 1) * P], k.ident[0:r, 0:r])
                    nc.tensor.transpose(tr(t)[0:ROPE, BANK + 2 * P:BANK + 2 * P + r], kr[0:r, t, :], k.ident[0:r, 0:r]).then_inc(turned, 1)

                for t in range(NT):
                    down(t)
                    if t:
                        turn(t - 1)
                turn(NT - 1)

            def copy_q(act, t):
                r = ROWS[t]
                act.wait_ge(turned, t + 1)
                nc.scalar.activation(m["cqT"][:, :, t * P:t * P + r], tr(t)[:, 0:JQ * P].rearrange("p (j q) -> p j q", q=P)[:, :, 0:r],
                                     ACT.Copy).then_inc(turned_q, 1)

            @block.scalar
            def _(act):
                for t in range(NT):
                    r = ROWS[t]
                    act.wait_ge(z_ready, t + 1)
                    if t >= 2:
                        act.wait_ge(squared, t - 1)
                    nc.scalar.activation(junk[0:r, t % 2, 0:Q_LORA], z(t)[0:r, 0:Q_LORA], ACT.Square, accum_out=ms[0:r, t, 0:1])
                    nc.scalar.activation(junk[0:r, t % 2, Q_LORA:], z(t)[0:r, Q_LORA:Q_LORA + KV_LORA], ACT.Square,
                                         accum_out=ms[0:r, t, 1:2]).then_inc(squared, 1)
                    if t:
                        copy_q(act, t - 1)
                copy_q(act, NT - 1)

            @block.gpsimd
            def _(pool):
                pool.memset(m["mask"][:], 0.0).then_inc(filled, 1)
                pool.wait_ge(filled, 1)
                pool.memset(m["mask"][0:HD, m["mask_width"][0] - HD:m["mask_width"][0]], NEG).then_inc(filled, 1)
                for t in range(NT):
                    r = ROWS[t]
                    pool.wait_ge(mean_done, 2 * (t + 1))
                    pool.tensor_tensor(ms[0:r, t, 2:4], ms[0:r, t, 0:2], k.half[0:r, 0:1].to_broadcast([r, 2]), ALU.pow).then_inc(inv_done, 1)

            @block.vector
            def _(dve):
                steps = Steps(dve, rot_step)
                dve.wait_ge(g_in, 64)

                def norm(t):
                    r = ROWS[t]
                    dve.wait_ge(squared, t + 1)
                    dve.wait_ge(z_ready, t + 1)
                    nc.vector.tensor_scalar(ms[0:r, t, 0:1], ms[0:r, t, 0:1], 1.0 / Q_LORA, RMS_EPS, ALU.mult, ALU.add).then_inc(mean_done, 1)
                    nc.vector.tensor_scalar(ms[0:r, t, 1:2], ms[0:r, t, 1:2], 1.0 / KV_LORA, RMS_EPS, ALU.mult, ALU.add).then_inc(mean_done, 1)
                    x1 = z(t)[0:r, DOWN - ROPE:DOWN - half]
                    x2 = z(t)[0:r, DOWN - half:DOWN]
                    cos, sin = m["cos"][0:r, t, :], m["sin"][0:r, t, :]
                    nc.vector.tensor_tensor(rot[0:r, 0], x1, cos, ALU.mult)
                    nc.vector.tensor_tensor(rot[0:r, 1], x2, sin, ALU.mult)
                    nc.vector.tensor_tensor(rot[0:r, 2], x1, sin, ALU.mult)
                    steps.then(nc.vector.tensor_tensor(rot[0:r, 3], x2, cos, ALU.mult))
                    nc.vector.tensor_tensor(kr[0:r, t, 0:half], rot[0:r, 0], rot[0:r, 1], ALU.subtract)
                    steps.then(nc.vector.tensor_tensor(kr[0:r, t, half:ROPE], rot[0:r, 2], rot[0:r, 3], ALU.add))
                    dve.wait_ge(inv_done, t + 1)
                    if t >= 2:
                        dve.wait_ge(turned, t - 1)
                    nc.vector.scalar_tensor_tensor(cq[0:r, t % 2, :], z(t)[0:r, 0:Q_LORA], ms[0:r, t, 2:3], gains[0:r, 0:Q_LORA], ALU.mult, ALU.mult)
                    nc.vector.scalar_tensor_tensor(ckv[0:r, t, :], z(t)[0:r, Q_LORA:Q_LORA + KV_LORA], ms[0:r, t, 3:4],
                                                   gains[0:r, Q_LORA:], ALU.mult, ALU.mult).then_inc(normed, 1)

                def copy_k(t):
                    r = ROWS[t]
                    at = NEW_AT if t == 4 else t * P
                    dve.wait_ge(turned, t + 1)
                    nc.vector.tensor_copy(m["ckvT"][:, :, at:at + r], tr(t)[:, BANK:BANK + JC * P].rearrange("p (j q) -> p j q", q=P)[:, :, 0:r])
                    for h in range(4):
                        last = nc.vector.tensor_copy(m["kh"][h // 2][h % 2][HD:QW, at:at + r], tr(t)[0:ROPE, BANK + 2 * P:BANK + 2 * P + r])
                    last.then_inc(turned_k, 1)

                for t in range(NT):
                    norm(t)
                    if t:
                        copy_k(t - 1)
                copy_k(NT - 1)


def expert_loads(k, sp, layer, slot, expert, gu_in, dn_in, gu, dn):
    at = bass.ds(expert, 1)
    sp.dma_start(gu[:, :, 0:EH], k.w_gate[layer, at].rearrange("a (j p) f -> p (a j) f", p=P)).then_inc(gu_in, 16)
    sp.dma_start(gu[:, :, EH:2 * EH], k.w_up[layer, at].rearrange("a (j p) f -> p (a j) f", p=P)).then_inc(gu_in, 16)
    sp.dma_start(dn[:], k.w_down[layer, at].rearrange("a (j p) d -> p (a j) d", p=P)).then_inc(dn_in, 16)


def prefetch_experts(k, sp, layer, slots):
    for n in slots:
        expert_loads(k, sp, layer, n, n, k.gu_in[layer][n], k.dn_in[layer][n], k.w_gu[n], k.w_dn[n])


def mix_out(k, tag, layer, w_out):
    nc = k.nc
    with ExitStack() as c:
        sb = lambda n, s, d=F32: c.enter_context(nc.sbuf_tensor(f"{tag}_{n}", s, d))
        sem = lambda n: new_signal(k, f"{tag}_{n}")
        w = sb("w", [P, J, D])
        g = sb("g", [P, D])
        b = sb("b", [P, D])
        wr = sb("wr", [P, J, GROUPS + NE])
        br = sb("br", [P, GROUPS + NE])
        stats = sb("stats", [P, 2, 2, 6])
        mv = sb("mv", [P, 2, 4])
        w_in, p_in, turned, mixT_act, mixT_dve, y_ready, y_read, steps_s, var_done, inv_done, centred, scaled, x_ready = (
            sem(n) for n in ("w_in p_in turned mixT_act mixT_dve y_ready y_read step var_done inv_done centred "
                             "scaled x_ready").split())
        xt_ready, xt_act, xt_dve, logit_mm, logit_done, out_sem = (sem(n) for n in "xt_ready xt_act xt_dve logit_mm logit_done out".split())
        n_p = 64 + (32 if layer == 0 else 0)
        tr = banks(k, 0, 2)
        y = lambda t: banks(k, 2 + 2 * (t % 2), 2)
        xtr = banks(k, 6, 1)
        lg = banks(k, 7, 1)

        with nc.Block() as block:

            @block.sync
            def _(sp):
                sp.dma_start(w[:], w_out.rearrange("(j p) n -> p j n", p=P)).then_inc(w_in, 16)
                if layer == 0:
                    sp.dma_start(k.x[:, 0:4, :], k.x_rows[0:SEQ, :].rearrange("(t p) d -> p t d", p=P)).then_inc(p_in, 16)
                    sp.dma_start(k.x[0:NEW, 4, :], k.x_rows[SEQ:T, :]).then_inc(p_in, 16)
                sp.dma_start(g[:], k.ln_g[layer, 0:1, :].to_broadcast([P, D])).then_inc(p_in, 16)
                sp.dma_start(b[:], k.ln_b[layer, 0:1, :].to_broadcast([P, D])).then_inc(p_in, 16)
                sp.dma_start(wr[:], k.w_r[layer]).then_inc(p_in, 16)
                sp.dma_start(br[:], k.b_r[layer:layer + 1, :].to_broadcast([P, GROUPS + NE])).then_inc(p_in, 16)
                if layer == 1:
                    prefetch_experts(k, sp, 1, [2])
                for t in range(NT):
                    sp.wait_ge(x_ready, t + 1)
                    sp.dma_start(k.x_d[t * P:t * P + ROWS[t], :], k.x[0:ROWS[t], t, :]).then_inc(out_sem, 16)
                sp.wait_ge(out_sem, 16 * NT)

            @block.tensor
            def _(pe):
                for t in range(NT):
                    if t:
                        pe.wait_ge(mixT_act, t)
                        pe.wait_ge(mixT_dve, t)
                    for j in range(J):
                        last = nc.tensor.transpose(tr[:, j * P:j * P + ROWS[t]], k.mix[0:ROWS[t], t, j * P:(j + 1) * P],
                                                   k.ident[0:ROWS[t], 0:ROWS[t]])
                    last.then_inc(turned, 1)
                pe.wait_ge(w_in, 16)
                pe.wait_ge(mixT_act, NT)
                pe.wait_ge(mixT_dve, NT)

                def out_proj(t):
                    if t >= 2:
                        pe.wait_ge(y_read, t - 1)
                    for h in range(2):
                        for j in range(J):
                            last = nc.tensor.matmul(y(t)[0:ROWS[t], h * BANK:(h + 1) * BANK], k.xT[:, j, t * P:t * P + ROWS[t]],
                                                    w[:, j, h * BANK:(h + 1) * BANK], start=(j == 0), stop=(j == J - 1))
                    last.then_inc(y_ready, 1)

                def turn_x(t):
                    pe.wait_ge(x_ready, t + 1)
                    for h in range(2):
                        if t or h:
                            pe.wait_ge(xt_act if h else xt_dve, t + h)
                        for j in range(4):
                            f = (4 * h + j) * P
                            last = nc.tensor.transpose(xtr[:, j * P:j * P + ROWS[t]], k.x[0:ROWS[t], t, f:f + P], k.ident[0:ROWS[t], 0:ROWS[t]])
                        last.then_inc(xt_ready, 1)
                    pe.wait_ge(xt_act, t + 1)
                    pe.wait_ge(xt_dve, t + 1)
                    pe.wait_ge(p_in, n_p)
                    if t:
                        pe.wait_ge(logit_done, t)
                    for j in range(J):
                        last = nc.tensor.matmul(lg[:, t * 64:t * 64 + GROUPS + NE], k.xT[:, j, t * P:(t + 1) * P], wr[:, j, :],
                                                start=(j == 0), stop=(j == J - 1))
                    last.then_inc(logit_mm, 1)

                for t in range(NT):
                    out_proj(t)
                    if t:
                        turn_x(t - 1)
                turn_x(NT - 1)

            @block.scalar
            def _(act):
                for t in range(NT):
                    r = ROWS[t]
                    act.wait_ge(turned, t + 1)
                    nc.scalar.activation(k.xT[:, 0:4, t * P:t * P + r], tr[:, 0:BANK].rearrange("p (j q) -> p j q", q=P)[:, :, 0:r],
                                         ACT.Copy).then_inc(mixT_act, 1)
                for t in range(NT):
                    r = ROWS[t]
                    act.wait_ge(xt_ready, 2 * t + 1)
                    act.wait_ge(y_ready, t + 1)
                    nc.scalar.activation(k.xT[:, 0:4, t * P:t * P + r], xtr.rearrange("p (j q) -> p j q", q=P)[:, :, 0:r],
                                         ACT.Copy).then_inc(xt_act, 1)

            @block.vector
            def _(dve):
                for t in range(NT):
                    r = ROWS[t]
                    dve.wait_ge(turned, t + 1)
                    nc.vector.tensor_copy(k.xT[:, 4:8, t * P:t * P + r], tr[:, BANK:2 * BANK].rearrange("p (j q) -> p j q", q=P)[:, :, 0:r]).then_inc(mixT_dve, 1)
                dve.wait_ge(p_in, n_p)
                steps = Steps(dve, steps_s)

                def rest(t):
                    r = ROWS[t]
                    dve.wait_ge(xt_ready, 2 * t + 2)
                    nc.vector.tensor_copy(k.xT[:, 4:8, t * P:t * P + r], xtr.rearrange("p (j q) -> p j q", q=P)[:, :, 0:r]).then_inc(xt_dve, 1)
                    dve.wait_ge(logit_mm, t + 1)
                    nc.vector.tensor_tensor(k.logits[:, t, :], lg[:, t * 64:t * 64 + GROUPS + NE], br[:], ALU.add).then_inc(logit_done, 1)

                for t in range(NT):
                    norm_tile(k, dve, steps, t, lambda t: y(t)[0:ROWS[t], :], y_ready, t + 1, y_read, stats, mv, var_done, inv_done, centred)
                    if t:
                        rest(t - 1)
                rest(NT - 1)

            @block.gpsimd
            def _(pool):
                pool.wait_ge(p_in, n_p)
                for t in range(NT):
                    norm_tail(k, pool, t, g, b, mv, var_done, inv_done, centred, scaled, x_ready)


def norm_tile(k, dve, steps, t, y, y_sem, y_count, y_read, stats, mv, var_done, inv_done, centred):
    nc = k.nc
    r = ROWS[t]
    x = k.x[0:r, t, :]
    dve.wait_ge(y_sem, y_count)
    steps.then(nc.vector.scalar_tensor_tensor(x, x, ALPHA, y(t), ALU.mult, ALU.add))
    for h in range(2):
        last = nc.vector.bn_stats(stats[0:r, t % 2, h, :], x[:, h * BANK:(h + 1) * BANK])
        if y_read is not None and h == 0:
            last.then_inc(y_read, 1)
    steps.then(last)
    steps.then(nc.vector.bn_aggr(mv[0:r, t % 2, 0:2], stats[0:r, t % 2, :, :].rearrange("p a b -> p (a b)")))
    nc.vector.tensor_scalar(mv[0:r, t % 2, 2:3], mv[0:r, t % 2, 1:2], LN_EPS, None, ALU.add).then_inc(var_done, 1)
    dve.wait_ge(inv_done, t + 1)
    nc.vector.tensor_scalar(x, x, mv[0:r, t % 2, 0:1], mv[0:r, t % 2, 3:4], ALU.subtract, ALU.mult).then_inc(centred, 1)


def norm_tail(k, pool, t, g, b, mv, var_done, inv_done, centred, scaled, x_ready):
    r = ROWS[t]
    pool.wait_ge(var_done, t + 1)
    pool.tensor_tensor(mv[0:r, t % 2, 3:4], mv[0:r, t % 2, 2:3], k.half[0:r, :], ALU.pow).then_inc(inv_done, 1)
    pool.wait_ge(centred, t + 1)
    pool.tensor_tensor(k.x[0:r, t, :], k.x[0:r, t, :], g[0:r, :], ALU.mult).then_inc(scaled, 1)
    pool.wait_ge(scaled, t + 1)
    pool.tensor_tensor(k.x[0:r, t, :], k.x[0:r, t, :], b[0:r, :], ALU.add).then_inc(x_ready, 1)


def route(k, tag, layer, r):
    nc = k.nc
    NX = NB_TAB - NE
    with ExitStack() as c:
        sb = lambda n, s, d=F32: c.enter_context(nc.sbuf_tensor(f"{tag}_{n}", s, d))
        sem = lambda n: new_signal(k, f"{tag}_{n}")
        glog = sb("glog", [P, NT, 8])
        top_g = sb("top_g", [P, NT, 8])
        idx_g = sb("idx_g", [P, NT, 8], U32)
        neg_g = sb("neg_g", [P, NT])
        exp_g = sb("exp_g", [P, NT, GROUPS])
        gate = sb("gate", [P, NT])
        g_of = sb("g_of", [P, NT])
        pen = sb("pen", [P, NT, GROUPS])
        elog = sb("elog", [P, NT, NE])
        top_e = sb("top_e", [P, NT, 8])
        idx_e = sb("idx_e", [P, NT, 8], U32)
        gap = sb("gap", [P, NT])
        e_gap = sb("e_gap", [P, NT])
        den = sb("den", [P, NT])
        e_of = sb("e_of", [P, 2, NT])
        hot = sb("hot", [P, 2, NT, NE])
        both = sb("both", [P, NT, NE])
        work = sb("work", [P, 2, NT, NE])
        rank = sb("rank", [P, 2, NT])
        over = sb("over", [P, 2, NT])
        base = sb("base", [P, 2, NT])
        flag = sb("flag", [P, 2, NT])
        block_of = sb("block_of", [P, 2, NT])
        place = sb("place", [P, 2, NT])
        count = sb("count", [P, NE])
        extra = sb("extra", [P, NE])
        xend = sb("xend", [P, NE])
        xbase = sb("xbase", [P, NE])
        tri = sb("tri", [P, P])
        ones = sb("ones", [P, P])
        valid = sb("valid", [P, NT])
        slot_id = sb("slot_id", [P, 2, NT])
        iota_i = sb("iota_i", [P, P], I32)
        iota = sb("iota", [P, P])
        id_i = sb("id_i", [P, 2, NT], I32)
        hot_p = sb("hot_p", [P, 2, NT, CB])
        hot_b = sb("hot_b", [P, 2, NT, NB_TAB])
        lst = sb("lst", [CB, NB_TAB])
        far = sb("far", [CB, NB_TAB])
        tok = sb("tok", [CB, NB_TAB])
        tab_a = sb("tab_a", [1, NX, NE])
        tab_b = sb("tab_b", [1, NX, NE])
        tab_f = sb("tab_f", [1, NB_TAB])
        trip = sb("trip", [1, 4])
        steps_s, filled, consts, gmax_done, gexp_done, gap_done, egap_done, hot_done, ranked, listed, lists_ready = (
            sem(n) for n in "step filled consts gmax_done gexp_done gap_done egap_done hot_done ranked listed lists".split())
        cum = banks(k, 0, 1)
        tot = banks(k, 1, 1)
        lps = banks(k, 2, 1)

        with nc.Block() as block:

            @block.gpsimd
            def _(pool):
                n = 0

                def step(ins):
                    nonlocal n
                    n += 1
                    ins.then_inc(filled, 1)
                    pool.wait_ge(filled, n)
                step(pool.memset(tri[:], 1.0))
                step(pool.affine_select(out=tri[:], in_=tri[:], compare_op=ALU.is_gt, fill=0.0, base=0, pattern=[[1, P]], channel_multiplier=-1))
                step(pool.memset(ones[:], 1.0))
                step(pool.memset(valid[:], 1.0))
                step(pool.memset(valid[NEW:P, 4:5], 0.0))
                step(pool.iota(iota_i[:], [[1, P]], base=0, channel_multiplier=0))
                step(pool.tensor_copy(iota[:], iota_i[:]))
                step(pool.iota(id_i[:], [[T, 2], [P, NT]], base=1, channel_multiplier=1))
                step(pool.tensor_copy(slot_id[:], id_i[:]))
                step(pool.memset(slot_id[NEW:P, :, 4], 0.0))
                step(pool.memset(glog[:], -3e38))
                pool.sem_inc(consts, 1)

            @block.scalar
            def _(act):
                act.wait_ge(gmax_done, 1)
                for t in range(NT):
                    last = nc.scalar.activation(exp_g[:, t, :], glog[:, t, 0:GROUPS], ACT.Exp, bias=neg_g[:, t:t + 1], accum_out=gate[:, t:t + 1])
                last.then_inc(gexp_done, 1)
                act.wait_ge(gap_done, 1)
                nc.scalar.activation(e_gap[:], gap[:], ACT.Exp).then_inc(egap_done, 1)

            @block.tensor
            def _(pe):
                pe.wait_ge(hot_done, 1)
                for t in range(NT):
                    for a in range(t):
                        nc.tensor.matmul(cum[:, t * NE:(t + 1) * NE], ones[:], both[:, a, :], start=(a == 0), stop=False)
                    nc.tensor.matmul(cum[:, t * NE:(t + 1) * NE], tri[:], both[:, t, :], start=(t == 0), stop=True)
                for t in range(NT):
                    last = nc.tensor.matmul(tot[:, 0:NE], ones[:], both[:, t, :], start=(t == 0), stop=(t == NT - 1))
                last.then_inc(ranked, 1)
                pe.wait_ge(listed, 1)
                for n in range(2 * NT):
                    c_, t = n // NT, n % NT
                    last = nc.tensor.matmul(lps[0:CB, 0:NB_TAB], hot_p[:, c_, t, :], hot_b[:, c_, t, :], start=(n == 0), stop=(n == 2 * NT - 1))
                last.then_inc(lists_ready, 1)

            @block.vector
            def _(dve):
                v = nc.vector
                steps = Steps(dve, steps_s)
                dve.wait_ge(consts, 1)
                steps.then(v.tensor_copy(glog[:, :, 0:GROUPS], k.logits[:, :, 0:GROUPS]))
                for t in range(NT):
                    last = v.max(top_g[:, t, :], glog[:, t, :])
                steps.then(last)
                v.tensor_scalar(neg_g[:], top_g[:, :, 0], -1.0, None, ALU.mult).then_inc(gmax_done, 1)
                for t in range(NT):
                    last = v.max_index(idx_g[:, t, :], top_g[:, t, :], glog[:, t, :])
                steps.then(last)
                steps.then(v.tensor_copy(g_of[:], idx_g[:, :, 0]))
                steps.then(v.tensor_tensor(pen[:], iota[:, 0:GROUPS].unsqueeze(1).to_broadcast([P, NT, GROUPS]),
                                           g_of[:].unsqueeze(2).to_broadcast([P, NT, GROUPS]), ALU.is_equal))
                steps.then(v.tensor_scalar(pen[:], pen[:], 1e30, -1e30, ALU.mult, ALU.add))
                for t in range(NT):
                    last = v.tensor_tensor(elog[:, t, :].rearrange("p (g e) -> p g e", e=PER_GROUP),
                                           k.logits[:, t, GROUPS:].rearrange("p (g e) -> p g e", e=PER_GROUP),
                                           pen[:, t, :].unsqueeze(2).to_broadcast([P, GROUPS, PER_GROUP]), ALU.add)
                steps.then(last)
                for t in range(NT):
                    last = v.max(top_e[:, t, :], elog[:, t, :])
                steps.then(last)
                v.tensor_tensor(gap[:], top_e[:, :, 1], top_e[:, :, 0], ALU.subtract).then_inc(gap_done, 1)
                for t in range(NT):
                    last = v.max_index(idx_e[:, t, :], top_e[:, t, :], elog[:, t, :])
                steps.then(last)
                for c_ in range(2):
                    last = v.tensor_copy(e_of[:, c_, :], idx_e[:, :, c_])
                steps.then(last)
                for c_ in range(2):
                    last = v.tensor_tensor(hot[:, c_], iota[:, 0:NE].unsqueeze(1).to_broadcast([P, NT, NE]),
                                           e_of[:, c_, :].unsqueeze(2).to_broadcast([P, NT, NE]), ALU.is_equal)
                steps.then(last)
                for c_ in range(2):
                    last = v.tensor_tensor(hot[:, c_], hot[:, c_], valid[:].unsqueeze(2).to_broadcast([P, NT, NE]), ALU.mult)
                steps.then(last)
                v.tensor_tensor(both[:], hot[:, 0], hot[:, 1], ALU.add).then_inc(hot_done, 1)
                dve.wait_ge(gexp_done, 1)
                dve.wait_ge(egap_done, 1)
                v.tensor_scalar(den[:], e_gap[:], 1.0, None, ALU.add)
                steps.then(v.reciprocal(gate[:], gate[:]))
                steps.then(v.reciprocal(den[:], den[:]))
                steps.then(v.tensor_tensor(r["weight"][:, 0, :], gate[:], den[:], ALU.mult))
                v.tensor_tensor(r["weight"][:, 1, :], r["weight"][:, 0, :], e_gap[:], ALU.mult)
                dve.wait_ge(ranked, 1)
                steps.then(v.tensor_copy(count[:], tot[:, 0:NE]))
                steps.then(v.tensor_scalar(extra[:], count[:], float(CB), None, ALU.is_gt))
                for n in range(2, -(-T // CB)):
                    steps.then(v.tensor_scalar(xbase[:], count[:], float(n * CB), None, ALU.is_gt))
                    steps.then(v.tensor_tensor(extra[:], extra[:], xbase[:], ALU.add))
                steps.then(v.tensor_tensor_scan(xend[:], ones[:, 0:NE], extra[:], float(NE), ALU.mult, ALU.add))
                steps.then(v.tensor_tensor(xbase[:], xend[:], extra[:], ALU.subtract))
                for src, dst in ((cum[:, 0:NT * NE].rearrange("p (t e) -> p t e", e=NE), rank),
                                 (xbase[:].unsqueeze(1).to_broadcast([P, NT, NE]), base)):
                    for c_ in range(2):
                        last = v.tensor_tensor(work[:, c_], hot[:, c_], src, ALU.mult)
                    steps.then(last)
                    steps.then(v.tensor_reduce(dst[:], work[:], AX_X, ALU.add))
                steps.then(v.tensor_scalar(over[:], rank[:], float(CB), None, ALU.is_ge))
                for n in range(2, -(-T // CB)):
                    steps.then(v.tensor_scalar(flag[:], rank[:], float(n * CB), None, ALU.is_ge))
                    steps.then(v.tensor_tensor(over[:], over[:], flag[:], ALU.add))
                steps.then(v.tensor_tensor(block_of[:], base[:], over[:], ALU.add))
                steps.then(v.tensor_tensor(block_of[:], block_of[:], e_of[:], ALU.subtract))
                steps.then(v.tensor_scalar(flag[:], over[:], 1.0, None, ALU.is_ge))
                steps.then(v.scalar_tensor_tensor(block_of[:], block_of[:], -1.0, flag[:], ALU.add, ALU.mult))
                steps.then(v.tensor_tensor(block_of[:], block_of[:], e_of[:], ALU.add))
                steps.then(v.scalar_tensor_tensor(place[:], over[:], -float(CB), rank[:], ALU.mult, ALU.add))
                for c_ in range(2):
                    v.tensor_tensor(hot_p[:, c_], iota[:, 0:CB].unsqueeze(1).to_broadcast([P, NT, CB]),
                                    place[:, c_, :].unsqueeze(2).to_broadcast([P, NT, CB]), ALU.is_equal)
                    last = v.tensor_tensor(hot_b[:, c_], iota[:, 0:NB_TAB].unsqueeze(1).to_broadcast([P, NT, NB_TAB]),
                                           block_of[:, c_, :].unsqueeze(2).to_broadcast([P, NT, NB_TAB]), ALU.is_equal)
                steps.then(last)
                for c_ in range(2):
                    last = v.tensor_tensor(hot_b[:, c_], hot_b[:, c_], slot_id[:, c_, :].unsqueeze(2).to_broadcast([P, NT, NB_TAB]), ALU.mult)
                last.then_inc(listed, 1)
                nx = iota[0:1, NE:NE + NX].unsqueeze(2).to_broadcast([1, NX, NE])
                v.tensor_tensor(tab_a[:], nx, xbase[0:1, :].unsqueeze(1).to_broadcast([1, NX, NE]), ALU.is_ge)
                steps.then(v.tensor_tensor(tab_b[:], nx, xend[0:1, :].unsqueeze(1).to_broadcast([1, NX, NE]), ALU.is_lt))
                steps.then(v.tensor_tensor(tab_a[:], tab_a[:], tab_b[:], ALU.mult))
                steps.then(v.tensor_tensor(tab_a[:], tab_a[:], iota[0:1, 0:NE].unsqueeze(1).to_broadcast([1, NX, NE]), ALU.mult))
                v.tensor_copy(tab_f[:, 0:NE], iota[0:1, 0:NE])
                steps.then(v.tensor_reduce(tab_f[:, NE:NB_TAB], tab_a[:], AX_X, ALU.add))
                steps.then(v.tensor_copy(r["expert"][:], tab_f[:]))
                steps.then(v.tensor_scalar(trip[:, 0:1], xend[0:1, NE - 1:NE], float(NE), None, ALU.is_gt))
                for n in range(1, (NB_TAB - NE) // RING):
                    steps.then(v.tensor_scalar(trip[:, 1:2], xend[0:1, NE - 1:NE], float(NE + n * RING), None, ALU.is_gt))
                    steps.then(v.tensor_tensor(trip[:, 0:1], trip[:, 0:1], trip[:, 1:2], ALU.add))
                steps.then(v.tensor_scalar(trip[:, 2:3], trip[:, 0:1], float(NE // RING), None, ALU.add))
                steps.then(v.tensor_copy(r["trips"][:], trip[:, 2:3]))
                dve.wait_ge(lists_ready, 1)
                steps.then(v.tensor_scalar(lst[:], lps[0:CB, 0:NB_TAB], -1.0, None, ALU.add))
                v.tensor_scalar(far[:], lst[:], 0.0, FAR, ALU.is_lt, ALU.mult)
                steps.then(v.tensor_scalar(tok[:], lst[:], float(T), -float(T), ALU.is_ge, ALU.mult))
                steps.then(v.tensor_tensor(lst[:], lst[:], far[:], ALU.add))
                v.tensor_copy(r["slots"][:], lst[:])
                steps.then(v.tensor_tensor(tok[:], tok[:], lst[:], ALU.add))
                steps.then(v.tensor_copy(r["tokens"][:], tok[:]))


def experts(k, tag, layer, r):
    nc, passed = k.nc, k.passed
    first_trips = NE // RING
    with ExitStack() as c:
        sb = lambda n, s, d=F32: c.enter_context(nc.sbuf_tensor(f"{tag}_{n}", s, d))
        sem = lambda n: new_signal(k, f"{tag}_{n}")
        w_gu = [*k.w_gu, sb("w_gu3", [P, J, 2 * EH])]
        w_dn = [*k.w_dn, sb("w_dn3", [P, JE, D])]
        x_idx = [sb(f"x_idx{n}", [CB, 1], I32) for n in range(RING)]
        y_idx = [sb(f"y_idx{n}", [CB, 1], I32) for n in range(RING)]
        xg = [sb(f"xg{n}", [CB, D]) for n in range(RING)]
        xgT = sb("xgT", [P, 2, J, CB])
        silu = sb("silu", [CB, 2, EH])
        hid = sb("hid", [CB, 2, EH])
        hidT = sb("hidT", [P, 2, JE, CB])
        yo = [sb(f"yo{n}", [CB, D]) for n in range(RING)]
        gu_in, dn_in = k.gu_in[layer], k.dn_in[layer]
        x_in = [sem(f"x_in{n}") for n in range(RING)]
        y_out = [sem(f"y_out{n}") for n in range(RING)]
        zeroed, x_turned, xgT_ready, gu_ready, silu_ready, hid_ready, hid_turned, hidT_ready, y_ready, y_act, y_dve, xi_done, yi_done = (
            sem(n) for n in ("zeroed x_turned xgT_ready gu_ready silu_ready hid_ready hid_turned hidT_ready y_ready "
                             "y_act y_dve xi_done yi_done").split())
        gu = lambda b: banks(k, b % 2, 1)
        y = lambda b: banks(k, 2 + b % 2, 1)
        xtr = lambda b: banks(k, 4 + b % 2, 1)
        htr = lambda b: banks(k, 6 + b % 2, 1)

        def trips(eng):
            return eng.value_load(r["trips"][0:1, 0:1], min_val=first_trips, max_val=NB_TAB // RING - 1)

        with nc.Block() as block:

            @block.sync
            def _(sp):
                n_trips = trips(sp)
                s = RING - 1
                expert_loads(k, sp, layer, s, s, gu_in[s], dn_in[s], w_gu[s], w_dn[s])
                with sp.Fori(0, n_trips - 1) as i:
                    for s in range(RING):
                        hold(sp, passed, (y_ready, RING * i + s + 1))
                        expert = sp.value_load(r["expert"][0:1, bass.ds(RING * (i + 1) + s, 1)], min_val=0, max_val=NE - 1)
                        expert_loads(k, sp, layer, s, expert, gu_in[s], dn_in[s], w_gu[s], w_dn[s])

            @block.gpsimd
            def _(pool):
                n_trips = trips(pool)
                for s in range(RING):
                    pool.memset(xg[s][:], 0.0).then_inc(zeroed, 1)
                pool.wait_ge(zeroed, RING)

                def gather(i, s):
                    if isinstance(i, int):
                        assert i == 0
                    else:
                        hold(pool, passed, (x_turned, RING * (i - 1) + s + 1))
                    pool.tensor_copy(x_idx[s][:], r["tokens"][:, bass.ds(RING * i + s, 1)]).then_inc(xi_done, 1)
                    hold(pool, passed, (xi_done, RING * i + s + 1))
                    pool.indirect_dma_start(out=xg[s][:], out_offset=None, in_=k.x_d[:, :],
                                            in_offset=bass.IndirectOffsetOnAxis(ap=x_idx[s][:, 0:1], axis=0),
                                            bounds_check=T - 1, oob_is_err=False).then_inc(x_in[s], 16)

                def scatter(i, s):
                    hold(pool, passed, (y_act, RING * i + s + 1), (y_dve, RING * i + s + 1), (y_out[s], 16 * i))
                    pool.tensor_copy(y_idx[s][:], r["slots"][:, bass.ds(RING * i + s, 1)]).then_inc(yi_done, 1)
                    hold(pool, passed, (yi_done, RING * i + s + 1))
                    pool.indirect_dma_start(out=k.y_d[:, :], out_offset=bass.IndirectOffsetOnAxis(ap=y_idx[s][:, 0:1], axis=0),
                                            in_=yo[s][:], in_offset=None, bounds_check=2 * T - 1, oob_is_err=False).then_inc(y_out[s], 16)

                for s in range(RING):
                    gather(0, s)
                with pool.Fori(0, n_trips) as i:
                    for s in range(RING):
                        gather(i + 1, s)
                        scatter(i, s)
                for s in range(RING):
                    hold(pool, passed, (y_out[s], 16 * n_trips), (x_in[s], 16 * (n_trips + 1)))

            @block.tensor
            def _(pe):
                n_trips = trips(pe)

                def turn_x(i, s):
                    b = RING * i + s
                    hold(pe, passed, (x_in[s], 16 * (i + 1)), *([(xgT_ready, b - 1)] if s >= 2 else [(y_act, RING * i), (y_dve, RING * i)]))
                    for j in range(J):
                        last = nc.tensor.transpose(xtr(s)[:, j * CB:(j + 1) * CB], xg[s][:, j * P:(j + 1) * P], k.ident[0:CB, 0:CB])
                    last.then_inc(x_turned, 1)

                def up(i, s):
                    b = RING * i + s
                    hold(pe, passed, (gu_in[s], 32 * (i + 1)), (xgT_ready, b + 1), *[(hid_ready, b - 1)] * (s >= 2))
                    for j in range(J):
                        for h in range(2):
                            last = nc.tensor.matmul(gu(s)[h * CB:(h + 1) * CB, 0:EH], xgT[:, s % 2, j, :], w_gu[s][:, j, h * EH:(h + 1) * EH],
                                                    start=(j == 0), stop=(j == J - 1))
                    last.then_inc(gu_ready, 1)

                def down(i, s):
                    b = RING * i + s
                    hold(pe, passed, (hid_ready, b + 1), *[(hidT_ready, b - 1)] * (s >= 2))
                    for j in range(JE):
                        last = nc.tensor.transpose(htr(s)[:, j * CB:(j + 1) * CB], hid[:, s % 2, j * P:(j + 1) * P], k.ident[0:CB, 0:CB])
                    last.then_inc(hid_turned, 1)
                    hold(pe, passed, (dn_in[s], 16 * (i + 1)), (hidT_ready, b + 1), *[(y_act, b - 1), (y_dve, b - 1)] * (s >= 2))
                    for j in range(JE):
                        for h in range(2):
                            last = nc.tensor.matmul(y(s)[h * CB:(h + 1) * CB, :], hidT[:, s % 2, j, :], w_dn[s][:, j, h * BANK:(h + 1) * BANK],
                                                    start=(j == 0), stop=(j == JE - 1))
                    last.then_inc(y_ready, 1)

                with pe.Fori(0, n_trips) as i:
                    turn_x(i, 0)
                    for s in range(RING):
                        up(i, s)
                        if s + 1 < RING:
                            turn_x(i, s + 1)
                        if s:
                            down(i, s - 1)
                    down(i, RING - 1)

            @block.scalar
            def _(act):
                n_trips = trips(act)
                nc.scalar.preload_act_table(ACT.Silu)

                def gate(i, s):
                    b = RING * i + s
                    hold(act, passed, (gu_ready, b + 1), (hid_ready, b - 1 if s >= 2 else RING * i))
                    nc.scalar.activation(silu[:, s % 2, :], gu(s)[0:CB, 0:EH], ACT.Silu).then_inc(silu_ready, 1)

                def out(i, s):
                    hold(act, passed, (y_ready, RING * i + s + 1), (y_out[s], 16 * i))
                    nc.scalar.activation(yo[s][:, 0:BANK], y(s)[0:CB, :], ACT.Copy).then_inc(y_act, 1)

                with act.Fori(0, n_trips) as i:
                    for s in range(RING):
                        gate(i, s)
                        if s:
                            out(i, s - 1)
                    out(i, RING - 1)

            @block.vector
            def _(dve):
                n_trips = trips(dve)

                def copy_x(i, s):
                    b = RING * i + s
                    hold(dve, passed, (x_turned, b + 1), (gu_ready, b - 1 if s >= 2 else RING * i))
                    nc.vector.tensor_copy(xgT[:, s % 2, :, :].rearrange("p j q -> p (j q)"), xtr(s)).then_inc(xgT_ready, 1)

                def hidden(i, s):
                    b = RING * i + s
                    hold(dve, passed, (silu_ready, b + 1), (hid_turned, b - 1 if s >= 2 else RING * i))
                    nc.vector.tensor_tensor(hid[:, s % 2, :], silu[:, s % 2, :], gu(s)[CB:P, 0:EH], ALU.mult).then_inc(hid_ready, 1)

                def copy_h(i, s):
                    b = RING * i + s
                    hold(dve, passed, (hid_turned, b + 1), (y_ready, b - 1 if s >= 2 else RING * i))
                    nc.vector.tensor_copy(hidT[:, s % 2, :, :].rearrange("p j q -> p (j q)"), htr(s)[:, 0:JE * CB]).then_inc(hidT_ready, 1)

                def out(i, s):
                    hold(dve, passed, (y_ready, RING * i + s + 1), (y_out[s], 16 * i))
                    nc.vector.tensor_copy(yo[s][:, BANK:D], y(s)[CB:P, :]).then_inc(y_dve, 1)

                with dve.Fori(0, n_trips) as i:
                    copy_x(i, 0)
                    for s in range(RING):
                        if s + 1 < RING:
                            copy_x(i, s + 1)
                        hidden(i, s)
                        if s:
                            copy_h(i, s - 1)
                            out(i, s - 1)
                    copy_h(i, RING - 1)
                    out(i, RING - 1)


def combine(k, tag, layer, r, last_layer):
    nc = k.nc
    with ExitStack() as c:
        sb = lambda n, s, d=F32: c.enter_context(nc.sbuf_tensor(f"{tag}_{n}", s, d))
        sem = lambda n: new_signal(k, f"{tag}_{n}")
        g = sb("g", [P, D])
        b = sb("b", [P, D])
        ys = sb("ys", [P, 2, 2, D])
        stats = sb("stats", [P, 2, 2, 6])
        mv = sb("mv", [P, 2, 4])
        y_in = [sem("y_in0"), sem("y_in1")]
        p_in, steps_s, y_sum, y_used, var_done, inv_done, centred, scaled, x_ready, xt_ready, xt_act, xt_dve, out_sem = (
            sem(n) for n in "p_in step y_sum y_used var_done inv_done centred scaled x_ready xt_ready xt_act xt_dve out".split())
        tr = lambda t: banks(k, 2 * (t % 2), 2)

        with nc.Block() as block:

            @block.sync
            def _(sp):
                sp.dma_start(g[:], k.ln_g[layer, 1:2, :].to_broadcast([P, D])).then_inc(p_in, 16)
                sp.dma_start(b[:], k.ln_b[layer, 1:2, :].to_broadcast([P, D])).then_inc(p_in, 16)

                def out(t):
                    sp.wait_ge(x_ready, t + 1)
                    dst = k.o_y_p[0, t * P:(t + 1) * P, :] if t < 4 else k.o_y_s[0, :, :]
                    sp.dma_start(dst, k.x[0:ROWS[t], t, :]).then_inc(out_sem, 16)

                for t in range(NT):
                    if t >= 2:
                        sp.wait_ge(y_used, t - 1)
                    for c_ in range(2):
                        at = c_ * T + t * P
                        sp.dma_start(ys[0:ROWS[t], t % 2, c_, :], k.y_d[at:at + ROWS[t], :]).then_inc(y_in[t % 2], 16)
                    if last_layer and t >= 2:
                        out(t - 2)
                if not last_layer:
                    prefetch_experts(k, sp, layer + 1, range(2))
                if last_layer:
                    out(3)
                    out(4)
                    sp.wait_ge(out_sem, 16 * NT)

            def half_out(dve, t):
                dve.wait_ge(xt_ready, t + 1)
                nc.vector.tensor_copy(k.xT[:, 4:8, t * P:t * P + ROWS[t]],
                                      tr(t)[:, BANK:].rearrange("p (j q) -> p j q", q=P)[:, :, 0:ROWS[t]]).then_inc(xt_dve, 1)

            @block.vector
            def _(dve):
                steps = Steps(dve, steps_s)
                dve.wait_ge(p_in, 32)
                for t in range(NT):
                    rr = ROWS[t]
                    dve.wait_ge(y_in[t % 2], 32 * (t // 2 + 1))
                    y0, y1 = ys[0:rr, t % 2, 0, :], ys[0:rr, t % 2, 1, :]
                    steps.then(nc.vector.tensor_scalar(y0, y0, r["weight"][0:rr, 0, t:t + 1], None, ALU.mult))
                    nc.vector.scalar_tensor_tensor(y0, y1, r["weight"][0:rr, 1, t:t + 1], y0, ALU.mult, ALU.add).then_inc(y_sum, 1)
                    norm_tile(k, dve, steps, t, lambda t: ys[0:ROWS[t], t % 2, 0, :], y_sum, t + 1, y_used, stats, mv, var_done, inv_done, centred)
                    if not last_layer and t:
                        half_out(dve, t - 1)
                if not last_layer:
                    half_out(dve, NT - 1)

            @block.gpsimd
            def _(pool):
                pool.wait_ge(p_in, 32)
                for t in range(NT):
                    norm_tail(k, pool, t, g, b, mv, var_done, inv_done, centred, scaled, x_ready)

            if not last_layer:

                @block.tensor
                def _(pe):
                    for t in range(NT):
                        pe.wait_ge(x_ready, t + 1)
                        if t >= 2:
                            pe.wait_ge(xt_act, t - 1)
                            pe.wait_ge(xt_dve, t - 1)
                        for j in range(J):
                            last = nc.tensor.transpose(tr(t)[:, j * P:j * P + ROWS[t]], k.x[0:ROWS[t], t, j * P:(j + 1) * P], k.ident[0:ROWS[t], 0:ROWS[t]])
                        last.then_inc(xt_ready, 1)

                @block.scalar
                def _(act):
                    for t in range(NT):
                        act.wait_ge(xt_ready, t + 1)
                        nc.scalar.activation(k.xT[:, 0:4, t * P:t * P + ROWS[t]],
                                             tr(t)[:, 0:BANK].rearrange("p (j q) -> p j q", q=P)[:, :, 0:ROWS[t]], ACT.Copy).then_inc(xt_act, 1)


def mixture(k, tag, layer, last_layer):
    with ExitStack() as c:
        sb = lambda n, s, d=F32: c.enter_context(k.nc.sbuf_tensor(f"{tag}_{n}", s, d))
        r = {"weight": sb("weight", [P, 2, NT]), "expert": sb("expert", [1, NB_TAB], I32), "trips": sb("trips", [1, 1], I32),
             "slots": sb("slots", [CB, NB_TAB], I32), "tokens": sb("tokens", [CB, NB_TAB], I32)}
        route(k, tag + "_route", layer, r)
        experts(k, tag + "_experts", layer, r)
        combine(k, tag + "_combine", layer, r, last_layer)


def stream_step(nc, dram):
    with ExitStack() as ctx:
        k = Core(nc, ctx, dram)
        setup_and_gates(k)
        attend(k, False, None)
        mix_out(k, "mix0", 0, k.ab_w_out)
        clear_signals(k)
        mixture(k, "moe0", 0, False)
        clear_signals(k)
        with ExitStack() as c:
            sb = lambda n, s, d=F32: c.enter_context(nc.sbuf_tensor(f"mla_{n}", s, d))
            cqT = k.w_dn[2][:].rearrange("p j d -> p (j d)")[:, 0:JQ * TP].rearrange("p (j t) -> p j t", j=JQ)
            m = {"cqT": cqT, "ckvT": sb("ckvT", [P, JC, KEYS]),
                 "kh": [[sb(f"kh{a}{h}", [QW, KEYS]) for h in range(2)] for a in range(2)], "mask": sb("mask", [P, 704]),
                 "mask_width": [704, 704, 704, 704, T], "cos": sb("cos", [P, NT, ROPE // 2]), "sin": sb("sin", [P, NT, ROPE // 2])}
            mla_latents(k, m)
            attend(k, True, m)
        mix_out(k, "mix1", 1, k.mla_w_out)
        clear_signals(k)
        mixture(k, "moe1", 1, True)
        clear_signals(k)


_OUTS = [
    ("o_y_p", (1, SEQ, D)), ("o_y_s", (1, NEW, D)),
    ("o_fk_p", (1, 1, SEQ, HEADS, HD)), ("o_fv_p", (1, 1, SEQ, HEADS, HD)), ("o_logf_p", (1, 1, SEQ, HEADS)),
    ("o_sk_p", (1, 1, SEQ, HEADS, HD)), ("o_sv_p", (1, 1, SEQ, HEADS, HD)),
    ("o_ckv_p", (1, 1, SEQ, KV_LORA)), ("o_kr_p", (1, 1, SEQ, ROPE)),
    ("o_fk_s", (1, 1, NEW, HEADS, HD)), ("o_fv_s", (1, 1, NEW, HEADS, HD)), ("o_logf_s", (1, 1, NEW, HEADS)),
    ("o_sk_s", (1, 1, NEW, HEADS, HD)), ("o_sv_s", (1, 1, NEW, HEADS, HD)),
    ("o_ckv_s", (1, 1, NEW, KV_LORA)), ("o_kr_s", (1, 1, NEW, ROPE)),
]


def _laid_out(np, a):
    def by_feature(w):
        return w.reshape(w.shape[0] // P, P, -1).transpose(1, 0, 2)

    x_rows = np.concatenate([a["x_prompt"][0], a["x_sample"][0]])
    w_in = a["ab_w_in"][0]
    W = HEADS * HD
    starts = [0, W, 2 * W, 3 * W + HEADS, 4 * W + HEADS, 5 * W + HEADS]
    tiles = [by_feature(w_in[:, starts[3 * side + n] + p * P:starts[3 * side + n] + (p + 1) * P]).reshape(P, J * P)
             for side in range(2) for p in range(4) for n in range(3)]
    heads_t = lambda c: c[0, 0].reshape(PAST, 4, P).transpose(1, 2, 0)
    heads_v = lambda c: c[0, 0].reshape(4, P, 4, P).transpose(2, 1, 0, 3).reshape(4, P, 4 * P)
    w_uq = a["mla_w_uq"][0].reshape(JQ, P, 8, 2 * QW).transpose(2, 1, 0, 3).reshape(8, P, JQ * 2 * QW)
    ukv = a["mla_w_ukv"][0].reshape(JC, P, 8, 2, 2, HD)
    ukv = ukv.transpose(2, 1, 0, 4, 3, 5).reshape(8, P, JC * 2 * P)
    w_r = np.stack([by_feature(np.concatenate([a["moe_w_group"][l]] + [a["moe_w_router"][l, g] for g in range(GROUPS)], axis=1))
                    for l in range(2)])
    b_r = np.concatenate([a["moe_b_group"], a["moe_b_router"].reshape(2, NE)], axis=1)
    half = ROPE // 2
    freq = np.float32(10000.0) ** (-np.arange(half, dtype=np.float32) / np.float32(half))
    pos = np.concatenate([np.arange(SEQ), PAST + np.arange(NEW), np.zeros(TP - T)]).astype(np.float32)
    ang = pos[:, None] * freq[None, :].astype(np.float32)
    table = lambda f: f(ang).astype(np.float32).reshape(NT, P, half).transpose(1, 0, 2)
    return {
        "x_rows": x_rows, "x_t": by_feature(x_rows.T), "w_ab": np.stack(tiles),
        "w_f": by_feature(w_in[:, 3 * W:3 * W + HEADS]), "b_f": a["ab_b_forget"][0][:, None],
        "logf_past": a["cache_fox_logf"][0, 0].T,
        "k_past": np.concatenate([heads_t(a["cache_fox_k"]), heads_t(a["cache_sb_k"])]),
        "v_past": np.concatenate([heads_v(a["cache_fox_v"]), heads_v(a["cache_sb_v"])]),
        "ab_w_out": a["ab_w_out"][0], "mla_w_out": a["mla_w_out"][0], "w_mla_down": a["mla_w_down"][0],
        "g_q": a["mla_g_q"], "g_kv": a["mla_g_kv"], "w_uq": w_uq, "w_ukv": ukv,
        "ckv_past": by_feature(a["cache_mla_ckv"][0, 0].T), "kr_past": a["cache_mla_krope"][0, 0].T,
        "cos": table(np.cos), "sin": table(np.sin), "w_r": w_r, "b_r": b_r,
        "w_gate": a["moe_w_gate"].reshape(2, NE, D, EH), "w_up": a["moe_w_up"].reshape(2, NE, D, EH),
        "w_down": a["moe_w_down"].reshape(2, NE, EH, D), "ln_g": a["ln_g"], "ln_b": a["ln_b"],
    }


def kernel(**inputs):
    import numpy as np
    import concourse.bacc as bacc
    from concourse.bass_utils import run_bass_kernel_spmd

    nc = bacc.Bacc("TRN2", target_bir_lowering=False, num_devices=1)
    arrays = {f"in_{n}": np.ascontiguousarray(v) for n, v in _laid_out(np, {n: np.asarray(v) for n, v in inputs.items()}).items()}
    dram = {n[3:]: nc.dram_tensor(n, v.shape, F32, kind="ExternalInput").ap() for n, v in arrays.items()}
    for name, shape in _OUTS:
        dram[name] = nc.dram_tensor(name, shape, F32, kind="ExternalOutput").ap()
    for name, shape in (("cum_d", (HEADS, KEYS)), ("x_d", (T, D)), ("y_d", (2 * T, D))):
        dram[name] = nc.dram_tensor(name, shape, F32, kind="Internal").ap()
    rows = lambda n: dram[n].rearrange("a b t h d -> (a b t) (h d)")
    dram["o_kv"] = {"fox": [rows(n) for n in ("o_fk_p", "o_fv_p", "o_fk_s", "o_fv_s")],
                    "sb": [rows(n) for n in ("o_sk_p", "o_sv_p", "o_sk_s", "o_sv_s")]}
    stream_step(nc, dram)
    got = run_bass_kernel_spmd(nc, [arrays], core_ids=[0]).results[0]
    return tuple(got[name] for name, _ in _OUTS)
```

```python
from contextlib import ExitStack

import concourse.bass as bass
from concourse import mybir

F32 = mybir.dt.float32
F32R = mybir.dt.float32r
I32 = mybir.dt.int32
U32 = mybir.dt.uint32
ALU = mybir.AluOpType
ACT = mybir.ActivationFunctionType
AX_X = mybir.AxisListType.X

P = 128
BANK = 512
D = 1024
J = D // P
SEQ, NEW, PAST = 512, 64, 512
T = SEQ + NEW
NT = 5
TP = NT * P
ROWS = [P, P, P, P, NEW]
KEYS = SEQ + PAST + NEW
NEW_AT = SEQ + PAST
VB = 9
KEY_RANGE = [(0, P), (0, 2 * P), (0, 3 * P), (0, 4 * P), (SEQ, KEYS)]
HD = 64
HEADS = 8
ROPE = 32
QW = HD + ROPE
Q_LORA, KV_LORA = 384, 256
JQ, JC = Q_LORA // P, KV_LORA // P
DOWN = Q_LORA + KV_LORA + ROPE
GROUPS, PER_GROUP, NE = 4, 8, 32
EH = 256
JE = EH // P
CB = 64
RING = 4
NB_MAX = NE + (2 * T) // CB
MORE = -(-T // CB) - 1
NB_TAB = -(-NB_MAX // RING) * RING + RING
ALPHA = 4.0 ** 0.25
LN_EPS, RMS_EPS = 1e-5, 1e-6
NEG = -1e30
FAR = 1e6
UNITS = 2 * NT
BLOCKS_OF = [1, 2, 3, 4, 5]
WIDTH = [hi - lo for lo, hi in KEY_RANGE]
WIDE = sum(WIDTH)
LEAD = 3
SCORE_BANK = [0, 1, 2, 3, 0, 2, 3, 0, 1, 2]


def hold(eng, passed, *counts):
    for sem, count in counts:
        eng.wait_ge(sem, count)
    eng.sem_inc(passed, 1)


class Steps:

    def __init__(self, eng, sem, base=0, passed=None):
        self.eng, self.sem, self.base, self.n, self.passed = eng, sem, base, 0, passed

    def then(self, ins):
        self.n += 1
        ins.then_inc(self.sem, 1)
        self.eng.wait_ge(self.sem, self.base + self.n)
        if self.passed is not None:
            self.eng.sem_inc(self.passed, 1)


class Core:

    def __init__(self, nc, ctx, dram):
        self.nc, self.ctx = nc, ctx
        self.x_rows = dram["x_rows"]
        self.x_t = dram["x_t"]
        self.w_ab = dram["w_ab"]
        self.w_f = dram["w_f"]
        self.b_f = dram["b_f"]
        self.logf_past = dram["logf_past"]
        self.k_past = dram["k_past"]
        self.v_past = dram["v_past"]
        self.w_out = dram["w_out"]
        self.w_latent_d = dram["w_latent"]
        self.w_rope_d = dram["w_rope"]
        self.g_q = dram["g_q"]
        self.g_kv = dram["g_kv"]
        self.w_uq = dram["w_uq"]
        self.w_ukv = dram["w_ukv"]
        self.ckv_past = dram["ckv_past"]
        self.kr_past = dram["kr_past"]
        self.cos = dram["cos"]
        self.sin = dram["sin"]
        self.w_r = dram["w_r"]
        self.b_r = dram["b_r"]
        self.w_gate_up = dram["w_gate_up"]
        self.w_down = dram["w_down"]
        self.ln_g = dram["ln_g"]
        self.ln_b = dram["ln_b"]
        self.o_y_p = dram["o_y_p"]
        self.o_y_s = dram["o_y_s"]
        self.o_logf_p = dram["o_logf_p"]
        self.o_ckv_p = dram["o_ckv_p"]
        self.o_kr_p = dram["o_kr_p"]
        self.o_logf_s = dram["o_logf_s"]
        self.o_ckv_s = dram["o_ckv_s"]
        self.o_kr_s = dram["o_kr_s"]
        self.cum_d = dram["cum_d"]
        self.x_d = dram["x_d"]
        self.y_d = dram["y_d"]
        self.o_kv = dram["o_kv"]

        def sb(name, shape, dt=F32):
            return ctx.enter_context(nc.sbuf_tensor(name, shape, dt))

        self.psum = ctx.enter_context(nc.psum_tensor("psum", [P, 8, BANK], F32))
        self.passed = ctx.enter_context(nc.semaphore("passed"))
        self.w_out_in = [ctx.enter_context(nc.semaphore(f"w_out_in{l}")) for l in range(2)]
        self.gu_in = [[ctx.enter_context(nc.semaphore(f"gu_in{l}{n}")) for n in range(RING)] for l in range(2)]
        self.dn_in = [[ctx.enter_context(nc.semaphore(f"dn_in{l}{n}")) for n in range(RING)] for l in range(2)]
        self.signals = []
        self.sb = sb
        self.xT = sb("xT", [P, J, TP])
        self.mix = sb("mix", [P, NT, D])
        self.ident = sb("ident", [P, P])
        self.cum_tok = sb("cum_tok", [P, NT, HEADS])
        self.half = sb("half", [P, 1])
        self.logits = sb("logits", [P, NT, GROUPS + NE])
        self.w_latent = self.mix[:, :, :].rearrange("p t d -> p (t d)").rearrange("p (j n) -> p j n", j=J)
        self.w_rope = sb("w_rope", [P, J, ROPE])
        self.w_latent_in = ctx.enter_context(nc.semaphore("w_latent_in"))
        self.glog = sb("glog", [P, NT, 8])
        self.tri = sb("tri", [P, P])
        self.ones = sb("ones", [P, P])
        self.iota = sb("iota", [P, P])
        self.slot_id = sb("slot_id", [P, 2, NT])
        self.beyond = sb("beyond", [P, NT])
        self.blocks_at = sb("blocks_at", [P, MORE])
        self.w_gu = [sb(f"w_gu{s}", [P, J, 2 * EH]) for s in range(2)]


def new_signal(k, name):
    k.signals.append(k.nc.alloc_semaphore(name))
    return k.signals[-1]


def clear_signals(k):
    k.nc.clear_and_free_semaphores(k.signals)
    k.signals = []
    k.nc.all_engine_barrier()


def r32(ap):
    return ap.bitcast(F32R)


def split_hi(nc, hi, a):
    return nc.scalar.activation(r32(hi), a, ACT.Copy)


def split_lo(nc, lo, a, hi):
    return nc.vector.tensor_tensor(r32(lo), a, hi, ALU.subtract)


def split_matmul(nc, dst, a, b, first, last):
    (ah, al), (bh, bl) = a, b
    nc.tensor.matmul(dst, r32(ah), r32(bh), start=first, stop=False)
    nc.tensor.matmul(dst, r32(ah), r32(bl), start=False, stop=False)
    return nc.tensor.matmul(dst, r32(al), r32(bh), start=False, stop=last)


def banks(k, first, count):
    return k.psum[:, first:first + count, :].rearrange("p b n -> p (b n)")


class Gates:

    def __init__(self, k):
        self.k, self.nc = k, k.nc
        sem = lambda n: new_signal(k, f"g_{n}")
        flat = lambda a: a[:].rearrange("p j n -> p (j n)")
        room_a, room_b = flat(k.w_gu[0]), flat(k.w_gu[1])
        self.logf, self.cum, self.ones = (room_a[0:HEADS, n * KEYS:(n + 1) * KEYS] for n in range(3))
        self.low = room_a[0:HEADS, 3 * KEYS:3 * KEYS + T]
        self.t_abs, self.t_exp, self.t_ln = (room_b[0:HEADS, n * T:(n + 1) * T] for n in range(3))
        at = 3 * T
        self.tok = room_b[:, at:at + NT * HEADS].rearrange("p (t h) -> p t h", t=NT)
        at += NT * HEADS
        self.wf = room_b[:, at:at + J * HEADS].rearrange("p (j h) -> p j h", j=J)
        at += J * HEADS
        self.iota_i = room_b[:, at:at + P].bitcast(I32)
        at += P
        self.id_i = room_b[:, at:at + 2 * NT].bitcast(I32).rearrange("p (c t) -> p c t", c=2)
        at += 2 * NT
        self.bf = room_b[0:HEADS, at:at + 1]
        self.xt_in = [sem("xt_in0"), sem("xt_in1")]
        self.f_in, self.filled, self.consts, self.z_ready, self.act_step, self.dve_step = (
            sem(n) for n in ("f_in", "filled", "consts", "z_ready", "act_step", "dve_step"))
        self.out, self.tok_t, self.tok_e, self.cum_ready, self.x_hi_done, self.x_lo_done = (
            sem(n) for n in ("out", "tok_t", "tok_e", "cum_ready", "x_hi_done", "x_lo_done"))
        self.z = banks(k, 0, 2)[0:HEADS, 0:T]
        self.trans = banks(k, 2, 1)

    def load(self, sp):
        k = self.k
        sp.dma_start(self.wf, k.w_f).then_inc(self.f_in, 16)
        for b in range(2):
            sp.dma_start(k.xT[:, 4 * b:4 * b + 4, 0:T], k.x_t[:, 4 * b:4 * b + 4, :]).then_inc(self.xt_in[b], 16)
        sp.dma_start(self.bf, k.b_f).then_inc(self.f_in, 16)
        sp.dma_start(self.logf[:, SEQ:NEW_AT], k.logf_past).then_inc(self.f_in, 16)
        for n in range(3):
            sp.dma_start(k.wp[n][:].rearrange("p j n -> p (j n)"), k.w_ab[n]).then_inc(k.wp_in[n], 16)

    def store(self, sp):
        k = self.k
        sp.wait_ge(self.cum_ready, 2)
        sp.dma_start(k.cum_d, self.cum).then_inc(self.out, 16)
        sp.wait_ge(self.tok_e, 4)
        sp.dma_start(k.o_logf_p.rearrange("a b (t p) h -> p (a b t) h", p=P), self.tok[:, 0:4, :]).then_inc(self.out, 16)
        sp.dma_start(k.o_logf_s.rearrange("a b t h -> (a b t) h"), self.tok[0:NEW, 4, :]).then_inc(self.out, 16)
        sp.wait_ge(self.out, 48)

    def fill(self, pool):
        k = self.k
        pool.memset(k.ident[:], 0.0).then_inc(self.filled, 1)
        pool.wait_ge(self.filled, 1)
        pool.affine_select(out=k.ident[:], in_=k.ident[:], compare_op=ALU.not_equal, fill=1.0, base=0,
                           pattern=[[-1, P]], channel_multiplier=1).then_inc(self.filled, 1)
        for n, (dst, value) in enumerate(((k.half[:], -0.5), (self.ones, 1.0), (k.cum_tok[NEW:P, 4, :], 0.0))):
            pool.wait_ge(self.filled, n + 2)
            pool.memset(dst, value).then_inc(self.filled, 1)
        pool.wait_ge(self.filled, 5)
        n = 0

        def step(ins):
            nonlocal n
            n += 1
            ins.then_inc(self.consts, 1)
            pool.wait_ge(self.consts, n)
        step(pool.memset(k.tri[:], 1.0))
        step(pool.affine_select(out=k.tri[:], in_=k.tri[:], compare_op=ALU.is_gt, fill=0.0, base=0, pattern=[[1, P]], channel_multiplier=-1))
        step(pool.memset(k.ones[:], 1.0))
        step(pool.memset(k.beyond[:], 0.0))
        step(pool.memset(k.beyond[NEW:P, 4:5], 1000.0))
        step(pool.iota(self.iota_i, [[1, P]], base=0, channel_multiplier=0))
        step(pool.tensor_copy(k.iota[:], self.iota_i))
        step(pool.tensor_scalar(k.blocks_at[:], k.iota[:, 1:1 + MORE], float(CB), None, ALU.mult))
        step(pool.iota(self.id_i, [[T, 2], [P, NT]], base=1, channel_multiplier=1))
        step(pool.tensor_copy(k.slot_id[:], self.id_i))
        step(pool.memset(k.slot_id[NEW:P, :, 4], 0.0))
        step(pool.memset(k.glog[:], -3e38))

    def products(self, pe):
        nc, k, z = self.nc, self.k, self.z
        pe.wait_ge(self.f_in, 48)
        for j in range(J):
            if j % 4 == 0:
                pe.wait_ge(self.xt_in[j // 4], 16)
            nc.tensor.matmul(z[:, 0:SEQ], self.wf[:, j, :], k.xT[:, j, 0:SEQ], start=(j == 0), stop=(j == J - 1))
            last = nc.tensor.matmul(z[:, SEQ:T], self.wf[:, j, :], k.xT[:, j, SEQ:T], start=(j == 0), stop=(j == J - 1))
        last.then_inc(self.z_ready, 1)
        pe.wait_ge(self.filled, 2)
        pe.wait_ge(self.x_lo_done, J)

    def turn(self, pe):
        pe.wait_ge(self.cum_ready, 2)
        for n, src in enumerate((self.logf, self.cum)):
            for t in range(NT):
                at = t * P if t < 4 else NEW_AT
                last = self.nc.tensor.transpose(self.trans[0:ROWS[t], (n * NT + t) * HEADS:(n * NT + t + 1) * HEADS],
                                                src[:, at:at + ROWS[t]], self.k.ident[0:HEADS, 0:HEADS])
        last.then_inc(self.tok_t, 1)

    def split_x_hi(self, act):
        for j in range(J):
            if j % 4 == 0:
                act.wait_ge(self.xt_in[j // 4], 16)
            split_hi(self.nc, self.k.x_hi[:, j, :], self.k.xT[:, j, 0:T]).then_inc(self.x_hi_done, 1)

    def logs(self, act):
        steps = Steps(act, self.act_step)
        act.wait_ge(self.z_ready, 1)
        act.wait_ge(self.f_in, 48)
        steps.then(self.nc.scalar.activation(self.t_abs, self.z, ACT.Abs, bias=self.bf))
        steps.then(self.nc.scalar.activation(self.t_exp, self.t_abs, ACT.Exp, scale=-1.0))
        self.nc.scalar.activation(self.t_ln, self.t_exp, ACT.Ln, bias=1.0).then_inc(self.act_step, 1)

    def split_x_lo(self, dve):
        for j in range(J):
            dve.wait_ge(self.x_hi_done, j + 1)
            split_lo(self.nc, self.k.x_lo[:, j, :], self.k.xT[:, j, 0:T], self.k.x_hi[:, j, :]).then_inc(self.x_lo_done, 1)

    def sums(self, dve):
        v, steps = self.nc.vector, Steps(dve, self.dve_step)
        logf, low, t_ln, cum, ones = self.logf, self.low, self.t_ln, self.cum, self.ones
        dve.wait_ge(self.f_in, 48)
        dve.wait_ge(self.act_step, 1)
        steps.then(v.tensor_scalar(low, self.z, self.bf, 0.0, ALU.add, ALU.min))
        dve.wait_ge(self.act_step, 3)
        v.tensor_tensor(logf[:, 0:SEQ], low[:, 0:SEQ], t_ln[:, 0:SEQ], ALU.subtract).then_inc(self.dve_step, 1)
        steps.n += 1
        steps.then(v.tensor_tensor(logf[:, NEW_AT:KEYS], low[:, SEQ:T], t_ln[:, SEQ:T], ALU.subtract))
        dve.wait_ge(self.filled, 5)
        v.tensor_tensor_scan(cum[:, 0:SEQ], ones[:, 0:SEQ], logf[:, 0:SEQ], 0.0, ALU.mult, ALU.add).then_inc(self.cum_ready, 1)
        v.tensor_tensor_scan(cum[:, SEQ:KEYS], ones[:, SEQ:KEYS], logf[:, SEQ:KEYS], 0.0, ALU.mult, ALU.add).then_inc(self.cum_ready, 1)

    def copy_turned(self, dve):
        dve.wait_ge(self.tok_t, 1)
        dve.wait_ge(self.filled, 5)
        for n, dst in enumerate((self.tok, self.k.cum_tok)):
            at = n * NT * HEADS
            self.nc.vector.tensor_copy(dst[:, 0:4, :], self.trans[:, at:at + 4 * HEADS].rearrange("p (t h) -> p t h", h=HEADS)).then_inc(self.tok_e, 1)
            self.nc.vector.tensor_copy(dst[0:NEW, 4, :], self.trans[0:NEW, at + 4 * HEADS:at + 5 * HEADS]).then_inc(self.tok_e, 1)


def unit_of(u):
    h, t = u // NT, u % NT
    lo, hi = KEY_RANGE[t]
    return h, t, ROWS[t], lo, hi - lo


AB_AFTER = {"q0": -1, "q1": 0, "k0": 2, "k1": 3, "kt": 4, "v0": 5, "v1": 7, "vt": 8}
MLA_AFTER = {"q": -1, "q4": 0, "k": 2, "v": 4, "t4": 6, "t": 8}


def attend(k, mla, m, gates=None):
    nc, passed = k.nc, k.passed
    PAIRS, SB_PAIRS = 8, 4
    tag = "mla" if mla else "ab"
    with ExitStack() as c:
        sb = lambda n, s, d=F32: c.enter_context(nc.sbuf_tensor(f"{tag}_{n}", s, d))
        sem = lambda n: new_signal(k, f"{tag}_{n}")
        v_all = [sb(f"v_all{a}", [P, VB, P]) for a in range(2)]
        score = sb("score", [P, WIDE])
        probs = sb("probs", [P, WIDE])
        probsT = sb("probsT", [P, 2, 5, P])
        small = sb("small", [P, NT, 4])
        if mla:
            wq, wkv = m["wq"], m["wkv"]
            q_tok = sb("q_tok", [P, NT, 2, QW])
            rot = sb("rot", [P, 4, NT, 2, ROPE // 2])
            qh = [[sb(f"q{a}{h}", [QW, T]) for h in range(2)] for a in range(2)]
            kh = m["kh"]
        else:
            wp = k.wp
            w_hi = [sb(f"w_hi{a}", [P, J, P]) for a in range(2)]
            w_lo = [sb(f"w_lo{a}", [P, J, P]) for a in range(2)]
            room = k.xT[:, :, :].rearrange("p j n -> p (j n)")
            cumk = [[room[:, (2 * a + h) * KEYS:(2 * a + h + 1) * KEYS] for h in range(2)] for a in range(2)]
            qh = [[sb(f"q{a}{h}", [P, T]) for h in range(2)] for a in range(2)]
            kT = [sb(f"kT{a}", [P, KEYS]) for a in range(2)]
            kh = [[kT[a], kT[a]] for a in range(2)]
            vT = sb("vT", [P, T])
            k_tok = sb("k_tok", [P, NT, P])
            bias = sb("bias", [P, WIDE])
            rest = bias
            cumq = sb("cumq", [P, 2, NT])
            ones = sb("ones", [P, T])
        if mla:
            names = ("zeroed projected proj_act proj_dve scores_ready scored probs_ready probsT_ready "
                     "probsT_used o_ready o_done dve_step rot_step roped")
        else:
            names = ("zeroed hi0 hi1 hi2 lo0 lo1 lo2 kp_in0 kp_in1 vp_in0 vp_in1 cumk_in0 cumk_in1 cumq_ready projected proj_act proj_dve k_out v_out "
                     "scores_ready scored bias_ready bias_step probs_ready probsT_ready probsT_used o_ready o_done "
                     "dve_step act_step soft_ready masked rest_done logit_ready")
        s = {n: sem(n) for n in names.split()}
        s.update({f"w{n}_in": w_in for n, w_in in enumerate(m["w_in"] if mla else k.wp_in)})
        n_zeroed = 5 if mla else 8
        STEPS = 6 if mla else 5
        slot = lambda u: banks(k, SCORE_BANK[u], 2 if u % NT == NT - 1 else 1)
        at_tile = lambda a, t: a[:, sum(WIDTH[:t]):sum(WIDTH[:t + 1])]
        bank_t, bank_o = banks(k, 4, 1), banks(k, 5, 1)
        proj = banks(k, 6, 2)
        HT = T // 2
        halves = proj.rearrange("p (b n) -> p b n", b=2)[:, :, 0:HT]
        by_half = lambda a: a.rearrange("p (b n) -> p b n", b=2)

        def of_parity(each, p, par):
            return p * (each // 2) + (each - par * (each // 2))

        def each_pair(eng, pair):
            if mla:
                with eng.Fori(0, PAIRS // 2 - 1) as i:
                    pair(2 * i, 0, "mla", True)
                    pair(2 * i + 1, 1, "mla", True)
                pair(PAIRS - 2, 0, "mla", True)
                pair(PAIRS - 1, 1, "mla", False)
                return
            with eng.Fori(0, SB_PAIRS // 2) as i:
                pair(2 * i, 0, "sb", True)
                pair(2 * i + 1, 1, "sb", True)
            for p in range(SB_PAIRS, PAIRS):
                pair(p, p % 2, "fox", p + 1 < PAIRS)

        def steps_after(after, u):
            return [name for name in after if after[name] == u]

        with nc.Block() as block:

            @block.sync
            def _(sp):
                row = lambda a, at: a[bass.ds(at, 1), :, :].rearrange("a p n -> p (a n)")

                def load_w(p, n):
                    if mla:
                        hold(sp, passed, (s["projected"], STEPS * p))
                        sp.dma_start(wq[:], row(k.w_uq, p)).then_inc(s["w0_in"], 16)
                        sp.dma_start(wkv[:], row(k.w_ukv, p)).then_inc(s["w1_in"], 16)
                        return
                    hold(sp, passed, (s[f"lo{n}"], p))
                    sp.dma_start(wp[n][:].rearrange("p j n -> p (j n)"), row(k.w_ab, p * 3 + n)).then_inc(s[f"w{n}_in"], 16)

                def load_past(p, par, fox):
                    if not isinstance(p, int) or p:
                        hold(sp, passed, (s["o_ready"], UNITS * (p - 1)))
                    sp.dma_start(kT[par][:, SEQ:NEW_AT], row(k.k_past, p)).then_inc(s[f"kp_in{par}"], 16)
                    sp.dma_start(v_all[par][:, 4:8, :].rearrange("p b n -> p (b n)"), row(k.v_past, p)).then_inc(s[f"vp_in{par}"], 16)
                    if fox:
                        fox_p = p - SB_PAIRS
                        if fox_p >= 2:
                            hold(sp, passed, (s["bias_ready"], UNITS * (fox_p - 1)))
                        for h in range(2):
                            sp.dma_start(cumk[par][h], k.cum_d[bass.ds(2 * fox_p + h, 1), :].to_broadcast([P, KEYS])).then_inc(s[f"cumk_in{par}"], 16)

                def store(p, par, kind, kv):
                    o_p, o_s = k.o_kv[kind][kv], k.o_kv[kind][kv + 2]
                    at = p - SB_PAIRS if kind == "fox" else p
                    done = STEPS * p + (5 if kv else 3)
                    hold(sp, passed, (s["proj_act"], done), (s["proj_dve"], done))
                    full, new = (v_all[par][:, 0:4, :], v_all[par][0:NEW, 8, :]) if kv else (k_tok[:, 0:4, :], k_tok[0:NEW, 4, :])
                    out = s["v_out"] if kv else s["k_out"]
                    sp.dma_start(o_p.rearrange("(t p) c -> p t c", p=P)[:, :, bass.ds(at * P, P)], full).then_inc(out, 16)
                    sp.dma_start(o_s[:, bass.ds(at * P, P)], new).then_inc(out, 16)

                def pair(p, par, kind, more):
                    if not more:
                        return
                    if mla:
                        if not (isinstance(p, int) and p + 2 >= PAIRS):
                            load_w(p + 2, 0)
                        return
                    last_w = isinstance(p, int) and p + 2 >= PAIRS
                    kind = "fox" if p + 1 >= SB_PAIRS else "sb"
                    load_past(p + 1, 1 - par, kind == "fox")
                    for n in range(3):
                        if not last_w:
                            load_w(p + 2, n)
                    store(p + 1, 1 - par, kind, 0)
                    store(p + 1, 1 - par, kind, 1)

                if mla:
                    load_w(1, 0)
                    with sp.Fori(0, PAIRS // 2 - 1) as i:
                        pair(2 * i, 0, "mla", True)
                        pair(2 * i + 1, 1, "mla", True)
                    sp.wait_ge(m["latents_out"], 64)
                else:
                    gates.load(sp)
                    load_past(0, 0, False)
                    for n in range(3):
                        load_w(1, n)
                    store(0, 0, "sb", 0)
                    gates.store(sp)
                    store(0, 0, "sb", 1)
                    for p in range(PAIRS):
                        pair(p, p % 2, None, p + 1 < PAIRS)
                        if p == SB_PAIRS:
                            prefetch_w_out(k, sp, 0)
                    sp.wait_ge(s["k_out"], 32 * PAIRS)
                    sp.wait_ge(s["v_out"], 32 * PAIRS)

            @block.tensor
            def _(pe):
                def banks_free(p, step, *more):
                    n = STEPS * p + step
                    hold(pe, passed, (s["proj_act"], n), (s["proj_dve"], n), *more)

                def project_ab(p, par, step):
                    n = "qkv".index(step[0])
                    if step[1] == "t":
                        banks_free(p, 2 if n == 1 else 4)
                        for t in range(NT):
                            at = NEW_AT if (t == 4 and n == 1) else t * P
                            src = kT[par] if n == 1 else vT
                            last = nc.tensor.transpose(proj[0:ROWS[t], t * P:(t + 1) * P], src[:, at:at + ROWS[t]], k.ident[:])
                        last.then_inc(s["projected"], 1)
                        return
                    half = int(step[1])
                    if half == 0:
                        banks_free(p, (0, 1, 3)[n], (s[f"lo{n}"], p + 1))
                    for j in range(4 * half, 4 * half + 4):
                        for b in range(2):
                            at = slice(b * HT, (b + 1) * HT)
                            last = split_matmul(nc, halves[:, b, :], (w_hi[(par + n) % 2][:, j, :], w_lo[(par + n) % 2][:, j, :]),
                                                (k.x_hi[:, j, at], k.x_lo[:, j, at]),
                                                j == 0, j == J - 1)
                    if half:
                        last.then_inc(s["projected"], 1)

                def project_mla(p, par, step):
                    order = list(MLA_AFTER).index(step)
                    more = {"q": [(s["w0_in"], 16 * (p + 1))], "k": [], "q4": [(s["w1_in"], 16 * (p + 1))], "v": [],
                            "t4": [(s["roped"], p + 1)], "t": []}[step]
                    banks_free(p, order, *more)
                    group = lambda dst, pairs: [nc.tensor.matmul(dst, a, b, start=(n == 0), stop=(n == len(pairs) - 1)) for n, (a, b) in enumerate(pairs)][-1]
                    q_tile = lambda t: [(m["cqT"][:, j, t * P:t * P + ROWS[t]], wq[:, j, :]) for j in range(JQ)]
                    k_part = lambda lo, hi: [(wkv[:, j, 0:P], m["ckvT"][:, j, lo:hi]) for j in range(JC)]
                    v_block = lambda b, rows: [(m["ckvT"][:, j, b * P:b * P + rows], wkv[:, j, P:2 * P]) for j in range(JC)]
                    turn = lambda dst, h, t: nc.tensor.transpose(dst, q_tok[0:ROWS[t], t, h, :], k.ident[0:ROWS[t], 0:ROWS[t]])
                    if step == "q":
                        for t in range(4):
                            last = group(k.psum[:, 6 + t // 2, (t % 2) * 2 * QW:(t % 2 + 1) * 2 * QW], q_tile(t))
                    elif step == "q4":
                        group(proj[0:NEW, 0:2 * QW], q_tile(4))
                        last = group(proj[:, BANK:BANK + NEW], k_part(NEW_AT, KEYS))
                    elif step == "k":
                        group(proj[:, 0:BANK], k_part(0, BANK))
                        last = group(proj[:, BANK:2 * BANK], k_part(BANK, 2 * BANK))
                    elif step == "v":
                        for b in range(8):
                            last = group(proj[:, b * P:(b + 1) * P], v_block(b, P))
                    elif step == "t4":
                        group(proj[0:NEW, 0:P], v_block(8, NEW))
                        for h in range(2):
                            last = turn(proj[0:QW, BANK + h * NEW:BANK + (h + 1) * NEW], h, 4)
                    else:
                        for h in range(2):
                            for t in range(4):
                                last = turn(proj[0:QW, h * BANK + t * P:h * BANK + (t + 1) * P], h, t)
                    last.then_inc(s["projected"], 1)

                project, after = (project_mla, MLA_AFTER) if mla else (project_ab, AB_AFTER)

                def scores(p, par, u):
                    h, t, rows, lo, width = unit_of(u)
                    n = UNITS * p + u
                    if u == 0:
                        hold(pe, passed, (s["proj_act"], STEPS * (p + 1)), (s["proj_dve"], STEPS * (p + 1)),
                             *([] if mla else [(s[f"kp_in{par}"], of_parity(16, p, par))]))
                    elif u >= LEAD:
                        hold(pe, passed, (s["scored"], n - LEAD + 1))
                    q = qh[par][h][0:QW, t * P:t * P + rows] if mla else qh[par][h][:, t * P:t * P + rows]
                    key = kh[par][h][0:QW, lo:lo + width] if mla else kh[par][h][:, lo:lo + width]
                    last = nc.tensor.matmul(slot(u)[0:rows, 0:min(width, BANK)], q, key[:, 0:min(width, BANK)], start=True, stop=True)
                    if width > BANK:
                        last = nc.tensor.matmul(slot(u)[0:rows, BANK:width], q, key[:, BANK:width], start=True, stop=True)
                    last.then_inc(s["scores_ready"], 1)

                def turn(p, u):
                    _, t, rows, _, _ = unit_of(u)
                    n = UNITS * p + u
                    hold(pe, passed, (s["probs_ready"], n + 1), (s["probsT_used"], n))
                    for b in range(BLOCKS_OF[t]):
                        wide = NEW if b == 4 else P
                        last = nc.tensor.transpose(bank_t[0:wide, b * rows:(b + 1) * rows],
                                                   at_tile(probs, t)[0:rows, b * P:b * P + wide], k.ident[0:rows, 0:rows])
                    last.then_inc(s["probsT_ready"], 1)

                def values(p, par, u):
                    h, t, rows, _, _ = unit_of(u)
                    n = UNITS * p + u
                    hold(pe, passed, (s["probsT_used"], n + 1), (s["o_done"], n), *([(s[f"vp_in{par}"], of_parity(16, p, par))] if u == 4 and not mla else []))
                    first_block = 0 if t < 4 else 4
                    for b in range(BLOCKS_OF[t]):
                        last = nc.tensor.matmul(bank_o[0:rows, 0:HD], probsT[:, u % 2, b, 0:rows],
                                                v_all[par][:, first_block + b, h * HD:(h + 1) * HD], start=(b == 0), stop=(b == BLOCKS_OF[t] - 1))
                    last.then_inc(s["o_ready"], 1)

                def pair(p, par, kind, more):
                    def projections(u):
                        for step in steps_after(after, u) if more else []:
                            project(p + 1, 1 - par, step)
                    for u in range(LEAD):
                        scores(p, par, u)
                    projections(-1)
                    for u in range(UNITS):
                        turn(p, u)
                        if u + LEAD < UNITS:
                            scores(p, par, u + LEAD)
                        projections(u)
                        values(p, par, u)

                pe.wait_ge(s["zeroed"], n_zeroed)
                if not mla:
                    gates.products(pe)
                for step in after:
                    project(0, 0, step)
                    if step == "v1":
                        gates.turn(pe)
                if not mla:
                    pe.wait_ge(gates.tok_e, 4)
                each_pair(pe, pair)

            copied = list(MLA_AFTER) if mla else ["q1", "k1", "kt", "v1", "vt"]
            after_of = MLA_AFTER if mla else AB_AFTER

            def splits(split, p, par, u):
                if mla:
                    return
                last = lambda ahead: isinstance(p, int) and p + ahead >= PAIRS
                if u == 1 and not last(1):
                    split(p + 1, 1 - par, 2)
                if u == 4 and not last(2):
                    split(p + 2, par, 0)
                if u == 8 and not last(2):
                    split(p + 2, par, 1)

            def first_copies(split, copy_out, gates_part):
                if not mla:
                    split(0, 0, 0)
                    split(0, 0, 1)
                    gates_part()
                for step in copied:
                    copy_out(0, 0, step)
                    if not mla:
                        {"q1": lambda: split(0, 0, 2), "k1": lambda: split(1, 1, 0), "v1": lambda: split(1, 1, 1)}.get(step, lambda: None)()

            @block.scalar
            def _(act):
                nc.scalar.preload_act_table_set("natural_log_exp_and_others")
                if not mla:
                    gates.split_x_hi(act)
                act.wait_ge(s["zeroed"], n_zeroed)
                copy = lambda dst, src, scale=1.0: nc.scalar.activation(dst, src, ACT.Copy, scale=scale)

                def copy_out(p, par, step):
                    n = STEPS * p + copied.index(step) + 1
                    waits = [(s["projected"], n)]
                    if step == "kt":
                        waits.append((s["k_out"], 32 * p))
                    if step == "vt":
                        waits.append((s["v_out"], 32 * p))
                    hold(act, passed, *waits)
                    if mla:
                        last = {
                            "q": lambda: copy(q_tok[:, 0:2, :, :].rearrange("p t h c -> p (t h c)"), proj[:, 0:4 * QW]),
                            "q4": lambda: copy(q_tok[0:NEW, 4, :, :].rearrange("p h c -> p (h c)"), proj[0:NEW, 0:2 * QW]),
                            "k": lambda: copy(kh[par][0][0:HD, 0:NEW_AT], proj[0:HD, :]),
                            "v": lambda: copy(v_all[par][:, 0:4, :].rearrange("p b c -> p (b c)"), proj[:, 0:BANK]),
                            "t4": lambda: copy(v_all[par][0:NEW, 8, :], proj[0:NEW, 0:P]),
                            "t": lambda: copy(qh[par][0][:, 0:SEQ], proj[0:QW, 0:BANK]),
                        }[step]()
                    else:
                        last = {
                            "q1": lambda: copy(by_half(qh[par][0][0:HD, :]), halves[0:HD], HD ** -0.5),
                            "k1": lambda: copy(kT[par][:, 0:HT], halves[:, 0, :]),
                            "kt": lambda: copy(k_tok[:, 0:4, :].rearrange("p t c -> p (t c)"), proj[:, 0:BANK]),
                            "v1": lambda: copy(vT[:, 0:HT], halves[:, 0, :]),
                            "vt": lambda: copy(v_all[par][:, 0:4, :].rearrange("p t c -> p (t c)"), proj[:, 0:BANK]),
                        }[step]()
                    last.then_inc(s["proj_act"], 1)

                def split(p, par, n):
                    used = STEPS * (p - 1) + (2, 4)[n] if n < 2 else STEPS * p + 1
                    waits = [] if isinstance(p, int) and p == 0 and n < 2 else [(s["projected"], used)]
                    hold(act, passed, (s[f"w{n}_in"], 16 * (p + 1)), *waits)
                    split_hi(nc, w_hi[(par + n) % 2][:], wp[n][:]).then_inc(s[f"hi{n}"], 1)

                def soften(p, u):
                    _, t, rows, _, width = unit_of(u)
                    n = UNITS * p + u
                    z, r = slot(u)[0:rows, 0:width], at_tile(rest, t)[0:rows]
                    steps = Steps(act, s["act_step"], base=2 * n, passed=passed)
                    hold(act, passed, (s["scores_ready"], n + 1), (s["scored"], n - NT + 1 if u >= NT else UNITS * p))
                    steps.then(nc.scalar.activation(r, z, ACT.Abs))
                    steps.then(nc.scalar.activation(r, r, ACT.Exp, scale=-1.0))
                    nc.scalar.activation(r, r, ACT.Ln, bias=1.0).then_inc(s["soft_ready"], 1)

                def exponent(p, u, kind):
                    _, t, rows, _, width = unit_of(u)
                    n = UNITS * p + u
                    ready = (s["logit_ready"], n + 1) if kind == "sb" else (s["scored"], n + 1)
                    hold(act, passed, ready, (s["probsT_ready"], n - NT + 1 if u >= NT else UNITS * p))
                    if kind == "sb":
                        nc.scalar.activation(at_tile(probs, t)[0:rows], at_tile(score, t)[0:rows], ACT.Exp).then_inc(s["probs_ready"], 1)
                    else:
                        nc.scalar.activation(at_tile(probs, t)[0:rows], at_tile(score, t)[0:rows], ACT.Exp, scale=-1.0,
                                             bias=small[0:rows, u % NT, 0:1], accum_out=small[0:rows, u % NT, 1:2]).then_inc(s["probs_ready"], 1)

                def turn_out(p, u):
                    _, t, rows, _, _ = unit_of(u)
                    n = UNITS * p + u
                    hold(act, passed, (s["probsT_ready"], n + 1), (s["o_ready"], n - 1 if u >= 2 else UNITS * p))
                    full = min(BLOCKS_OF[t], 4)
                    last = copy(probsT[:, u % 2, 0:full, 0:rows], bank_t[:, 0:full * rows].rearrange("p (b q) -> p b q", q=rows))
                    if t == 4:
                        last = copy(probsT[0:NEW, u % 2, 4, 0:NEW], bank_t[0:NEW, 4 * NEW:5 * NEW])
                    last.then_inc(s["probsT_used"], 1)

                def pair(p, par, kind, more):
                    def copies(u):
                        for step in copied if more else []:
                            if after_of[step] == u:
                                copy_out(p + 1, 1 - par, step)
                    if kind == "sb":
                        for u in range(LEAD):
                            soften(p, u)
                    exponent(p, 0, kind)
                    exponent(p, 1, kind)
                    copies(-1)
                    for u in range(UNITS):
                        turn_out(p, u)
                        if kind == "sb" and u + LEAD < UNITS:
                            soften(p, u + LEAD)
                        if u + 2 < UNITS:
                            exponent(p, u + 2, kind)
                        copies(u)
                        splits(split, p, par, u)

                first_copies(split, copy_out, lambda: gates.logs(act))
                each_pair(act, pair)

            @block.vector
            def _(dve):
                v = nc.vector
                if mla:
                    v.memset(q_tok[NEW:P, 4, :, :], 0.0).then_inc(s["zeroed"], 1)
                    v.memset(small[:], 0.0).then_inc(s["zeroed"], 1)
                else:
                    for a in range(2):
                        v.memset(qh[a][0][HD:P, :], 0.0).then_inc(s["zeroed"], 1)
                        v.memset(qh[a][1][0:HD, :], 0.0).then_inc(s["zeroed"], 1)
                    v.memset(ones[:], 1.0).then_inc(s["zeroed"], 1)
                for a in range(2):
                    v.memset(v_all[a][NEW:P, 8, :], 0.0).then_inc(s["zeroed"], 1)
                v.memset(probsT[:, :, 4, :], 0.0).then_inc(s["zeroed"], 1)
                dve.wait_ge(s["zeroed"], n_zeroed)
                if not mla:
                    gates.split_x_lo(dve)

                def rotate(p):
                    steps = Steps(dve, s["rot_step"], base=p, passed=passed)
                    half = ROPE // 2
                    x1, x2 = q_tok[:, :, :, HD:HD + half], q_tok[:, :, :, HD + half:QW]
                    both = lambda a: a.unsqueeze(2).to_broadcast([P, NT, 2, half])
                    hold(dve, passed, (s["proj_act"], STEPS * p + 2), (s["proj_dve"], STEPS * p + 2))
                    v.tensor_tensor(rot[:, 0], x1, both(m["cos"][:]), ALU.mult)
                    v.tensor_tensor(rot[:, 1], x2, both(m["sin"][:]), ALU.mult)
                    v.tensor_tensor(rot[:, 2], x1, both(m["sin"][:]), ALU.mult)
                    steps.then(v.tensor_tensor(rot[:, 3], x2, both(m["cos"][:]), ALU.mult))
                    v.tensor_tensor(x1, rot[:, 0], rot[:, 1], ALU.subtract)
                    v.tensor_tensor(x2, rot[:, 2], rot[:, 3], ALU.add).then_inc(s["roped"], 1)

                def copy_out(p, par, step):
                    n = STEPS * p + copied.index(step) + 1
                    waits = [(s["projected"], n)]
                    if step == "kt":
                        waits.append((s["k_out"], 32 * p))
                    if step == "vt":
                        waits.append((s["v_out"], 32 * p))
                    hold(dve, passed, *waits)
                    if mla:
                        def q4():
                            v.tensor_copy(kh[par][0][0:HD, NEW_AT:KEYS], proj[0:HD, BANK:BANK + NEW])
                            return v.tensor_copy(kh[par][1][0:HD, NEW_AT:KEYS], proj[HD:P, BANK:BANK + NEW])

                        def t4():
                            v.tensor_copy(qh[par][0][:, SEQ:T], proj[0:QW, BANK:BANK + NEW])
                            return v.tensor_copy(qh[par][1][:, SEQ:T], proj[0:QW, BANK + NEW:BANK + 2 * NEW])
                        last = {
                            "q": lambda: v.tensor_copy(q_tok[:, 2:4, :, :].rearrange("p t h c -> p (t h c)"), proj[:, BANK:BANK + 4 * QW]),
                            "q4": q4,
                            "k": lambda: v.tensor_copy(kh[par][1][0:HD, 0:NEW_AT], proj[HD:P, :]),
                            "v": lambda: v.tensor_copy(v_all[par][:, 4:8, :].rearrange("p b c -> p (b c)"), proj[:, BANK:2 * BANK]),
                            "t4": t4,
                            "t": lambda: v.tensor_copy(qh[par][1][:, 0:SEQ], proj[0:QW, BANK:2 * BANK]),
                        }[step]()
                    else:
                        def k1():
                            v.tensor_copy(kT[par][:, HT:SEQ], halves[:, 1, 0:SEQ - HT])
                            return v.tensor_copy(kT[par][:, NEW_AT:KEYS], halves[:, 1, SEQ - HT:HT])
                        last = {
                            "q1": lambda: v.tensor_scalar(by_half(qh[par][1][HD:P, :]), halves[HD:P], HD ** -0.5, None, ALU.mult),
                            "k1": k1,
                            "kt": lambda: v.tensor_copy(k_tok[0:NEW, 4, :], proj[0:NEW, BANK:BANK + P]),
                            "v1": lambda: v.tensor_copy(vT[:, HT:T], halves[:, 1, :]),
                            "vt": lambda: v.tensor_copy(v_all[par][0:NEW, 8, :], proj[0:NEW, BANK:BANK + P]),
                        }[step]()
                    last.then_inc(s["proj_dve"], 1)
                    if step == "q4":
                        rotate(p)

                def split(p, par, n):
                    hold(dve, passed, (s[f"hi{n}"], p + 1))
                    split_lo(nc, w_lo[(par + n) % 2][:], wp[n][:], w_hi[(par + n) % 2][:]).then_inc(s[f"lo{n}"], 1)

                def logits(p, u, kind):
                    _, t, rows, _, width = unit_of(u)
                    n = UNITS * p + u
                    hold(dve, passed, (s["scores_ready"], n + 1), *([(s["bias_ready"], n + 1 - UNITS * SB_PAIRS)] if kind == "fox" else []),
                         (s["probs_ready"], n - NT + 1 if u >= NT else UNITS * p))
                    add = at_tile(bias, t)[0:rows] if kind == "fox" else m["mask"][0:rows, m["mask_width"][t] - width:m["mask_width"][t]]
                    v.tensor_tensor_reduce(out=at_tile(score, t)[0:rows], in0=slot(u)[0:rows, 0:width], in1=add,
                                           scale=-1.0 if kind == "fox" else -float(QW) ** -0.5, scalar=3e38, op0=ALU.add, op1=ALU.min,
                                           accum_out=small[0:rows, u % NT, 0:1]).then_inc(s["scored"], 1)

                def softplus(p, u):
                    _, t, rows, _, width = unit_of(u)
                    n = UNITS * p + u
                    hold(dve, passed, (s["soft_ready"], n + 1), (s["probs_ready"], n - NT + 1 if u >= NT else UNITS * p))
                    v.scalar_tensor_tensor(at_tile(score, t)[0:rows], slot(u)[0:rows, 0:width], 0.0,
                                           at_tile(rest, t)[0:rows], ALU.max, ALU.add).then_inc(s["rest_done"], 1)

                def stick(p, u):
                    _, t, rows, _, width = unit_of(u)
                    n = UNITS * p + u
                    hold(dve, passed, (s["masked"], n + 1))
                    steps = Steps(dve, s["dve_step"], base=n, passed=passed)
                    steps.then(v.tensor_tensor_scan(at_tile(rest, t)[0:rows][:, ::-1], ones[0:rows, 0:width],
                                                    at_tile(score, t)[0:rows][:, ::-1], 0.0, ALU.mult, ALU.add))
                    v.tensor_tensor(at_tile(score, t)[0:rows], slot(u)[0:rows, 0:width], at_tile(rest, t)[0:rows],
                                    ALU.subtract).then_inc(s["scored"], 1)

                def finish(p, u, kind):
                    h, t, rows, _, _ = unit_of(u)
                    n = UNITS * p + u
                    place = {"sb": p + PAIRS - SB_PAIRS, "fox": p - SB_PAIRS, "mla": p}[kind]
                    dst = k.mix[0:rows, t, bass.ds(place * P + h * HD, HD)]
                    if kind == "sb":
                        hold(dve, passed, (s["o_ready"], n + 1))
                        v.tensor_copy(dst, bank_o[0:rows, 0:HD]).then_inc(s["o_done"], 1)
                        return
                    steps = Steps(dve, s["dve_step"], base=n, passed=passed)
                    hold(dve, passed, (s["probs_ready"], n + 1))
                    steps.then(v.reciprocal(small[0:rows, u % NT, 2:3], small[0:rows, u % NT, 1:2]))
                    hold(dve, passed, (s["o_ready"], n + 1))
                    v.tensor_scalar(dst, bank_o[0:rows, 0:HD], small[0:rows, u % NT, 2:3], None, ALU.mult).then_inc(s["o_done"], 1)

                def pair(p, par, kind, more):
                    def copies(u):
                        for step in copied if more else []:
                            if after_of[step] == u:
                                copy_out(p + 1, 1 - par, step)
                    if kind == "sb":
                        for u in range(LEAD):
                            softplus(p, u)
                        stick(p, 0)
                        stick(p, 1)
                    else:
                        if kind == "fox":
                            fox_p = p - SB_PAIRS
                            if fox_p:
                                hold(dve, passed, (s["bias_ready"], UNITS * fox_p))
                            for h in range(2):
                                last = v.tensor_copy(cumq[:, h, :].unsqueeze(2), k.cum_tok[:, :, bass.ds(2 * fox_p + h, 1)])
                            last.then_inc(s["cumq_ready"], 1)
                        logits(p, 0, kind)
                        logits(p, 1, kind)
                    copies(-1)
                    for u in range(UNITS):
                        if u + 2 < UNITS:
                            if kind == "sb":
                                stick(p, u + 2)
                            else:
                                logits(p, u + 2, kind)
                        if kind == "sb" and u + LEAD < UNITS:
                            softplus(p, u + LEAD)
                        finish(p, u, kind)
                        copies(u)
                        splits(split, p, par, u)

                first_copies(split, copy_out, lambda: gates.sums(dve))
                if not mla:
                    gates.copy_turned(dve)
                each_pair(dve, pair)

            if not mla:

                @block.gpsimd
                def _(pool):
                    gates.fill(pool)
                    pool.wait_ge(s["zeroed"], n_zeroed)
                    fills = {x: pool.to_reg(x) for x in (NEG, 0.0)}

                    def decay(p, par, u):
                        h, t, rows, lo, width = unit_of(u)
                        n = UNITS * p + u
                        fox_p = p - SB_PAIRS
                        steps = Steps(pool, s["bias_step"], base=UNITS * fox_p + u, passed=passed)
                        hold(pool, passed, *([(s[f"cumk_in{par}"], of_parity(32, fox_p, par)), (s["cumq_ready"], fox_p + 1)] if u == 0 else []),
                             (s["scored"], n - NT + 1 if u >= NT else UNITS * p))
                        steps.then(pool.tensor_scalar(at_tile(bias, t)[0:rows], cumk[par][h][0:rows, lo:lo + width], -1.0,
                                                      cumq[0:rows, h, t:t + 1], ALU.mult, ALU.add))
                        d = at_tile(bias, t)[0:rows, width - rows:width]
                        pool.affine_select(out=d, in_=d, compare_op=ALU.is_ge, fill=fills[NEG], base=0, pattern=[[-1, rows]],
                                           channel_multiplier=1).then_inc(s["bias_ready"], 1)

                    def cut(p, u, src, fill, done):
                        _, t, rows, _, width = unit_of(u)
                        hold(pool, passed, (s[src], UNITS * p + u + 1))
                        d = at_tile(score, t)[0:rows, width - rows:width]
                        pool.affine_select(out=d, in_=d, compare_op=ALU.is_gt, fill=fills[fill], base=0, pattern=[[-1, rows]],
                                           channel_multiplier=1).then_inc(s[done], 1)

                    def pair(p, par, kind, more):
                        if kind == "fox":
                            for u in range(UNITS):
                                decay(p, par, u)
                            return
                        for u in range(LEAD):
                            cut(p, u, "rest_done", 0.0, "masked")
                        cut(p, 0, "scored", NEG, "logit_ready")
                        cut(p, 1, "scored", NEG, "logit_ready")
                        for u in range(2, UNITS):
                            cut(p, u, "scored", NEG, "logit_ready")
                            if u + 1 < UNITS:
                                cut(p, u + 1, "rest_done", 0.0, "masked")

                    each_pair(pool, pair)


def mla_latents(k, m):
    nc = k.nc
    half = ROPE // 2
    with ExitStack() as c:
        sb = lambda n, s, d=F32: c.enter_context(nc.sbuf_tensor(f"lat_{n}", s, d))
        sem = lambda n: new_signal(k, f"lat_{n}")
        gains = sb("gains", [P, Q_LORA + KV_LORA])
        junk = sb("junk", [P, 2, Q_LORA + KV_LORA])
        cq = sb("cq", [P, 2, Q_LORA])
        ckv, kr, out_sem = m["ckv"], m["kr"], m["latents_out"]
        rot = sb("rot", [P, 4, half])
        ms = sb("ms", [P, NT, 4])
        g_in, past_in, z_ready, squared, mean_done, inv_done, normed, turned, turned_q, turned_k, rot_step, filled = (
            sem(n) for n in ("g_in past_in z_ready squared mean_done inv_done normed turned turned_q turned_k "
                             "rot_step filled").split())
        z = lambda t: banks(k, 2 * (t % 2), 2)
        tr = lambda t: banks(k, 4 + 2 * (t % 2), 2)

        with nc.Block() as block:

            @block.sync
            def _(sp):
                sp.dma_start(gains[:, 0:Q_LORA], k.g_q.to_broadcast([P, Q_LORA])).then_inc(g_in, 16)
                sp.dma_start(gains[:, Q_LORA:], k.g_kv.to_broadcast([P, KV_LORA])).then_inc(g_in, 16)
                sp.dma_start(m["cos"][:], k.cos).then_inc(g_in, 16)
                sp.dma_start(m["sin"][:], k.sin).then_inc(g_in, 16)
                sp.dma_start(m["wq"][:].rearrange("p j n -> p (j n)"), k.w_uq[0]).then_inc(m["w_in"][0], 16)
                sp.dma_start(m["wkv"][:].rearrange("p j n -> p (j n)"), k.w_ukv[0]).then_inc(m["w_in"][1], 16)
                sp.dma_start(m["ckvT"][:, :, SEQ:NEW_AT], k.ckv_past).then_inc(past_in, 16)
                for h in range(4):
                    sp.dma_start(m["kh"][h // 2][h % 2][HD:QW, SEQ:NEW_AT], k.kr_past).then_inc(past_in, 16)
                sp.wait_ge(normed, NT)
                sp.dma_start(k.o_ckv_p.rearrange("a b (t p) c -> p (a b t) c", p=P), ckv[:, 0:4, :]).then_inc(out_sem, 16)
                sp.dma_start(k.o_ckv_s.rearrange("a b t c -> (a b t) c"), ckv[0:NEW, 4, :]).then_inc(out_sem, 16)
                sp.dma_start(k.o_kr_p.rearrange("a b (t p) c -> p (a b t) c", p=P), kr[:, 0:4, :]).then_inc(out_sem, 16)
                sp.dma_start(k.o_kr_s.rearrange("a b t c -> (a b t) c"), kr[0:NEW, 4, :]).then_inc(out_sem, 16)
                sp.wait_ge(past_in, 80)

            @block.tensor
            def _(pe):
                pe.wait_ge(k.w_latent_in, 32)

                def down(t):
                    if t >= 2:
                        pe.wait_ge(normed, t - 1)
                        pe.wait_ge(squared, t - 1)
                    for lo, hi, w in ((0, BANK, k.w_latent[:, :, 0:BANK]), (BANK, DOWN - ROPE, k.w_latent[:, :, BANK:]), (DOWN - ROPE, DOWN, k.w_rope)):
                        for j in range(J):
                            last = nc.tensor.matmul(z(t)[0:ROWS[t], lo:hi], k.xT[:, j, t * P:t * P + ROWS[t]], w[:, j, :],
                                                    start=(j == 0), stop=(j == J - 1))
                    last.then_inc(z_ready, 1)

                def turn(t):
                    r = ROWS[t]
                    pe.wait_ge(normed, t + 1)
                    if t >= 2:
                        pe.wait_ge(turned_q, t - 1)
                        pe.wait_ge(turned_k, t - 1)
                    for j in range(JQ):
                        nc.tensor.transpose(tr(t)[:, j * P:j * P + r], cq[0:r, t % 2, j * P:(j + 1) * P], k.ident[0:r, 0:r])
                    for j in range(JC):
                        nc.tensor.transpose(tr(t)[:, BANK + j * P:BANK + j * P + r], ckv[0:r, t, j * P:(j + 1) * P], k.ident[0:r, 0:r])
                    nc.tensor.transpose(tr(t)[0:ROPE, BANK + 2 * P:BANK + 2 * P + r], kr[0:r, t, :], k.ident[0:r, 0:r]).then_inc(turned, 1)

                for t in range(NT):
                    down(t)
                    if t:
                        turn(t - 1)
                turn(NT - 1)

            def copy_q(act, t):
                r = ROWS[t]
                act.wait_ge(turned, t + 1)
                nc.scalar.activation(m["cqT"][:, :, t * P:t * P + r], tr(t)[:, 0:JQ * P].rearrange("p (j q) -> p j q", q=P)[:, :, 0:r],
                                     ACT.Copy).then_inc(turned_q, 1)

            @block.scalar
            def _(act):
                for t in range(NT):
                    r = ROWS[t]
                    act.wait_ge(z_ready, t + 1)
                    if t >= 2:
                        act.wait_ge(squared, t - 1)
                    nc.scalar.activation(junk[0:r, t % 2, 0:Q_LORA], z(t)[0:r, 0:Q_LORA], ACT.Square, accum_out=ms[0:r, t, 0:1])
                    nc.scalar.activation(junk[0:r, t % 2, Q_LORA:], z(t)[0:r, Q_LORA:Q_LORA + KV_LORA], ACT.Square,
                                         accum_out=ms[0:r, t, 1:2]).then_inc(squared, 1)
                    if t:
                        copy_q(act, t - 1)
                copy_q(act, NT - 1)

            @block.gpsimd
            def _(pool):
                pool.memset(m["mask"][:], 0.0).then_inc(filled, 1)
                pool.wait_ge(filled, 1)
                pool.memset(m["mask"][0:HD, m["mask_width"][0] - HD:m["mask_width"][0]], NEG).then_inc(filled, 1)
                for t in range(NT):
                    r = ROWS[t]
                    pool.wait_ge(mean_done, 2 * (t + 1))
                    pool.tensor_tensor(ms[0:r, t, 2:4], ms[0:r, t, 0:2], k.half[0:r, 0:1].to_broadcast([r, 2]), ALU.pow).then_inc(inv_done, 1)

            @block.vector
            def _(dve):
                steps = Steps(dve, rot_step)
                dve.wait_ge(g_in, 64)

                def norm(t):
                    r = ROWS[t]
                    dve.wait_ge(squared, t + 1)
                    dve.wait_ge(z_ready, t + 1)
                    nc.vector.tensor_scalar(ms[0:r, t, 0:1], ms[0:r, t, 0:1], 1.0 / Q_LORA, RMS_EPS, ALU.mult, ALU.add).then_inc(mean_done, 1)
                    nc.vector.tensor_scalar(ms[0:r, t, 1:2], ms[0:r, t, 1:2], 1.0 / KV_LORA, RMS_EPS, ALU.mult, ALU.add).then_inc(mean_done, 1)
                    x1 = z(t)[0:r, DOWN - ROPE:DOWN - half]
                    x2 = z(t)[0:r, DOWN - half:DOWN]
                    cos, sin = m["cos"][0:r, t, :], m["sin"][0:r, t, :]
                    nc.vector.tensor_tensor(rot[0:r, 0], x1, cos, ALU.mult)
                    nc.vector.tensor_tensor(rot[0:r, 1], x2, sin, ALU.mult)
                    nc.vector.tensor_tensor(rot[0:r, 2], x1, sin, ALU.mult)
                    steps.then(nc.vector.tensor_tensor(rot[0:r, 3], x2, cos, ALU.mult))
                    nc.vector.tensor_tensor(kr[0:r, t, 0:half], rot[0:r, 0], rot[0:r, 1], ALU.subtract)
                    steps.then(nc.vector.tensor_tensor(kr[0:r, t, half:ROPE], rot[0:r, 2], rot[0:r, 3], ALU.add))
                    dve.wait_ge(inv_done, t + 1)
                    if t >= 2:
                        dve.wait_ge(turned, t - 1)
                    nc.vector.scalar_tensor_tensor(cq[0:r, t % 2, :], z(t)[0:r, 0:Q_LORA], ms[0:r, t, 2:3], gains[0:r, 0:Q_LORA], ALU.mult, ALU.mult)
                    nc.vector.scalar_tensor_tensor(ckv[0:r, t, :], z(t)[0:r, Q_LORA:Q_LORA + KV_LORA], ms[0:r, t, 3:4],
                                                   gains[0:r, Q_LORA:], ALU.mult, ALU.mult).then_inc(normed, 1)

                def copy_k(t):
                    r = ROWS[t]
                    at = NEW_AT if t == 4 else t * P
                    dve.wait_ge(turned, t + 1)
                    nc.vector.tensor_copy(m["ckvT"][:, :, at:at + r], tr(t)[:, BANK:BANK + JC * P].rearrange("p (j q) -> p j q", q=P)[:, :, 0:r])
                    for h in range(4):
                        last = nc.vector.tensor_copy(m["kh"][h // 2][h % 2][HD:QW, at:at + r], tr(t)[0:ROPE, BANK + 2 * P:BANK + 2 * P + r])
                    last.then_inc(turned_k, 1)

                for t in range(NT):
                    norm(t)
                    if t:
                        copy_k(t - 1)
                copy_k(NT - 1)


def load_gate_up(k, sp, layer, expert, gu_in, gu):
    sp.dma_start(gu[:].rearrange("p j n -> p (j n)"), k.w_gate_up[layer, bass.ds(expert, 1)].rearrange("a p n -> p (a n)")).then_inc(gu_in, 16)


def load_down(k, sp, layer, expert, dn_in, dn):
    sp.dma_start(dn[:].rearrange("p j n -> p (j n)"), k.w_down[layer, bass.ds(expert, 1)].rearrange("a p n -> p (a n)")).then_inc(dn_in, 16)


def prefetch_w_out(k, sp, layer):
    for h in range(2):
        sp.dma_start(k.w_gu[h][:].rearrange("p j n -> p (j n)"), k.w_out[layer, h]).then_inc(k.w_out_in[layer], 16)


def prefetch_gate_up(k, sp, layer, slots):
    for n in slots:
        load_gate_up(k, sp, layer, n, k.gu_in[layer][n], k.w_gu[n])


def prefetch_down(k, sp, layer, slots):
    for n in slots:
        load_down(k, sp, layer, n, k.dn_in[layer][n], k.w_dn[n])


def mix_out(k, tag, layer):
    nc = k.nc
    with ExitStack() as c:
        sb = lambda n, s, d=F32: c.enter_context(nc.sbuf_tensor(f"{tag}_{n}", s, d))
        sem = lambda n: new_signal(k, f"{tag}_{n}")
        g = sb("g", [P, D])
        b = sb("b", [P, D])
        wr = sb("wr", [P, J, GROUPS + NE])
        br = sb("br", [P, GROUPS + NE])
        stats = sb("stats", [P, 2, 2, 6])
        mv = sb("mv", [P, 2, 4])
        p_in, turned, mixT_act, mixT_dve, y_ready, y_read, steps_s, var_done, inv_done, x_ready = (
            sem(n) for n in "p_in turned mixT_act mixT_dve y_ready y_read step var_done inv_done x_ready".split())
        xt_ready, xt_act, xt_dve, logit_mm, logit_done, out_sem = (sem(n) for n in "xt_ready xt_act xt_dve logit_mm logit_done out".split())
        n_p = 64 + (32 if layer == 0 else 0)
        mtr, xtr = banks(k, 0, 2), banks(k, 2, 2)
        y = lambda t: banks(k, 4 + 2 * (t % 2), 2)
        lg = banks(k, 0, 1)
        w = k.w_gu
        w_hi = [sb(f"w_hi{h}", [P, J, BANK]) for h in range(2)]
        w_lo = [sb(f"w_lo{h}", [P, J, BANK]) for h in range(2)]
        mix_hi = sb("mix_hi", [P, 2, J, P])
        mix_lo = sb("mix_lo", [P, 2, J, P])
        pad = sem("pad")
        w_hi_done, w_lo_done = sem("w_hi_done"), sem("w_lo_done")

        with nc.Block() as block:

            @block.sync
            def _(sp):
                if layer == 0:
                    sp.dma_start(k.x[:, 0:4, :], k.x_rows[0:SEQ, :].rearrange("(t p) d -> p t d", p=P)).then_inc(p_in, 16)
                    sp.dma_start(k.x[0:NEW, 4, :], k.x_rows[SEQ:T, :]).then_inc(p_in, 16)
                sp.dma_start(g[:], k.ln_g[layer, 0:1, :].to_broadcast([P, D])).then_inc(p_in, 16)
                sp.dma_start(b[:], k.ln_b[layer, 0:1, :].to_broadcast([P, D])).then_inc(p_in, 16)
                sp.dma_start(wr[:], k.w_r[layer]).then_inc(p_in, 16)
                sp.dma_start(br[:], k.b_r[layer:layer + 1, :].to_broadcast([P, GROUPS + NE])).then_inc(p_in, 16)
                sp.wait_ge(w_lo_done, 2 * J)
                prefetch_gate_up(k, sp, layer, [0, 1])
                for t in range(NT):
                    sp.wait_ge(x_ready, t + 1)
                    sp.dma_start(k.x_d[t * P:t * P + ROWS[t], :], k.x[0:ROWS[t], t, :]).then_inc(out_sem, 16)
                sp.wait_ge(out_sem, 16 * NT)

            @block.tensor
            def _(pe):
                def turn(tr, src, t, done):
                    for j in range(J):
                        last = nc.tensor.transpose(tr[:, j * P:j * P + ROWS[t]], src[0:ROWS[t], t, j * P:(j + 1) * P],
                                                   k.ident[0:ROWS[t], 0:ROWS[t]])
                    last.then_inc(done, 1)

                def turn_mix(t):
                    if t:
                        pe.wait_ge(mixT_act, t)
                        pe.wait_ge(mixT_dve, t)
                    turn(mtr, k.mix, t, turned)

                def out_proj(t):
                    pe.wait_ge(mixT_act, t + 1)
                    pe.wait_ge(mixT_dve, t + 1)
                    if t >= 2:
                        pe.wait_ge(y_read, t - 1)
                    for h in range(2):
                        for j in range(J):
                            if t == 0:
                                pe.wait_ge(w_lo_done, h * J + j + 1)
                            part = lambda a: a[:, t % 2, j, 0:ROWS[t]]
                            last = split_matmul(nc, y(t)[0:ROWS[t], h * BANK:(h + 1) * BANK], (part(mix_hi), part(mix_lo)),
                                                (w_hi[h][:, j, :], w_lo[h][:, j, :]), j == 0, j == J - 1)
                    last.then_inc(y_ready, 1)

                def turn_x(t):
                    pe.wait_ge(x_ready, t + 1)
                    if t:
                        pe.wait_ge(xt_act, t)
                        pe.wait_ge(xt_dve, t)
                    turn(xtr, k.x, t, xt_ready)

                def logits(t):
                    pe.wait_ge(xt_act, t + 1)
                    pe.wait_ge(xt_dve, t + 1)
                    if t == 0:
                        pe.wait_ge(pad, 1)
                        pe.wait_ge(p_in, n_p)
                        pe.wait_ge(mixT_dve, NT)
                    else:
                        pe.wait_ge(logit_done, t)
                    for j in range(J):
                        last = nc.tensor.matmul(lg[:, 0:GROUPS + NE], k.xT[:, j, t * P:(t + 1) * P], wr[:, j, :],
                                                start=(j == 0), stop=(j == J - 1))
                    last.then_inc(logit_mm, 1)

                turn_mix(0)
                turn_mix(1)
                for t in range(NT):
                    out_proj(t)
                    if t + 2 < NT:
                        turn_mix(t + 2)
                    if t >= 1:
                        turn_x(t - 1)
                    if t >= 2:
                        logits(t - 2)
                logits(NT - 2)
                turn_x(NT - 1)
                logits(NT - 1)

            @block.scalar
            def _(act):
                def copy(tr, t, done):
                    nc.scalar.activation(k.xT[:, 0:4, t * P:t * P + ROWS[t]], tr[:, 0:BANK].rearrange("p (j q) -> p j q", q=P)[:, :, 0:ROWS[t]],
                                         ACT.Copy).then_inc(done, 1)

                def copy_mix(t):
                    act.wait_ge(turned, t + 1)
                    if t >= 2:
                        act.wait_ge(y_ready, t - 1)
                    split_hi(nc, mix_hi[:, t % 2, :, 0:ROWS[t]], mtr.rearrange("p (j q) -> p j q", q=P)[:, :, 0:ROWS[t]]).then_inc(mixT_act, 1)
                copy_mix(0)
                copy_mix(1)
                act.wait_ge(k.w_out_in[layer], 32)
                for h in range(2):
                    for j in range(J):
                        split_hi(nc, w_hi[h][:, j, :], w[h][:, j, :]).then_inc(w_hi_done, 1)
                for t in range(NT):
                    if t + 2 < NT:
                        copy_mix(t + 2)
                    if t >= 1:
                        act.wait_ge(xt_ready, t)
                        copy(xtr, t - 1, xt_act)
                act.wait_ge(xt_ready, NT)
                copy(xtr, NT - 1, xt_act)

            @block.vector
            def _(dve):
                def copy(tr, t, done):
                    nc.vector.tensor_copy(k.xT[:, 4:8, t * P:t * P + ROWS[t]],
                                          tr[:, BANK:].rearrange("p (j q) -> p j q", q=P)[:, :, 0:ROWS[t]]).then_inc(done, 1)

                def copy_mix(t):
                    dve.wait_ge(mixT_act, t + 1)
                    if t >= 2:
                        dve.wait_ge(y_ready, t - 1)
                    split_lo(nc, mix_lo[:, t % 2, :, 0:ROWS[t]], mtr.rearrange("p (j q) -> p j q", q=P)[:, :, 0:ROWS[t]],
                             mix_hi[:, t % 2, :, 0:ROWS[t]]).then_inc(mixT_dve, 1)

                def copy_x(t):
                    dve.wait_ge(xt_ready, t + 1)
                    copy(xtr, t, xt_dve)

                def add_bias(t):
                    dve.wait_ge(logit_mm, t + 1)
                    nc.vector.tensor_tensor(k.logits[:, t, :], lg[:, 0:GROUPS + NE], br[:], ALU.add).then_inc(logit_done, 1)

                copy_mix(0)
                copy_mix(1)
                for h in range(2):
                    for j in range(J):
                        dve.wait_ge(w_hi_done, h * J + j + 1)
                        split_lo(nc, w_lo[h][:, j, :], w[h][:, j, :], w_hi[h][:, j, :]).then_inc(w_lo_done, 1)
                dve.wait_ge(p_in, n_p)
                steps = Steps(dve, steps_s)
                for t in range(NT):
                    if t + 2 < NT:
                        copy_mix(t + 2)
                    if t >= 1:
                        copy_x(t - 1)
                    dve.wait_ge(y_ready, t + 1)
                    x = k.x[0:ROWS[t], t, :]
                    steps.then(nc.vector.scalar_tensor_tensor(x, x, ALPHA, y(t)[0:ROWS[t], :], ALU.mult, ALU.add))
                    norm_tile(k, dve, steps, t, g, b, stats, mv, var_done, inv_done, x_ready, read=y_read)
                    if t >= 2:
                        add_bias(t - 2)
                add_bias(NT - 2)
                copy_x(NT - 1)
                add_bias(NT - 1)

            @block.gpsimd
            def _(pool):
                pool.memset(k.xT[:, :, T:TP], 0.0).then_inc(pad, 1)
                for t in range(NT):
                    inverse_std(k, pool, t, mv, var_done, inv_done)


def norm_tile(k, dve, steps, t, g, b, stats, mv, var_done, inv_done, x_ready, read=None):
    nc = k.nc
    r = ROWS[t]
    x = k.x[0:r, t, :]
    for h in range(2):
        last = nc.vector.bn_stats(stats[0:r, t % 2, h, :], x[:, h * BANK:(h + 1) * BANK])
        if read is not None and h == 0:
            last.then_inc(read, 1)
    steps.then(last)
    steps.then(nc.vector.bn_aggr(mv[0:r, t % 2, 0:2], stats[0:r, t % 2, :, :].rearrange("p a b -> p (a b)")))
    nc.vector.tensor_scalar(mv[0:r, t % 2, 2:3], mv[0:r, t % 2, 1:2], LN_EPS, None, ALU.add).then_inc(var_done, 1)
    steps.then(nc.vector.scalar_tensor_tensor(x, x, mv[0:r, t % 2, 0:1], g[0:r, :], ALU.subtract, ALU.mult))
    dve.wait_ge(inv_done, t + 1)
    nc.vector.scalar_tensor_tensor(x, x, mv[0:r, t % 2, 3:4], b[0:r, :], ALU.mult, ALU.add).then_inc(x_ready, 1)


def inverse_std(k, pool, t, mv, var_done, inv_done):
    r = ROWS[t]
    pool.wait_ge(var_done, t + 1)
    pool.tensor_tensor(mv[0:r, t % 2, 3:4], mv[0:r, t % 2, 2:3], k.half[0:r, :], ALU.pow).then_inc(inv_done, 1)


def route(k, tag, layer, r):
    nc = k.nc
    NX = NB_TAB - NE
    with ExitStack() as c:
        sb = lambda n, s, d=F32: c.enter_context(nc.sbuf_tensor(f"{tag}_{n}", s, d))
        sem = lambda n: new_signal(k, f"{tag}_{n}")
        top_g = sb("top_g", [P, NT, 8])
        idx_g = sb("idx_g", [P, NT, 8], U32)
        neg_g = sb("neg_g", [P, NT])
        exp_g = sb("exp_g", [P, NT, GROUPS])
        gate = sb("gate", [P, NT])
        g_of = sb("g_of", [P, NT])
        pen = sb("pen", [P, NT, GROUPS])
        elog = sb("elog", [P, NT, NE])
        top_e = sb("top_e", [P, NT, 8])
        idx_e = sb("idx_e", [P, NT, 8], U32)
        gap = sb("gap", [P, NT])
        e_gap = sb("e_gap", [P, NT])
        den = sb("den", [P, NT])
        e_of = sb("e_of", [P, 2, NT])
        hot = sb("hot", [P, 2, NT, NE])
        both = sb("both", [P, NT + 1, NE])
        work = sb("work", [P, 2, NT, NE])
        rank = sb("rank", [P, 2, NT])
        over = sb("over", [P, 2, NT])
        base = sb("base", [P, 2, NT])
        flag = sb("flag", [P, 2, NT])
        block_of = sb("block_of", [P, 2, NT])
        place = sb("place", [P, 2, NT])
        count = sb("count", [P, NE])
        extra = sb("extra", [P, NE])
        xend = sb("xend", [P, NE])
        xbase = sb("xbase", [P, NE])
        hot_p = sb("hot_p", [P, 2, NT, CB])
        hot_b = sb("hot_b", [P, 2, NT, NB_TAB])
        lst = sb("lst", [CB, NB_TAB])
        far = sb("far", [CB, NB_TAB])
        tok = sb("tok", [CB, NB_TAB])
        tab = sb("tab", [1, NX, NE])
        tab_f = sb("tab_f", [1, NB_TAB])
        trip = sb("trip", [1, 3])
        ended = sb("ended", [1, NX // RING])
        above_e = sb("above_e", [P, NE, MORE])
        above_s = sb("above_s", [P, 2 * NT, MORE])
        glog, tri, ones, iota, slot_id, blocks_at = k.glog, k.tri, k.ones, k.iota, k.slot_id, k.blocks_at
        blank, cleared = sem("blank"), sem("cleared")
        steps_s, gmax_done, gexp_done, gap_done, egap_done, hot_done, ranked, listed, lists_ready = (
            sem(n) for n in "step gmax_done gexp_done gap_done egap_done hot_done ranked listed lists".split())
        cum = banks(k, 0, 1)
        tot = cum[:, NT * NE:(NT + 1) * NE]
        lps = banks(k, 2, 1)

        with nc.Block() as block:

            @block.sync
            def _(sp):
                prefetch_down(k, sp, layer, [0, 1])
                for n in (2, 3):
                    prefetch_gate_up(k, sp, layer, [n])
                    prefetch_down(k, sp, layer, [n])

            @block.gpsimd
            def _(pool):
                pool.memset(both[:, NT, :], 0.0).then_inc(blank, 1)
                pool.wait_ge(blank, 1)
                pool.memset(k.mix[0:CB, 0:RING, :], 0.0).then_inc(cleared, 1)
                pool.wait_ge(cleared, 1)

            @block.scalar
            def _(act):
                act.wait_ge(gmax_done, 1)
                for t in range(NT):
                    last = nc.scalar.activation(exp_g[:, t, :], glog[:, t, 0:GROUPS], ACT.Exp, bias=neg_g[:, t:t + 1], accum_out=gate[:, t:t + 1])
                last.then_inc(gexp_done, 1)
                act.wait_ge(gap_done, 1)
                nc.scalar.activation(e_gap[:], gap[:], ACT.Exp).then_inc(egap_done, 1)
                for t in range(NT):
                    nc.scalar.activation(k.x[0:ROWS[t], t, :], k.x[0:ROWS[t], t, :], ACT.Copy, scale=ALPHA)
                nc.scalar.preload_act_table(ACT.Silu)

            @block.tensor
            def _(pe):
                pe.wait_ge(hot_done, 1)
                pe.wait_ge(blank, 1)
                flat = both[:].rearrange("p t e -> p (t e)")
                nc.tensor.matmul(cum[:, 0:(NT + 1) * NE], tri[:], flat, start=True, stop=False)
                for d in range(1, NT + 1):
                    last = nc.tensor.matmul(cum[:, d * NE:(NT + 1) * NE], ones[:], flat[:, 0:(NT + 1 - d) * NE], start=False, stop=(d == NT))
                last.then_inc(ranked, 1)
                pe.wait_ge(listed, 1)
                for n in range(2 * NT):
                    c_, t = n // NT, n % NT
                    last = nc.tensor.matmul(lps[0:CB, 0:NB_TAB], hot_p[:, c_, t, :], hot_b[:, c_, t, :], start=(n == 0), stop=(n == 2 * NT - 1))
                last.then_inc(lists_ready, 1)

            @block.vector
            def _(dve):
                v = nc.vector
                steps = Steps(dve, steps_s)
                steps.then(v.tensor_copy(glog[:, :, 0:GROUPS], k.logits[:, :, 0:GROUPS]))
                for t in range(NT):
                    last = v.max(top_g[:, t, :], glog[:, t, :])
                steps.then(last)
                v.tensor_scalar(neg_g[:], top_g[:, :, 0], -1.0, None, ALU.mult).then_inc(gmax_done, 1)
                for t in range(NT):
                    last = v.max_index(idx_g[:, t, :], top_g[:, t, :], glog[:, t, :])
                steps.then(last)
                steps.then(v.tensor_copy(g_of[:], idx_g[:, :, 0]))
                steps.then(v.tensor_tensor(pen[:], iota[:, 0:GROUPS].unsqueeze(1).to_broadcast([P, NT, GROUPS]),
                                           g_of[:].unsqueeze(2).to_broadcast([P, NT, GROUPS]), ALU.is_equal))
                steps.then(v.tensor_scalar(pen[:], pen[:], 1e30, -1e30, ALU.mult, ALU.add))
                for t in range(NT):
                    last = v.tensor_tensor(elog[:, t, :].rearrange("p (g e) -> p g e", e=PER_GROUP),
                                           k.logits[:, t, GROUPS:].rearrange("p (g e) -> p g e", e=PER_GROUP),
                                           pen[:, t, :].unsqueeze(2).to_broadcast([P, GROUPS, PER_GROUP]), ALU.add)
                steps.then(last)
                for t in range(NT):
                    last = v.max(top_e[:, t, :], elog[:, t, :])
                steps.then(last)
                v.tensor_tensor(gap[:], top_e[:, :, 1], top_e[:, :, 0], ALU.subtract).then_inc(gap_done, 1)
                for t in range(NT):
                    last = v.max_index(idx_e[:, t, :], top_e[:, t, :], elog[:, t, :])
                steps.then(last)
                steps.then(v.tensor_copy(e_of[:].rearrange("p c t -> p t c"), idx_e[:, :, 0:2]))
                steps.then(v.tensor_tensor(e_of[:], e_of[:], k.beyond[:].unsqueeze(1).to_broadcast([P, 2, NT]), ALU.add))
                for c_ in range(2):
                    last = v.tensor_tensor(hot[:, c_], iota[:, 0:NE].unsqueeze(1).to_broadcast([P, NT, NE]),
                                           e_of[:, c_, :].unsqueeze(2).to_broadcast([P, NT, NE]), ALU.is_equal)
                steps.then(last)
                v.tensor_tensor(both[:, 0:NT, :], hot[:, 0], hot[:, 1], ALU.add).then_inc(hot_done, 1)
                dve.wait_ge(gexp_done, 1)
                dve.wait_ge(egap_done, 1)
                v.tensor_scalar(den[:], e_gap[:], 1.0, None, ALU.add)
                steps.then(v.reciprocal(gate[:], gate[:]))
                steps.then(v.reciprocal(den[:], den[:]))
                steps.then(v.tensor_tensor(r["weight"][:, 0, :], gate[:], den[:], ALU.mult))
                v.tensor_tensor(r["weight"][:, 1, :], r["weight"][:, 0, :], e_gap[:], ALU.mult)
                dve.wait_ge(ranked, 1)
                steps.then(v.tensor_copy(count[:], tot))
                steps.then(v.tensor_tensor(above_e[:], count[:].unsqueeze(2).to_broadcast([P, NE, MORE]),
                                           blocks_at[:].unsqueeze(1).to_broadcast([P, NE, MORE]), ALU.is_gt))
                steps.then(v.tensor_reduce(extra[:], above_e[:], AX_X, ALU.add))
                steps.then(v.tensor_tensor_scan(xend[:], ones[:, 0:NE], extra[:], float(NE), ALU.mult, ALU.add))
                steps.then(v.tensor_tensor(xbase[:], xend[:], extra[:], ALU.subtract))
                for src, dst in ((cum[:, 0:NT * NE].rearrange("p (t e) -> p t e", e=NE), rank),
                                 (xbase[:].unsqueeze(1).to_broadcast([P, NT, NE]), base)):
                    for c_ in range(2):
                        last = v.tensor_tensor(work[:, c_], hot[:, c_], src, ALU.mult)
                    steps.then(last)
                    steps.then(v.tensor_reduce(dst[:], work[:], AX_X, ALU.add))
                steps.then(v.tensor_tensor(above_s[:], rank[:].rearrange("p c t -> p (c t)").unsqueeze(2).to_broadcast([P, 2 * NT, MORE]),
                                           blocks_at[:].unsqueeze(1).to_broadcast([P, 2 * NT, MORE]), ALU.is_ge))
                steps.then(v.tensor_reduce(over[:].rearrange("p c t -> p (c t)"), above_s[:], AX_X, ALU.add))
                steps.then(v.tensor_tensor(block_of[:], base[:], over[:], ALU.add))
                steps.then(v.tensor_tensor(block_of[:], block_of[:], e_of[:], ALU.subtract))
                steps.then(v.tensor_scalar(flag[:], over[:], 1.0, None, ALU.is_ge))
                steps.then(v.scalar_tensor_tensor(block_of[:], block_of[:], -1.0, flag[:], ALU.add, ALU.mult))
                steps.then(v.tensor_tensor(block_of[:], block_of[:], e_of[:], ALU.add))
                steps.then(v.scalar_tensor_tensor(place[:], over[:], -float(CB), rank[:], ALU.mult, ALU.add))
                for c_ in range(2):
                    v.tensor_tensor(hot_p[:, c_], iota[:, 0:CB].unsqueeze(1).to_broadcast([P, NT, CB]),
                                    place[:, c_, :].unsqueeze(2).to_broadcast([P, NT, CB]), ALU.is_equal)
                    last = v.tensor_tensor(hot_b[:, c_], iota[:, 0:NB_TAB].unsqueeze(1).to_broadcast([P, NT, NB_TAB]),
                                           block_of[:, c_, :].unsqueeze(2).to_broadcast([P, NT, NB_TAB]), ALU.is_equal)
                steps.then(last)
                for c_ in range(2):
                    last = v.tensor_tensor(hot_b[:, c_], hot_b[:, c_], slot_id[:, c_, :].unsqueeze(2).to_broadcast([P, NT, NB_TAB]), ALU.mult)
                last.then_inc(listed, 1)
                steps.then(v.tensor_tensor(tab[:], iota[0:1, NE:NE + NX].unsqueeze(2).to_broadcast([1, NX, NE]),
                                           xend[0:1, :].unsqueeze(1).to_broadcast([1, NX, NE]), ALU.is_ge))
                v.tensor_copy(tab_f[:, 0:NE], iota[0:1, 0:NE])
                steps.then(v.tensor_reduce(tab_f[:, NE:NB_TAB], tab[:], AX_X, ALU.add))
                steps.then(v.tensor_scalar(tab_f[:, NE:NB_TAB], tab_f[:, NE:NB_TAB], float(NE - 1), None, ALU.min))
                steps.then(v.tensor_copy(r["expert"][:], tab_f[:]))
                steps.then(v.tensor_scalar(ended[:], iota[0:1, NE:NB_TAB:RING], xend[0:1, NE - 1:NE], None, ALU.is_lt))
                steps.then(v.tensor_reduce(trip[:, 0:1], ended[:], AX_X, ALU.add))
                v.tensor_scalar(trip[:, 1:2], trip[:, 0:1], float(NE // RING), None, ALU.add)
                steps.then(v.tensor_scalar(trip[:, 2:3], trip[:, 0:1], float(NE // RING - 1), None, ALU.add))
                steps.then(v.tensor_copy(r["trips"][:], trip[:, 1:3]))
                dve.wait_ge(lists_ready, 1)
                steps.then(v.tensor_scalar(lst[:], lps[0:CB, 0:NB_TAB], -1.0, None, ALU.add))
                v.tensor_scalar(far[:], lst[:], 0.0, FAR, ALU.is_lt, ALU.mult)
                steps.then(v.tensor_scalar(tok[:], lst[:], float(T), -float(T), ALU.is_ge, ALU.mult))
                steps.then(v.tensor_tensor(lst[:], lst[:], far[:], ALU.add))
                v.tensor_copy(r["slots"][:], lst[:])
                steps.then(v.tensor_tensor(tok[:], tok[:], lst[:], ALU.add))
                steps.then(v.tensor_copy(r["tokens"][:], tok[:]))


def experts(k, tag, layer, r):
    nc, passed = k.nc, k.passed
    first_trips = NE // RING
    with ExitStack() as c:
        sb = lambda n, s, d=F32: c.enter_context(nc.sbuf_tensor(f"{tag}_{n}", s, d))
        sem = lambda n: new_signal(k, f"{tag}_{n}")
        x_idx = [sb(f"x_idx{n}", [CB, 1], I32) for n in range(RING)]
        y_idx = [sb(f"y_idx{n}", [CB, 1], I32) for n in range(RING)]
        xg = [k.mix[0:CB, n, :] for n in range(RING)]
        xgT = sb("xgT", [P, 2, J, CB])
        silu = sb("silu", [CB, 2, EH])
        hid = sb("hid", [CB, 2, EH])
        hidT = sb("hidT", [P, 2, JE, CB])
        yo = [sb(f"yo{n}", [CB, D]) for n in range(RING)]
        w_gu, w_dn, gu_in, dn_in = k.w_gu, k.w_dn, k.gu_in[layer], k.dn_in[layer]
        x_in = [sem(f"x_in{n}") for n in range(RING)]
        y_out = [sem(f"y_out{n}") for n in range(RING)]
        x_turned, xgT_ready, gu_ready, silu_ready, hid_ready, hid_turned, hidT_ready, y_ready, y_act, y_dve, xi_done, yi_done = (
            sem(n) for n in ("x_turned xgT_ready gu_ready silu_ready hid_ready hid_turned hidT_ready y_ready "
                             "y_act y_dve xi_done yi_done").split())
        gu = lambda b: banks(k, b % 2, 1)
        y = lambda b: banks(k, 2 + b % 2, 1)
        xtr = lambda b: banks(k, 4 + b % 2, 1)
        htr = lambda b: banks(k, 6 + b % 2, 1)

        def trips(eng):
            return eng.value_load(r["trips"][0:1, 0:1], min_val=first_trips, max_val=NB_TAB // RING - 1)

        with nc.Block() as block:

            @block.sync
            def _(sp):
                n_trips = trips(sp)
                sp.dma_start(r["g"][:], k.ln_g[layer, 1:2, :].to_broadcast([P, D])).then_inc(r["g_in"], 16)
                sp.dma_start(r["b"][:], k.ln_b[layer, 1:2, :].to_broadcast([P, D])).then_inc(r["g_in"], 16)
                with sp.Fori(0, n_trips - 1) as i:
                    for s in range(RING):
                        hold(sp, passed, (gu_ready, RING * i + s + 1))
                        expert = sp.value_load(r["expert"][0:1, bass.ds(RING * (i + 1) + s, 1)], min_val=0, max_val=NE - 1)
                        load_gate_up(k, sp, layer, expert, gu_in[s], w_gu[s])
                        hold(sp, passed, (y_ready, RING * i + s + 1))
                        load_down(k, sp, layer, expert, dn_in[s], w_dn[s])

            @block.gpsimd
            def _(pool):
                before_last = pool.value_load(r["trips"][0:1, 1:2], min_val=first_trips - 1, max_val=NB_TAB // RING - 2)

                def gather(i, s):
                    if isinstance(i, int):
                        assert i == 0
                    else:
                        hold(pool, passed, (x_turned, RING * (i - 1) + s + 1))
                    pool.tensor_copy(x_idx[s][:], r["tokens"][:, bass.ds(RING * i + s, 1)]).then_inc(xi_done, 1)
                    hold(pool, passed, (xi_done, RING * i + s + 1))
                    pool.indirect_dma_start(out=xg[s], out_offset=None, in_=k.x_d[:, :],
                                            in_offset=bass.IndirectOffsetOnAxis(ap=x_idx[s][:, 0:1], axis=0),
                                            bounds_check=T - 1, oob_is_err=False).then_inc(x_in[s], 16)

                def scatter(i, s):
                    hold(pool, passed, (y_act, RING * i + s + 1), (y_dve, RING * i + s + 1), (y_out[s], 16 * i))
                    pool.tensor_copy(y_idx[s][:], r["slots"][:, bass.ds(RING * i + s, 1)]).then_inc(yi_done, 1)
                    hold(pool, passed, (yi_done, RING * i + s + 1))
                    pool.indirect_dma_start(out=k.y_d[:, :], out_offset=bass.IndirectOffsetOnAxis(ap=y_idx[s][:, 0:1], axis=0),
                                            in_=yo[s][:], in_offset=None, bounds_check=2 * T - 1, oob_is_err=False).then_inc(y_out[s], 16)

                for s in range(RING):
                    gather(0, s)
                with pool.Fori(0, before_last) as i:
                    for s in range(RING):
                        gather(i + 1, s)
                        scatter(i, s)
                for s in range(RING):
                    scatter(before_last, s)
                for s in range(RING):
                    hold(pool, passed, (y_out[s], 16 * (before_last + 1)))

            @block.tensor
            def _(pe):
                n_trips = trips(pe)

                def turn_x(i, s):
                    b = RING * i + s
                    hold(pe, passed, (x_in[s], 16 * (i + 1)), *([(xgT_ready, b - 1)] if s >= 2 else [(y_act, RING * i), (y_dve, RING * i)]))
                    for j in range(J):
                        last = nc.tensor.transpose(xtr(s)[:, j * CB:(j + 1) * CB], xg[s][:, j * P:(j + 1) * P], k.ident[0:CB, 0:CB])
                    last.then_inc(x_turned, 1)

                def up(i, s):
                    b = RING * i + s
                    hold(pe, passed, (gu_in[s], 16 * (i + 1)), (xgT_ready, b + 1), *[(hid_ready, b - 1)] * (s >= 2))
                    for j in range(J):
                        for h in range(2):
                            last = nc.tensor.matmul(gu(s)[h * CB:(h + 1) * CB, 0:EH], xgT[:, s % 2, j, :], w_gu[s][:, j, h * EH:(h + 1) * EH],
                                                    start=(j == 0), stop=(j == J - 1))
                    last.then_inc(gu_ready, 1)

                def down(i, s):
                    b = RING * i + s
                    hold(pe, passed, (hid_ready, b + 1), *[(hidT_ready, b - 1)] * (s >= 2))
                    for j in range(JE):
                        last = nc.tensor.transpose(htr(s)[:, j * CB:(j + 1) * CB], hid[:, s % 2, j * P:(j + 1) * P], k.ident[0:CB, 0:CB])
                    last.then_inc(hid_turned, 1)
                    hold(pe, passed, (dn_in[s], 16 * (i + 1)), (hidT_ready, b + 1), *[(y_act, b - 1), (y_dve, b - 1)] * (s >= 2))
                    for j in range(JE):
                        for h in range(2):
                            last = nc.tensor.matmul(y(s)[h * CB:(h + 1) * CB, :], hidT[:, s % 2, j, :], w_dn[s][:, j, h * BANK:(h + 1) * BANK],
                                                    start=(j == 0), stop=(j == JE - 1))
                    last.then_inc(y_ready, 1)

                with pe.Fori(0, n_trips) as i:
                    turn_x(i, 0)
                    for s in range(RING):
                        up(i, s)
                        if s + 1 < RING:
                            turn_x(i, s + 1)
                        if s:
                            down(i, s - 1)
                    down(i, RING - 1)

            @block.scalar
            def _(act):
                n_trips = trips(act)

                def gate(i, s):
                    b = RING * i + s
                    hold(act, passed, (gu_ready, b + 1), (hid_ready, b - 1 if s >= 2 else RING * i))
                    nc.scalar.activation(silu[:, s % 2, :], gu(s)[0:CB, 0:EH], ACT.Silu).then_inc(silu_ready, 1)

                def out(i, s):
                    hold(act, passed, (y_ready, RING * i + s + 1), (y_out[s], 16 * i))
                    nc.scalar.activation(yo[s][:, 0:BANK], y(s)[0:CB, :], ACT.Copy).then_inc(y_act, 1)

                with act.Fori(0, n_trips) as i:
                    for s in range(RING):
                        gate(i, s)
                        if s:
                            out(i, s - 1)
                    out(i, RING - 1)

            @block.vector
            def _(dve):
                n_trips = trips(dve)

                def copy_x(i, s):
                    b = RING * i + s
                    hold(dve, passed, (x_turned, b + 1), (gu_ready, b - 1 if s >= 2 else RING * i))
                    nc.vector.tensor_copy(xgT[:, s % 2, :, :].rearrange("p j q -> p (j q)"), xtr(s)).then_inc(xgT_ready, 1)

                def hidden(i, s):
                    b = RING * i + s
                    hold(dve, passed, (silu_ready, b + 1), (hid_turned, b - 1 if s >= 2 else RING * i))
                    nc.vector.tensor_tensor(hid[:, s % 2, :], silu[:, s % 2, :], gu(s)[CB:P, 0:EH], ALU.mult).then_inc(hid_ready, 1)

                def copy_h(i, s):
                    b = RING * i + s
                    hold(dve, passed, (hid_turned, b + 1), (y_ready, b - 1 if s >= 2 else RING * i))
                    nc.vector.tensor_copy(hidT[:, s % 2, :, :].rearrange("p j q -> p (j q)"), htr(s)[:, 0:JE * CB]).then_inc(hidT_ready, 1)

                def out(i, s):
                    hold(dve, passed, (y_ready, RING * i + s + 1), (y_out[s], 16 * i))
                    nc.vector.tensor_copy(yo[s][:, BANK:D], y(s)[CB:P, :]).then_inc(y_dve, 1)

                with dve.Fori(0, n_trips) as i:
                    copy_x(i, 0)
                    for s in range(RING):
                        if s + 1 < RING:
                            copy_x(i, s + 1)
                        hidden(i, s)
                        if s:
                            copy_h(i, s - 1)
                            out(i, s - 1)
                    copy_h(i, RING - 1)
                    out(i, RING - 1)


def combine(k, tag, layer, r, last_layer):
    nc = k.nc
    with ExitStack() as c:
        sb = lambda n, s, d=F32: c.enter_context(nc.sbuf_tensor(f"{tag}_{n}", s, d))
        sem = lambda n: new_signal(k, f"{tag}_{n}")
        g, b = r["g"], r["b"]
        lent = k.w_gu[3][:].rearrange("p j n -> p (j n)").rearrange("p (t c d) -> p t c d", t=2, c=2)
        ys = [lent[:, 0], lent[:, 1]] + [sb(f"ys{t}", [P, 2, D]) for t in range(2, NT)]
        stats = sb("stats", [P, 2, 2, 6])
        mv = sb("mv", [P, 2, 4])
        y_in = [[sem(f"y_in{c_}{t}") for t in range(NT)] for c_ in range(2)]
        steps_s, scaled, added, var_done, inv_done, x_ready, xt_ready, xt_act, out_sem = (
            sem(n) for n in "step scaled added var_done inv_done x_ready xt_ready xt_act out".split())
        tr = lambda t: banks(k, 2 * (t % 2), 2)

        with nc.Block() as block:

            @block.sync
            def _(sp):
                for t in range(NT):
                    for c_ in range(2):
                        at = c_ * T + t * P
                        sp.dma_start(ys[t][0:ROWS[t], c_, :], k.y_d[at:at + ROWS[t], :]).then_inc(y_in[c_][t], 16)
                if not last_layer:
                    sp.dma_start(k.w_latent, k.w_latent_d).then_inc(k.w_latent_in, 16)
                    sp.dma_start(k.w_rope[:], k.w_rope_d).then_inc(k.w_latent_in, 16)
                    prefetch_w_out(k, sp, layer + 1)
                else:
                    for t in range(NT):
                        sp.wait_ge(x_ready, t + 1)
                        dst = k.o_y_p[0, t * P:(t + 1) * P, :] if t < 4 else k.o_y_s[0, :, :]
                        sp.dma_start(dst, k.x[0:ROWS[t], t, :]).then_inc(out_sem, 16)
                    sp.wait_ge(out_sem, 16 * NT)

            @block.vector
            def _(dve):
                steps = Steps(dve, steps_s)
                dve.wait_ge(r["g_in"], 32)
                for t in range(NT):
                    x = k.x[0:ROWS[t], t, :]
                    dve.wait_ge(y_in[1][t], 16)
                    dve.wait_ge(added, t + 1)
                    steps.then(nc.vector.scalar_tensor_tensor(x, ys[t][0:ROWS[t], 1, :], r["weight"][0:ROWS[t], 1, t:t + 1], x, ALU.mult, ALU.add))
                    norm_tile(k, dve, steps, t, g, b, stats, mv, var_done, inv_done, x_ready)

            @block.gpsimd
            def _(pool):
                def add(t):
                    x, y0 = k.x[0:ROWS[t], t, :], ys[t][0:ROWS[t], 0, :]
                    pool.wait_ge(scaled, t + 1)
                    pool.tensor_tensor(x, x, y0, ALU.add).then_inc(added, 1)
                add(0)
                for t in range(NT):
                    if t + 1 < NT:
                        add(t + 1)
                    inverse_std(k, pool, t, mv, var_done, inv_done)

            @block.scalar
            def _(act):
                for t in range(NT):
                    y0 = ys[t][0:ROWS[t], 0, :]
                    act.wait_ge(y_in[0][t], 16)
                    nc.scalar.activation(y0, y0, ACT.Copy, scale=r["weight"][0:ROWS[t], 0, t:t + 1]).then_inc(scaled, 1)
                if not last_layer:
                    for t in range(NT):
                        act.wait_ge(xt_ready, t + 1)
                        nc.scalar.activation(k.xT[:, :, t * P:t * P + ROWS[t]],
                                             tr(t).rearrange("p (j q) -> p j q", q=P)[:, :, 0:ROWS[t]], ACT.Copy).then_inc(xt_act, 1)

            if not last_layer:

                @block.tensor
                def _(pe):
                    for t in range(NT):
                        pe.wait_ge(x_ready, t + 1)
                        if t >= 2:
                            pe.wait_ge(xt_act, t - 1)
                        for j in range(J):
                            last = nc.tensor.transpose(tr(t)[:, j * P:j * P + ROWS[t]], k.x[0:ROWS[t], t, j * P:(j + 1) * P], k.ident[0:ROWS[t], 0:ROWS[t]])
                        last.then_inc(xt_ready, 1)


def routed(k, c, tag):
    sb = lambda n, s, d=F32: c.enter_context(k.nc.sbuf_tensor(f"{tag}_{n}", s, d))
    return {"weight": sb("weight", [P, 2, NT]), "expert": sb("expert", [1, NB_TAB], I32), "trips": sb("trips", [1, 2], I32),
            "slots": sb("slots", [CB, NB_TAB], I32), "tokens": sb("tokens", [CB, NB_TAB], I32),
            "g": sb("g", [P, D]), "b": sb("b", [P, D]), "g_in": new_signal(k, f"{tag}_g_in")}


def mixer_out_and_mixture(k, layer, last_layer):
    mix_out(k, f"mix{layer}", layer)
    clear_signals(k)
    with ExitStack() as c:
        r = routed(k, c, f"moe{layer}")
        k.w_gu += [c.enter_context(k.nc.sbuf_tensor(f"w_gu{n}_{layer}", [P, J, 2 * EH], F32)) for n in range(2, RING)]
        k.w_dn = [c.enter_context(k.nc.sbuf_tensor(f"w_dn{n}_{layer}", [P, JE, D], F32)) for n in range(RING)]
        route(k, f"moe{layer}_route", layer, r)
        experts(k, f"moe{layer}_experts", layer, r)
        combine(k, f"moe{layer}_combine", layer, r, last_layer)
        k.w_gu = k.w_gu[0:2]
    clear_signals(k)


def stream_step(nc, dram):
    with ExitStack() as ctx:
        k = Core(nc, ctx, dram)
        with ExitStack() as c:
            sb = lambda n, s, d=F32: c.enter_context(nc.sbuf_tensor(n, s, d))
            k.wp = [sb(f"w_{n}", [P, J, P]) for n in "qkv"]
            k.wp_in = [new_signal(k, f"w_{n}_in") for n in "qkv"]
            k.x_hi, k.x_lo = sb("x_hi", [P, J, T]), sb("x_lo", [P, J, T])
            attend(k, False, None, Gates(k))
        k.x = ctx.enter_context(nc.sbuf_tensor("x", [P, NT, D], F32))
        mixer_out_and_mixture(k, 0, False)
        with ExitStack() as c:
            sb = lambda n, s, d=F32: c.enter_context(nc.sbuf_tensor(f"mla_{n}", s, d))
            m = {"wq": sb("wq", [P, JQ, 2 * QW]), "wkv": sb("wkv", [P, JC, 2 * P]), "w_in": [new_signal(k, f"mla_w{n}_in") for n in range(2)],
                 "latents_out": new_signal(k, "latents_out"),
                 "ckv": sb("ckv", [P, NT, KV_LORA]), "kr": sb("kr", [P, NT, ROPE]), "cqT": sb("cqT", [P, JQ, TP]), "ckvT": sb("ckvT", [P, JC, KEYS]),
                 "kh": [[sb(f"kh{a}{h}", [QW, KEYS]) for h in range(2)] for a in range(2)], "mask": sb("mask", [P, 704]),
                 "mask_width": [704, 704, 704, 704, T], "cos": sb("cos", [P, NT, ROPE // 2]), "sin": sb("sin", [P, NT, ROPE // 2])}
            mla_latents(k, m)
            attend(k, True, m)
        mixer_out_and_mixture(k, 1, True)


_OUTS = [
    ("o_y_p", (1, SEQ, D)), ("o_y_s", (1, NEW, D)),
    ("o_fk_p", (1, 1, SEQ, HEADS, HD)), ("o_fv_p", (1, 1, SEQ, HEADS, HD)), ("o_logf_p", (1, 1, SEQ, HEADS)),
    ("o_sk_p", (1, 1, SEQ, HEADS, HD)), ("o_sv_p", (1, 1, SEQ, HEADS, HD)),
    ("o_ckv_p", (1, 1, SEQ, KV_LORA)), ("o_kr_p", (1, 1, SEQ, ROPE)),
    ("o_fk_s", (1, 1, NEW, HEADS, HD)), ("o_fv_s", (1, 1, NEW, HEADS, HD)), ("o_logf_s", (1, 1, NEW, HEADS)),
    ("o_sk_s", (1, 1, NEW, HEADS, HD)), ("o_sv_s", (1, 1, NEW, HEADS, HD)),
    ("o_ckv_s", (1, 1, NEW, KV_LORA)), ("o_kr_s", (1, 1, NEW, ROPE)),
]


def _laid_out(np, a):
    def by_feature(w):
        return w.reshape(w.shape[0] // P, P, -1).transpose(1, 0, 2)

    x_rows = np.concatenate([a["x_prompt"][0], a["x_sample"][0]])
    w_in = a["ab_w_in"][0]
    W = HEADS * HD
    starts = [0, W, 2 * W, 3 * W + HEADS, 4 * W + HEADS, 5 * W + HEADS]
    tiles = [by_feature(w_in[:, starts[3 * side + n] + p * P:starts[3 * side + n] + (p + 1) * P]).reshape(P, J * P)
             for side in (1, 0) for p in range(4) for n in range(3)]
    heads_t = lambda c: c[0, 0].reshape(PAST, 4, P).transpose(1, 2, 0)
    heads_v = lambda c: c[0, 0].reshape(4, P, 4, P).transpose(2, 1, 0, 3).reshape(4, P, 4 * P)
    w_uq = a["mla_w_uq"][0].reshape(JQ, P, 8, 2 * QW).transpose(2, 1, 0, 3).reshape(8, P, JQ * 2 * QW)
    ukv = a["mla_w_ukv"][0].reshape(JC, P, 8, 2, 2, HD)
    ukv = ukv.transpose(2, 1, 0, 4, 3, 5).reshape(8, P, JC * 2 * P)
    w_r = np.stack([by_feature(np.concatenate([a["moe_w_group"][l]] + [a["moe_w_router"][l, g] for g in range(GROUPS)], axis=1))
                    for l in range(2)])
    b_r = np.concatenate([a["moe_b_group"], a["moe_b_router"].reshape(2, NE)], axis=1)
    w_mla = a["mla_w_down"][0]
    gate_up = np.concatenate([a[n].reshape(2, NE, J, P, EH) for n in ("moe_w_gate", "moe_w_up")], axis=-1)
    gate_up = gate_up.transpose(0, 1, 3, 2, 4).reshape(2, NE, P, J * 2 * EH)
    half = ROPE // 2
    freq = np.float32(10000.0) ** (-np.arange(half, dtype=np.float32) / np.float32(half))
    pos = np.concatenate([np.arange(SEQ), PAST + np.arange(NEW), np.zeros(TP - T)]).astype(np.float32)
    ang = pos[:, None] * freq[None, :].astype(np.float32)
    table = lambda f: f(ang).astype(np.float32).reshape(NT, P, half).transpose(1, 0, 2)
    return {
        "x_rows": x_rows, "x_t": by_feature(x_rows.T), "w_ab": np.stack(tiles),
        "w_f": by_feature(w_in[:, 3 * W:3 * W + HEADS]), "b_f": a["ab_b_forget"][0][:, None],
        "logf_past": a["cache_fox_logf"][0, 0].T,
        "k_past": np.concatenate([heads_t(a["cache_sb_k"]), heads_t(a["cache_fox_k"])]),
        "v_past": np.concatenate([heads_v(a["cache_sb_v"]), heads_v(a["cache_fox_v"])]),
        "w_out": np.stack([a[n][0].reshape(J, P, 2, BANK).transpose(2, 1, 0, 3).reshape(2, P, J * BANK) for n in ("ab_w_out", "mla_w_out")]),
        "w_latent": by_feature(w_mla[:, 0:DOWN - ROPE]), "w_rope": by_feature(w_mla[:, DOWN - ROPE:]),
        "g_q": a["mla_g_q"], "g_kv": a["mla_g_kv"], "w_uq": w_uq, "w_ukv": ukv,
        "ckv_past": by_feature(a["cache_mla_ckv"][0, 0].T), "kr_past": a["cache_mla_krope"][0, 0].T,
        "cos": table(np.cos), "sin": table(np.sin), "w_r": w_r, "b_r": b_r,
        "w_gate_up": gate_up, "w_down": a["moe_w_down"].reshape(2, NE, JE, P, D).transpose(0, 1, 3, 2, 4).reshape(2, NE, P, JE * D), "ln_g": a["ln_g"], "ln_b": a["ln_b"],
    }


def kernel(**inputs):
    import numpy as np
    import concourse.bacc as bacc
    from concourse.bass_utils import run_bass_kernel_spmd

    nc = bacc.Bacc("TRN2", target_bir_lowering=False, num_devices=1)
    arrays = {f"in_{n}": np.ascontiguousarray(v) for n, v in _laid_out(np, {n: np.asarray(v) for n, v in inputs.items()}).items()}
    dram = {n[3:]: nc.dram_tensor(n, v.shape, F32, kind="ExternalInput").ap() for n, v in arrays.items()}
    for name, shape in _OUTS:
        dram[name] = nc.dram_tensor(name, shape, F32, kind="ExternalOutput").ap()
    for name, shape in (("cum_d", (HEADS, KEYS)), ("x_d", (T, D)), ("y_d", (2 * T, D))):
        dram[name] = nc.dram_tensor(name, shape, F32, kind="Internal").ap()
    rows = lambda n: dram[n].rearrange("a b t h d -> (a b t) (h d)")
    dram["o_kv"] = {"fox": [rows(n) for n in ("o_fk_p", "o_fv_p", "o_fk_s", "o_fv_s")],
                    "sb": [rows(n) for n in ("o_sk_p", "o_sv_p", "o_sk_s", "o_sv_s")]}
    stream_step(nc, dram)
    got = run_bass_kernel_spmd(nc, [arrays], core_ids=[0]).results[0]
    return tuple(got[name] for name, _ in _OUTS)
```
